# Optimizing a Trainium2 kernel written in Bass

```python
import jax, jax.numpy as jnp
from jax import lax
import numpy as np

D_MODEL = 1024
BATCH = 1
SEQ = 512
DEPTH = 1

ROPE_THETA = 10000.0
NORM_EPS = 1e-6
GN_EPS = 1e-5

RET_HEADS = 4
RET_DK = 64
RET_DV = 128
RET_CHUNK = 128

NSA_HEADS = 8
NSA_KV_HEADS = 2
NSA_DK = 64
NSA_GROUP = NSA_HEADS // NSA_KV_HEADS
CMP_BLOCK = 32
CMP_STRIDE = 16
CMP_HID = 256
SLC_BLOCK = 64
SLC_TOPK = 16
SLC_LOCAL = 2
WINDOW = 512
NSA_QBLOCK = 128
SEL_BIG = 1e9
NEG = -1e30

D_RET = RET_HEADS * RET_DV
D_NSA = NSA_HEADS * NSA_DK
D_MIX = D_RET + D_NSA

RET_QK = RET_HEADS * RET_DK
NSA_KV = NSA_KV_HEADS * NSA_DK
NSA_GATES = 3 * NSA_HEADS
SPLITS = [RET_QK, RET_QK, D_RET, D_RET, D_NSA] + [NSA_KV] * 6 + [NSA_GATES]
IN_COLS = sum(SPLITS)

D_FF = 2816
CONV_WIDTH = 3


def rms_norm(x, w):
    xf = x.astype(jnp.float32)
    y = xf * lax.rsqrt(jnp.mean(xf * xf, axis=-1, keepdims=True) + NORM_EPS)
    return (y * w.astype(jnp.float32)).astype(x.dtype)

def rope_angles(pos, dim):
    inv = 1.0 / (ROPE_THETA ** (jnp.arange(0, dim, 2, dtype=jnp.float32) / dim))
    ang = pos.astype(jnp.float32)[:, None] * inv[None, :]
    return jnp.cos(ang), jnp.sin(ang)

def apply_rope(x, cos, sin):
    x1, x2 = jnp.split(x, 2, axis=-1)
    c = cos[:, None, :]
    s = sin[:, None, :]
    return jnp.concatenate([x1 * c - x2 * s, x1 * s + x2 * c], axis=-1)

def masked_softmax(s, mask):
    s = jnp.where(mask, s, NEG)
    m = jnp.max(s, axis=-1, keepdims=True)
    e = jnp.where(mask, jnp.exp(s - m), 0.0)
    return e / jnp.maximum(jnp.sum(e, axis=-1, keepdims=True), 1e-30)

def retention(q, k, v, g, gn_w, cos, sin):
    f32 = jnp.float32
    B, S = q.shape[0], q.shape[1]
    H, C = RET_HEADS, RET_CHUNK
    N = S // C
    q = apply_rope(q.astype(f32), cos, sin)
    k = apply_rope(k.astype(f32), cos, sin) * (RET_DK ** -0.5)
    v = v.astype(f32).reshape(B, S, H, RET_DV)
    qc = q.reshape(B, N, C, H, RET_DK).transpose(0, 3, 1, 2, 4)
    kc = k.reshape(B, N, C, H, RET_DK).transpose(0, 3, 1, 2, 4)
    vc = v.reshape(B, N, C, H, RET_DV).transpose(0, 3, 1, 2, 4)
    log_gamma = jnp.log(1.0 - 2.0 ** (-5.0 - jnp.arange(H, dtype=f32)))
    i = jnp.arange(C, dtype=f32)
    diff = i[:, None] - i[None, :]
    decay = jnp.where(diff >= 0, jnp.exp(log_gamma[:, None, None] * jnp.maximum(diff, 0.0)), 0.0)
    scores = jnp.einsum('bhnid,bhnjd->bhnij', qc, kc) * decay[None, :, None]
    o_inner = jnp.einsum('bhnij,bhnje->bhnie', scores, vc)
    zeta = jnp.exp(log_gamma[:, None] * (C - 1.0 - i)[None, :])
    xi = jnp.exp(log_gamma[:, None] * (i + 1.0)[None, :])
    kv = jnp.einsum('bhnjd,bhnje->bhnde', kc * zeta[None, :, None, :, None], vc)
    chunk_decay = jnp.exp(log_gamma * C)[None, :, None, None]

    def step(state, kv_n):
        return state * chunk_decay + kv_n, state

    _, prev = lax.scan(step, jnp.zeros((B, H, RET_DK, RET_DV), f32), kv.transpose(2, 0, 1, 3, 4))
    prev = prev.transpose(1, 2, 0, 3, 4)
    o_cross = jnp.einsum('bhnid,bhnde->bhnie', qc, prev) * xi[None, :, None, :, None]
    o = (o_inner + o_cross).transpose(0, 2, 3, 1, 4).reshape(B, S, H, RET_DV)
    mu = jnp.mean(o, axis=-1, keepdims=True)
    var = jnp.mean(jnp.square(o - mu), axis=-1, keepdims=True)
    o = ((o - mu) * lax.rsqrt(var + GN_EPS)).reshape(B, S, D_RET) * gn_w.astype(f32)
    return jax.nn.silu(g.astype(f32)) * o

def compress(kv, pos_emb, w1, w2):
    B, S, G, D = kv.shape
    n_cmp = (S - CMP_BLOCK) // CMP_STRIDE + 1
    idx = (np.arange(n_cmp)[:, None] * CMP_STRIDE + np.arange(CMP_BLOCK)[None, :]).astype(np.int32)
    blocks = kv[:, idx] + pos_emb.astype(jnp.float32)[None, None, :, None, :]
    flat = blocks.transpose(0, 1, 3, 2, 4).reshape(B, n_cmp, G, CMP_BLOCK * D)
    hid = jax.nn.gelu(flat @ w1.astype(jnp.float32))
    return hid @ w2.astype(jnp.float32)

def nsa(q, k_cmp, v_cmp, k_slc, v_slc, k_win, v_win, gate_logits,
        cmp_k_pos, cmp_k_w1, cmp_k_w2, cmp_v_pos, cmp_v_w1, cmp_v_w2, cos, sin):
    f32 = jnp.float32
    B, S = q.shape[0], q.shape[1]
    G, R, D, QB = NSA_KV_HEADS, NSA_GROUP, NSA_DK, NSA_QBLOCK
    q = apply_rope(q.astype(f32), cos, sin) * (D ** -0.5)
    kc = compress(k_cmp.astype(f32), cmp_k_pos, cmp_k_w1, cmp_k_w2)
    vc = compress(v_cmp.astype(f32), cmp_v_pos, cmp_v_w1, cmp_v_w2)
    n_cmp = kc.shape[1]
    cmp_start = np.arange(n_cmp) * CMP_STRIDE
    cmp_end = (cmp_start + CMP_BLOCK - 1).astype(np.int32)
    ccos, csin = rope_angles(jnp.asarray(cmp_end), D)
    kc = apply_rope(kc, ccos, csin)
    ks = apply_rope(k_slc.astype(f32), cos, sin)
    kw = apply_rope(k_win.astype(f32), cos, sin)
    n_slc = S // SLC_BLOCK
    topk = min(SLC_TOPK, n_slc)
    slc_start = np.arange(n_slc) * SLC_BLOCK
    overlap = ((cmp_start[:, None] < slc_start[None, :] + SLC_BLOCK)
               & (cmp_start[:, None] + CMP_BLOCK > slc_start[None, :])).astype(np.float32)

    qg = q.reshape(B, S, G, R, D).transpose(0, 2, 3, 1, 4)
    kc_g = kc.transpose(0, 2, 1, 3)
    vc_g = vc.transpose(0, 2, 1, 3)
    ks_blk = ks.reshape(B, n_slc, SLC_BLOCK, G, D).transpose(0, 3, 1, 2, 4)
    vs_blk = v_slc.astype(f32).reshape(B, n_slc, SLC_BLOCK, G, D).transpose(0, 3, 1, 2, 4)
    pad = ((0, 0), (0, 0), (WINDOW, 0), (0, 0))
    kw_pad = jnp.pad(kw.transpose(0, 2, 1, 3), pad)
    vw_pad = jnp.pad(v_win.astype(f32).transpose(0, 2, 1, 3), pad)
    nqb = S // QB
    q_blocks = qg.reshape(B, G, R, nqb, QB, D).transpose(3, 0, 1, 2, 4, 5)
    bi = jnp.arange(B)[:, None, None, None]
    gi = jnp.arange(G)[None, :, None, None]
    jsl = jnp.arange(n_slc, dtype=jnp.int32)

    def block_fn(args):
        qb, blk = args
        t = blk * QB + jnp.arange(QB, dtype=jnp.int32)
        valid_c = jnp.asarray(cmp_end)[None, :] <= t[:, None]
        p_cmp = masked_softmax(jnp.einsum('bgrtd,bgnd->bgrtn', qb, kc_g), valid_c)
        o_cmp = jnp.einsum('bgrtn,bgnd->bgrtd', p_cmp, vc_g)
        imp = jnp.einsum('bgrtn,nj->bgtj', p_cmp, overlap)
        qblk = t // SLC_BLOCK
        blk_valid = jsl[None, :] <= qblk[:, None]
        forced = (jsl[None, :] == 0) | (blk_valid & (jsl[None, :] > qblk[:, None] - SLC_LOCAL))
        score = jnp.where(forced, SEL_BIG, jnp.where(blk_valid, imp, -SEL_BIG))
        _, sel = lax.top_k(score, topk)
        kg = ks_blk[bi, gi, sel]
        vg = vs_blk[bi, gi, sel]
        tok = sel[..., None] * SLC_BLOCK + jnp.arange(SLC_BLOCK, dtype=jnp.int32)
        smask = (tok <= t[None, None, :, None, None]).reshape(B, G, 1, QB, topk * SLC_BLOCK)
        s_slc = jnp.einsum('bgrtd,bgtksd->bgrtks', qb, kg).reshape(B, G, R, QB, topk * SLC_BLOCK)
        p_slc = masked_softmax(s_slc, smask).reshape(B, G, R, QB, topk, SLC_BLOCK)
        o_slc = jnp.einsum('bgrtks,bgtksd->bgrtd', p_slc, vg)
        kwb = lax.dynamic_slice_in_dim(kw_pad, blk * QB, WINDOW + QB, axis=2)
        vwb = lax.dynamic_slice_in_dim(vw_pad, blk * QB, WINDOW + QB, axis=2)
        kpos = blk * QB - WINDOW + jnp.arange(WINDOW + QB, dtype=jnp.int32)
        wmask = (kpos[None, :] <= t[:, None]) & (kpos[None, :] > t[:, None] - WINDOW) & (kpos[None, :] >= 0)
        p_win = masked_softmax(jnp.einsum('bgrtd,bgsd->bgrts', qb, kwb), wmask)
        o_win = jnp.einsum('bgrts,bgsd->bgrtd', p_win, vwb)
        return o_cmp, o_slc, o_win

    o_cmp, o_slc, o_win = lax.map(block_fn, (q_blocks, jnp.arange(nqb, dtype=jnp.int32)))

    def to_bshd(o):
        return o.transpose(1, 0, 4, 2, 3, 5).reshape(B, S, NSA_HEADS, D)

    gates = jax.nn.sigmoid(gate_logits.astype(f32)).reshape(B, S, 3, NSA_HEADS)[..., None]
    out = gates[:, :, 0] * to_bshd(o_cmp) + gates[:, :, 1] * to_bshd(o_slc) + gates[:, :, 2] * to_bshd(o_win)
    return out.reshape(B, S, D_NSA)

def conv_ffn(x, w_up, conv_w, w_down):
    u = x @ w_up
    c = u.shape[-1]
    u = lax.conv_general_dilated(u, conv_w[:, None, :].astype(u.dtype), window_strides=(1,),
                                 padding=[(CONV_WIDTH - 1, 0)],
                                 dimension_numbers=('NWC', 'WIO', 'NWC'),
                                 feature_group_count=c)
    gate, val = jnp.split(u, 2, axis=-1)
    return (jax.nn.gelu(gate) * val) @ w_down

def first_inputs(seed: int = 0) -> dict:
    key = jax.random.key(seed)
    ks = jax.random.split(key, 20)
    L = DEPTH

    def nrm(k, shape, scale):
        return jax.random.normal(k, shape, jnp.float32) * scale

    def gain(k, shape):
        return 1.0 + 0.02 * jax.random.normal(k, shape, jnp.float32)

    return {
        'x': nrm(ks[0], (BATCH, SEQ, D_MODEL), 1.0),
        'norm_mix_pre': gain(ks[1], (L, D_MODEL)),
        'w_in': nrm(ks[2], (L, D_MODEL, IN_COLS), D_MODEL ** -0.5),
        'ret_gn_w': gain(ks[3], (L, D_RET)),
        'cmp_k_pos': nrm(ks[4], (L, CMP_BLOCK, NSA_DK), 0.02),
        'cmp_k_w1': nrm(ks[5], (L, CMP_BLOCK * NSA_DK, CMP_HID), (CMP_BLOCK * NSA_DK) ** -0.5),
        'cmp_k_w2': nrm(ks[6], (L, CMP_HID, NSA_DK), CMP_HID ** -0.5),
        'cmp_v_pos': nrm(ks[7], (L, CMP_BLOCK, NSA_DK), 0.02),
        'cmp_v_w1': nrm(ks[8], (L, CMP_BLOCK * NSA_DK, CMP_HID), (CMP_BLOCK * NSA_DK) ** -0.5),
        'cmp_v_w2': nrm(ks[9], (L, CMP_HID, NSA_DK), CMP_HID ** -0.5),
        'w_out': nrm(ks[10], (L, D_MIX, D_MODEL), D_MIX ** -0.5),
        'norm_mix_post': gain(ks[11], (L, D_MODEL)),
        'norm_ffn_pre': gain(ks[12], (L, D_MODEL)),
        'ffn_w_up': nrm(ks[13], (L, D_MODEL, 2 * D_FF), D_MODEL ** -0.5),
        'ffn_conv': nrm(ks[14], (L, CONV_WIDTH, 2 * D_FF), CONV_WIDTH ** -0.5),
        'ffn_w_down': nrm(ks[15], (L, D_FF, D_MODEL), D_FF ** -0.5),
        'norm_ffn_post': gain(ks[16], (L, D_MODEL)),
    }

def first_block(x, norm_mix_pre, w_in, ret_gn_w, cmp_k_pos, cmp_k_w1, cmp_k_w2,
              cmp_v_pos, cmp_v_w1, cmp_v_w2, w_out, norm_mix_post, norm_ffn_pre,
              ffn_w_up, ffn_conv, ffn_w_down, norm_ffn_post):
    B, S, _ = x.shape
    cos, sin = rope_angles(jnp.arange(S, dtype=jnp.int32), NSA_DK)
    split_at = [int(v) for v in np.cumsum(SPLITS)[:-1]]
    for l in range(DEPTH):
        h = rms_norm(x, norm_mix_pre[l])
        proj = h @ w_in[l]
        (rq, rk, rv, rg, nq, kcm, vcm, ksl, vsl, kwn, vwn, ng) = jnp.split(proj, split_at, axis=-1)
        y_ret = retention(rq.reshape(B, S, RET_HEADS, RET_DK), rk.reshape(B, S, RET_HEADS, RET_DK),
                          rv, rg, ret_gn_w[l], cos, sin)
        kv = lambda a: a.reshape(B, S, NSA_KV_HEADS, NSA_DK)
        y_nsa = nsa(nq.reshape(B, S, NSA_HEADS, NSA_DK), kv(kcm), kv(vcm), kv(ksl), kv(vsl), kv(kwn), kv(vwn), ng,
                    cmp_k_pos[l], cmp_k_w1[l], cmp_k_w2[l], cmp_v_pos[l], cmp_v_w1[l], cmp_v_w2[l], cos, sin)
        mix = jnp.concatenate([y_ret, y_nsa], axis=-1).astype(x.dtype) @ w_out[l]
        x = x + rms_norm(mix, norm_mix_post[l])
        h = rms_norm(x, norm_ffn_pre[l])
        x = x + rms_norm(conv_ffn(h, ffn_w_up[l], ffn_conv[l], ffn_w_down[l]), norm_ffn_post[l])
    return x


DEPTH_2 = 2

N_EVEN = (DEPTH_2 + 1) // 2
N_ODD = DEPTH_2 // 2

A_WIDTH = D_MODEL // 2
A_HEADS = 4
A_HEAD_DIM = A_WIDTH // A_HEADS
MLSTM_CHUNK = 128
CONV_WIDTH_2 = 5

B_WIDTH = D_MODEL - A_WIDTH
B_GROUPS = 4
B_GROUP_DIM = B_WIDTH // B_GROUPS
SGU_CHUNK = 128

AB_IN = 4 * A_WIDTH + 4 * A_HEADS + 2 * B_WIDTH

C_HEADS = 16
C_NOPE = 64
C_ROPE = 32
C_V = 64
Q_LORA = 384
KV_LORA = 256
C_IN = Q_LORA + KV_LORA + C_ROPE
ROPE_BASE = 10000.0
Q_BLOCK = 128

D_FF_2 = 4 * D_MODEL

EPS = 1e-6


def rms_norm_2(x, g):
    xf = x.astype(jnp.float32)
    y = xf * lax.rsqrt(jnp.mean(xf * xf, axis=-1, keepdims=True) + EPS)
    return (y * g.astype(jnp.float32)).astype(x.dtype)

def centred_dwconv(x, w):
    pad = (w.shape[0] - 1) // 2
    return lax.conv_general_dilated(
        x, w[:, None, :].astype(x.dtype), window_strides=(1,),
        padding=[(pad, pad)], dimension_numbers=("NWC", "WIO", "NWC"),
        feature_group_count=x.shape[-1])

def mlstm_scan(q, k, v, log_i, log_f):
    bsz, nh, seq, dh = q.shape
    L = MLSTM_CHUNK
    nc = seq // L

    def to_chunks(t):
        return jnp.moveaxis(t.reshape(bsz, nh, nc, L, *t.shape[3:]), 2, 0)

    lower = jnp.tril(jnp.ones((L, L), dtype=bool))

    def step(carry, xs):
        C, n, m = carry
        qc, kc, vc, li, lf = xs
        b = jnp.cumsum(lf, axis=-1)
        dmat = jnp.where(lower, b[..., :, None] - b[..., None, :] + li[..., None, :], -jnp.inf)
        m_t = jnp.maximum(b + m[..., None], jnp.max(dmat, axis=-1))
        inter = jnp.exp(b + m[..., None] - m_t)
        s = jnp.einsum("bhtd,bhsd->bhts", qc, kc) * jnp.exp(dmat - m_t[..., None])
        num = (jnp.einsum("bhts,bhse->bhte", s, vc)
               + inter[..., None] * jnp.einsum("bhtd,bhde->bhte", qc, C))
        den = jnp.sum(s, axis=-1) + inter * jnp.einsum("bhtd,bhd->bht", qc, n)
        h = num / jnp.maximum(jnp.abs(den), jnp.exp(-m_t))[..., None]
        g = b[..., -1]
        w_log = g[..., None] - b + li
        m_new = jnp.maximum(g + m, jnp.max(w_log, axis=-1))
        decay = jnp.exp(g + m - m_new)
        w = jnp.exp(w_log - m_new[..., None])
        C_new = decay[..., None, None] * C + jnp.einsum("bhs,bhsd,bhse->bhde", w, kc, vc)
        n_new = decay[..., None] * n + jnp.einsum("bhs,bhsd->bhd", w, kc)
        return (C_new, n_new, m_new), h

    init = (jnp.zeros((bsz, nh, dh, dh), jnp.float32),
            jnp.zeros((bsz, nh, dh), jnp.float32),
            jnp.zeros((bsz, nh), jnp.float32))
    _, h = lax.scan(step, init, (to_chunks(q), to_chunks(k), to_chunks(v),
                                 to_chunks(log_i), to_chunks(log_f)))
    return jnp.moveaxis(h, 0, 2).reshape(bsz, nh, seq, dh)

def ab_mixer(h, w_in, conv_w, gate_b, head_g, v_g, ws, bs, w_out):
    bsz, seq, _ = h.shape
    p = h @ w_in
    qk, va, oa, gates, uv = jnp.split(
        p, [2 * A_WIDTH, 3 * A_WIDTH, 4 * A_WIDTH, 4 * A_WIDTH + 4 * A_HEADS], axis=-1)

    qk = jax.nn.silu(centred_dwconv(qk, conv_w))

    def heads(t):
        return t.reshape(bsz, seq, A_HEADS, A_HEAD_DIM).transpose(0, 2, 1, 3).astype(jnp.float32)

    q = heads(qk[..., :A_WIDTH]) * (A_HEAD_DIM ** -0.5)
    k = heads(qk[..., A_WIDTH:])
    v = heads(va)
    g = (gates + gate_b).astype(jnp.float32).reshape(bsz, seq, 4, A_HEADS).transpose(2, 0, 3, 1)
    li_f, lf_f = g[0], jax.nn.log_sigmoid(g[1])
    li_b, lf_b = g[2], jax.nn.log_sigmoid(g[3])
    h_fwd = mlstm_scan(q, k, v, li_f, lf_f)
    fl = lambda t: jnp.flip(t, axis=2)
    h_bwd = fl(mlstm_scan(fl(q), fl(k), fl(v), jnp.flip(li_b, -1), jnp.flip(lf_b, -1)))
    ha = rms_norm_2(h_fwd + h_bwd, head_g.reshape(A_HEADS, 1, A_HEAD_DIM))
    ha = ha.transpose(0, 2, 1, 3).reshape(bsz, seq, A_WIDTH).astype(h.dtype) * jax.nn.sigmoid(oa)

    u, vb = jnp.split(jax.nn.gelu(uv), 2, axis=-1)
    vb = rms_norm_2(vb.reshape(bsz, seq, B_GROUPS, B_GROUP_DIM), v_g.reshape(B_GROUPS, B_GROUP_DIM))
    vb = vb.reshape(bsz, seq // SGU_CHUNK, SGU_CHUNK, B_GROUPS, B_GROUP_DIM)
    sp = jnp.einsum("gts,bnsgc->bntgc", ws, vb) + bs.T[:, :, None]
    hb = u * sp.reshape(bsz, seq, B_WIDTH)

    return jnp.concatenate([ha, hb], axis=-1) @ w_out

def apply_rope_2(x, cos, sin):
    half = x.shape[-1] // 2
    x1, x2 = x[..., :half], x[..., half:]
    return jnp.concatenate([x1 * cos - x2 * sin, x1 * sin + x2 * cos], axis=-1).astype(x.dtype)

def mla_mixer(h, positions, w_in, q_g, kv_g, w_uq, w_ukv, w_out):
    bsz, seq, _ = h.shape
    cq, ckv, kr = jnp.split(h @ w_in, [Q_LORA, Q_LORA + KV_LORA], axis=-1)
    q = (rms_norm_2(cq, q_g) @ w_uq).reshape(bsz, seq, C_HEADS, C_NOPE + C_ROPE)
    kv = (rms_norm_2(ckv, kv_g) @ w_ukv).reshape(bsz, seq, C_HEADS, C_NOPE + C_V)

    half = C_ROPE // 2
    freq = ROPE_BASE ** (-jnp.arange(half, dtype=jnp.float32) / half)
    ang = positions.astype(jnp.float32)[..., None] * freq
    cos = jnp.cos(ang)[:, :, None, :]
    sin = jnp.sin(ang)[:, :, None, :]
    q_rope = apply_rope_2(q[..., C_NOPE:], cos, sin)
    k_rope = apply_rope_2(kr[:, :, None, :], cos, sin)
    qf = jnp.concatenate([q[..., :C_NOPE], q_rope], axis=-1)
    kf = jnp.concatenate([kv[..., :C_NOPE],
                          jnp.broadcast_to(k_rope, (bsz, seq, C_HEADS, C_ROPE))], axis=-1)
    v = kv[..., C_NOPE:]
    scale = (C_NOPE + C_ROPE) ** -0.5

    qb = jnp.moveaxis(qf.reshape(bsz, seq // Q_BLOCK, Q_BLOCK, C_HEADS, C_NOPE + C_ROPE), 1, 0)

    def attend(qblk):
        s = jnp.einsum("bqhd,bkhd->bhqk", qblk, kf, preferred_element_type=jnp.float32) * scale
        pr = jax.nn.softmax(s, axis=-1)
        return jnp.einsum("bhqk,bkhd->bqhd", pr.astype(v.dtype), v)

    o = lax.map(attend, qb)
    o = jnp.moveaxis(o, 0, 1).reshape(bsz, seq, C_HEADS * C_V)
    return o @ w_out

def second_inputs(seed: int = 0) -> dict:
    key = jax.random.key(seed)
    ks = iter(jax.random.split(key, 40))
    f32 = jnp.float32

    def nrm(shape, scale):
        return jax.random.normal(next(ks), shape, f32) * scale

    def gain(shape):
        return 1.0 + 0.02 * jax.random.normal(next(ks), shape, f32)

    x = jax.random.normal(next(ks), (BATCH, SEQ, D_MODEL), f32)
    offsets = jax.random.randint(next(ks), (BATCH, 1), 0, 1024, dtype=jnp.int32)
    positions = offsets + jnp.arange(SEQ, dtype=jnp.int32)[None, :]

    forget_b = jnp.linspace(3.0, 6.0, A_HEADS, dtype=f32)
    gate_b = jnp.concatenate([
        nrm((N_EVEN, A_HEADS), 0.1),
        forget_b + nrm((N_EVEN, A_HEADS), 0.1),
        nrm((N_EVEN, A_HEADS), 0.1),
        forget_b + nrm((N_EVEN, A_HEADS), 0.1)], axis=-1)

    return {
        "x": x,
        "positions": positions,
        "ab_norm": gain((N_EVEN, D_MODEL)),
        "ab_w_in": nrm((N_EVEN, D_MODEL, AB_IN), D_MODEL ** -0.5),
        "ab_conv": nrm((N_EVEN, CONV_WIDTH_2, 2 * A_WIDTH), CONV_WIDTH_2 ** -0.5),
        "ab_gate_b": gate_b,
        "ab_head_g": gain((N_EVEN, A_WIDTH)),
        "ab_v_g": gain((N_EVEN, B_WIDTH)),
        "ab_ws": nrm((N_EVEN, B_GROUPS, SGU_CHUNK, SGU_CHUNK), SGU_CHUNK ** -0.5),
        "ab_bs": gain((N_EVEN, B_GROUPS, SGU_CHUNK)),
        "ab_w_out": nrm((N_EVEN, A_WIDTH + B_WIDTH, D_MODEL), (A_WIDTH + B_WIDTH) ** -0.5),
        "c_norm": gain((N_ODD, D_MODEL)),
        "c_w_in": nrm((N_ODD, D_MODEL, C_IN), D_MODEL ** -0.5),
        "c_q_g": gain((N_ODD, Q_LORA)),
        "c_kv_g": gain((N_ODD, KV_LORA)),
        "c_w_uq": nrm((N_ODD, Q_LORA, C_HEADS * (C_NOPE + C_ROPE)), Q_LORA ** -0.5),
        "c_w_ukv": nrm((N_ODD, KV_LORA, C_HEADS * (C_NOPE + C_V)), KV_LORA ** -0.5),
        "c_w_out": nrm((N_ODD, C_HEADS * C_V, D_MODEL), (C_HEADS * C_V) ** -0.5),
        "ffn_norm": gain((DEPTH_2, D_MODEL)),
        "ffn_w1": nrm((DEPTH_2, D_MODEL, D_FF_2), D_MODEL ** -0.5),
        "ffn_w2": nrm((DEPTH_2, D_FF_2, D_MODEL), D_FF_2 ** -0.5),
        "final_norm": gain((D_MODEL,)),
    }

def second_block(x, positions, ab_norm, ab_w_in, ab_conv, ab_gate_b, ab_head_g, ab_v_g,
              ab_ws, ab_bs, ab_w_out, c_norm, c_w_in, c_q_g, c_kv_g, c_w_uq, c_w_ukv,
              c_w_out, ffn_norm, ffn_w1, ffn_w2, final_norm):
    for layer in range(DEPTH_2):
        j = layer // 2
        if layer % 2 == 0:
            x = x + ab_mixer(rms_norm_2(x, ab_norm[j]), ab_w_in[j], ab_conv[j], ab_gate_b[j],
                             ab_head_g[j], ab_v_g[j], ab_ws[j], ab_bs[j], ab_w_out[j])
        else:
            x = x + mla_mixer(rms_norm_2(x, c_norm[j]), positions, c_w_in[j], c_q_g[j],
                              c_kv_g[j], c_w_uq[j], c_w_ukv[j], c_w_out[j])
        hf = rms_norm_2(x, ffn_norm[layer])
        x = x + jnp.square(jax.nn.relu(hf @ ffn_w1[layer])) @ ffn_w2[layer]
    return rms_norm_2(x, final_norm)


def setup_inputs(seed=0):
    out = dict(first_inputs(seed))
    for name, value in second_inputs(seed + 1).items():
        if name != "x":
            out[name + "_2"] = value
    return out


def reference(
    x, norm_mix_pre, w_in, ret_gn_w, cmp_k_pos, cmp_k_w1, cmp_k_w2, cmp_v_pos, cmp_v_w1,
    cmp_v_w2, w_out, norm_mix_post, norm_ffn_pre, ffn_w_up, ffn_conv, ffn_w_down, norm_ffn_post,
    positions_2, ab_norm_2, ab_w_in_2, ab_conv_2, ab_gate_b_2, ab_head_g_2, ab_v_g_2, ab_ws_2,
    ab_bs_2, ab_w_out_2, c_norm_2, c_w_in_2, c_q_g_2, c_kv_g_2, c_w_uq_2, c_w_ukv_2, c_w_out_2,
    ffn_norm_2, ffn_w1_2, ffn_w2_2, final_norm_2,
):
    x = first_block(
        x, norm_mix_pre, w_in, ret_gn_w, cmp_k_pos, cmp_k_w1, cmp_k_w2, cmp_v_pos, cmp_v_w1,
        cmp_v_w2, w_out, norm_mix_post, norm_ffn_pre, ffn_w_up, ffn_conv, ffn_w_down,
        norm_ffn_post,
    )
    return second_block(
        x, positions_2, ab_norm_2, ab_w_in_2, ab_conv_2, ab_gate_b_2, ab_head_g_2, ab_v_g_2,
        ab_ws_2, ab_bs_2, ab_w_out_2, c_norm_2, c_w_in_2, c_q_g_2, c_kv_g_2, c_w_uq_2,
        c_w_ukv_2, c_w_out_2, ffn_norm_2, ffn_w1_2, ffn_w2_2, final_norm_2,
    )


_drawn_inputs = setup_inputs


def setup_inputs(seed=0):
    import zlib

    import numpy as np

    out = dict(_drawn_inputs(seed))
    spreads = {}
    factors = {'ret_gn_w': 3.466,
     'cmp_k_pos': 25.682,
     'cmp_v_pos': 4.902,
     'norm_mix_post': 2.976,
     'norm_ffn_pre': 3.06,
     'norm_ffn_post': 4.345,
     'ab_norm_2': 5.133,
     'ab_head_g_2': 64.0,
     'ab_v_g_2': 8.0,
     'ab_bs_2': 8.0,
     'c_norm_2': 8.0,
     'c_q_g_2': 8.0,
     'c_kv_g_2': 22.784,
     'ffn_norm_2': 11.411,
     'final_norm_2': 22.54}
    for name, (base, spread) in spreads.items():
        noise = np.random.default_rng([zlib.crc32(name.encode()), seed]).standard_normal(out[name].shape)
        drawn = base * np.exp(spread * noise) if base else spread * noise
        out[name] = __import__('jax').numpy.asarray(drawn.astype(out[name].dtype))
    for name, factor in factors.items():
        out[name] = (out[name] * factor).astype(out[name].dtype)
    return out
```

```python
from contextlib import ExitStack

import numpy as np

import concourse.bass as bass
from concourse import mybir

F32 = mybir.dt.float32
F32R = mybir.dt.float32r
BF16 = mybir.dt.bfloat16
I32 = mybir.dt.int32
ACT = mybir.ActivationFunctionType
ALU = mybir.AluOpType
AX = mybir.AxisListType

P = 128
S = 512
NT = S // P
D = 1024
KD = D // P
PANEL = 1024
NEG = -1e30
HALF_SWAP = [*range(16, 32), *range(16)]

RET_Q, RET_K, RET_V, RET_G = 0, 2, 4, 8
CMP_IN, NSA_Q, NSA_K, NSA_V, NSA_GATE = 12, 14, 18, 20, 24
CMP_W1, CMP_W2, OUT1 = 25, 33, 34
FF0 = 42
FF0_CHUNKS = [8, 8, 6]
AB_GATE = FF0 + sum(2 * c + KD for c in FF0_CHUNKS)
AB_QK = AB_GATE + 1
AB_V, AB_O, AB_VB, AB_U = AB_QK + 8, AB_QK + 12, AB_QK + 16, AB_QK + 20
OUT2 = AB_U + 4
FF1 = OUT2 + KD
FF_CHUNKS = 4
C_IN = FF1 + FF_CHUNKS * 16
MLA = C_IN + 6
HEADS = 16
OUT3 = MLA + HEADS
FF2 = OUT3 + KD
PANELS_USED = FF2 + FF_CHUNKS * 16
PANELS = (PANELS_USED + 2 + 3) // 4 * 4


def columns(*parts):
    at, out = 0, {}
    for name, n in parts:
        out[name] = (at, n)
        at += n
    return out, at


SMALL, SMALL_N = columns(
    ("ident", 128), ("ones", 128), ("g_mix_pre", 8), ("g_mix_post", 8), ("g_ffn_pre", 8), ("g_ffn_post", 8),
    ("gn", 4), ("cmp_pos", 64), ("conv0", 132), ("g_ab", 8), ("conv1", 40), ("gate_b", 1), ("g_head", 4),
    ("g_c", 8), ("g_cq", 3), ("g_ckv", 2), ("g_ffn1", 8), ("g_ffn2", 8), ("g_final", 8), ("freq", 1),
    ("rope_sign", 1), ("minus_half", 4))
FIRST, FIRST_N = columns(("rope_c", 512), ("rope_s", 512), ("cmp_c", 32), ("cmp_s", 32), ("decay", 2048))
SECOND, SECOND_N = columns(("sgu_b", 512), ("g_v", 512), ("ws_t", 512))
MASKS, MASKS_N = columns(("ident", 128), ("q_k", 128), ("k_q", 128), ("cmp_q_k", 128), ("cmp_k_q", 512))


def plus(v, i, k):
    return v if i is None else i * k + v



NORM_LIST = (
    [("mix_pre", KD, D, 1e-6)] + [(f"ret{h}", 1, P, 1e-5) for h in range(4)]
    + [("mix_post", KD, D, 1e-6), ("ffn_pre", KD, D, 1e-6), ("ffn_post", KD, D, 1e-6), ("ab", KD, D, 1e-6)]
    + [(f"head{h}", 1, P, 1e-6) for h in range(4)]
    + [("ffn1", KD, D, 1e-6), ("c", KD, D, 1e-6), ("cq", 3, 384, 1e-6), ("ckv", 2, 256, 1e-6),
       ("ffn2", KD, D, 1e-6), ("final", KD, D, 1e-6)])
NORM = {}
for _n, (_name, _k, _d, _e) in enumerate(NORM_LIST):
    NORM[_name] = (_n, sum(q[1] for q in NORM_LIST[:_n]), _k, _d, _e)
SPLIT_NORMS = ("mix_pre", "ffn_pre", "ab", "ffn1", "c", "cq", "ckv", "ffn2")
SPLITS_BEFORE = {}
_at = 0
for _name in SPLIT_NORMS:
    SPLITS_BEFORE[_name] = _at
    _at += NORM[_name][2]


def output_of(panel):
    return panel if panel <= CMP_W1 else panel - 2 if panel <= MLA else panel - 2 + 2 * HEADS


def attention_memory(sb, c, tag="a"):
    return dict(
        pr=sb("pr" + tag, [P, 4, S], F32, c), osb=sb("osb" + tag, [P, 2, S], F32, c),
        shift=sb("shift" + tag, [4, 2, S], F32R, c), negm=sb("negm" + tag, [P, 2, 4], F32, c),
        mx=sb("mx" + tag, [P, 2, 4], F32, c), w4=sb("w4" + tag, [P, 4], F32, c),
        wd=sb("wd" + tag, [P, S], F32, c), macc=sb("macc" + tag, [P, S], F32, c), nt=sb("nt" + tag, [P, S], F32, c))


def build(nc, A):
    with ExitStack() as ctx:
        build_in(nc, A, ctx)


def build_in(nc, A, ctx):
    def sb(name, shape, dt, c=ctx):
        return c.enter_context(nc.sbuf_tensor(name, shape, dt))

    def sem(name):
        return ctx.enter_context(nc.semaphore(name))

    x = sb("x", [P, KD, S], F32)
    small = sb("small", [P, SMALL_N], F32)
    masks = sb("masks", [P, MASKS_N], BF16)
    raw = sb("raw", [P, 4, PANEL], F32)
    w_hi = sb("w_hi", [P, 2, PANEL], F32R)
    w_lo = sb("w_lo", [P, 2, PANEL], F32R)
    ev = sb("ev", [P, 4, S], F32)
    h_hi = sb("h_hi", [P, KD, S], F32R)
    h_lo = sb("h_lo", [P, KD, S], F32R)
    tmp = sb("tmp", [P, 4, S], F32)
    r4 = sb("r4", [P, 6, 4], F32)
    ones_r = sb("ones_r", [4, P], F32R)
    ps = ctx.enter_context(nc.psum_tensor("ps", [P, 8, S], F32))

    with ExitStack() as c:
        first = sb("first", [P, FIRST_N], F32, c)
        rq_hi, rq_lo = sb("rq_hi", [P, 2, S], F32R, c), sb("rq_lo", [P, 2, S], F32R, c)
        rk_hi, rk_lo = sb("rk_hi", [P, 2, S], F32R, c), sb("rk_lo", [P, 2, S], F32R, c)
        nq_hi, nq_lo = sb("nq_hi", [P, 4, S], F32R, c), sb("nq_lo", [P, 4, S], F32R, c)
        nk_hi, nk_lo = sb("nk_hi", [P, 2, S], F32R, c), sb("nk_lo", [P, 2, S], F32R, c)
        rv = sb("rv", [P, NT, 512], F32, c)
        rg = sb("rg", [P, 4, S], F32, c)
        nv = sb("nv", [P, NT, 2, 2, P], F32, c)
        vc = sb("vc", [P, 2, P], F32, c)
        gates = sb("gates", [P, NT, 32], F32, c)
        kc_hi, kc_lo = sb("kc_hi", [P, P], F32R, c), sb("kc_lo", [P, P], F32R, c)
        ch_hi, ch_lo = sb("ch_hi", [P, 2, 64], F32R, c), sb("ch_lo", [P, 2, 64], F32R, c)
        cv_hi, cv_lo = sb("cv_hi", [P, 2, 2, P], F32R, c), sb("cv_lo", [P, 2, 2, P], F32R, c)
        kc_f = sb("kc_f", [P, 4, 32], F32, c)
        with ExitStack() as cc:
            xg_f = sb("xg_f", [P, 16, 62], F32, cc)
            xg_hi, xg_lo = sb("xg_hi", [P, 2, 16, 62], F32R, cc), sb("xg_lo", [P, 2, 16, 62], F32R, cc)
        with ExitStack() as cc:
            at1 = attention_memory(sb, cc)
        del cc
    with ExitStack() as c:
        hid_hi, hid_lo = sb("hid_hi", [P, 8, S], F32R, c), sb("hid_lo", [P, 8, S], F32R, c)
        hid_f = sb("hid_f", [P, 2, S], F32, c)
        conv_t = sb("conv_t", [P, 2, S], F32, c)
        act_t = sb("act_t", [P, S], F32, c)
        y = sb("y", [P, KD, S], F32, c)
    with ExitStack() as c:
        second = sb("second", [P, SECOND_N], F32, c)
        aq_hi, aq_lo = sb("aq_hi", [P, 8, S], F32R, c), sb("aq_lo", [P, 8, S], F32R, c)
        av = sb("av", [P, NT, 512], F32, c)
        ao = sb("ao", [P, 4, S], F32, c)
        a_t = sb("a_t", [P, NT, 64], F32, c)
        neg_m, floor_m = sb("neg_m", [64, S], F32, c), sb("floor_m", [64, S], F32, c)
        with ExitStack() as cc:
            gt = sb("gt", [P, 3, S], F32, cc)
            scan = sb("scan", [64, 2, 2 * S], F32, cc)
            li, la = sb("li", [64, S], F32, cc), sb("la", [64, S], F32, cc)
            vb = sb("vb", [P, NT, 512], F32, cc)
            qk_f = sb("qk_f", [P, 2, S], F32, cc)
        with ExitStack() as cc:
            rows = sb("rows", [P, 4, S], F32, cc)
            decays = sb("decays", [P, 2, S], F32, cc)
            diag = sb("diag", [P, 2, P], F32, cc)
            weights = sb("weights", [P, 4, S], F32, cc)
            den = sb("den", [P, S], F32, cc)
            part = sb("part", [P, 2, S], F32, cc)
    with ExitStack() as c:
        c_raw = sb("c_raw", [P, 5, S], F32, c)
        cq_hi, cq_lo = sb("cq_hi", [P, 5, S], F32R, c), sb("cq_lo", [P, 5, S], F32R, c)
        kr_hi, kr_lo = sb("kr_hi", [P, S], F32R, c), sb("kr_lo", [P, S], F32R, c)
        qf_hi, qf_lo = sb("qf_hi", [P, 2, S], F32R, c), sb("qf_lo", [P, 2, S], F32R, c)
        kf_hi, kf_lo = sb("kf_hi", [P, 2, S], F32R, c), sb("kf_lo", [P, 2, S], F32R, c)
        vh = sb("vh", [P, 2, NT, P], F32, c)
        trig = sb("trig", [P, 2, S], F32, c)
        ang = sb("ang", [P, 3, S], F32, c)
        pos_i = sb("pos_i", [P, S], I32, c)
        at2 = attention_memory(sb, c, "b")

    ones = small[:, SMALL["ones"][0]:SMALL["ones"][0] + P]
    ident = small[:, SMALL["ident"][0]:SMALL["ident"][0] + P]

    def col(name, n=0, k=1):
        return small[:, SMALL[name][0] + n:SMALL[name][0] + n + k]

    def mask(name):
        return masks[:, MASKS[name][0]:MASKS[name][0] + MASKS[name][1]]

    def table(t, where, name):
        return t[:, where[name][0]:where[name][0] + where[name][1]]

    raw_in = [sem(f"raw_in{n}") for n in range(4)]
    consts_in, x_in, first_in, second_in, pos_in = (sem(n) for n in (
        "consts_in", "x_in", "first_in", "second_in", "pos_in"))
    w_hi_ready, w_lo_ready, panel_read, tile_out, ev_used = (sem(n) for n in (
        "w_hi_ready", "w_lo_ready", "panel_read", "tile_out", "ev_used"))
    sq_ready, acc_ready, ss_ready, ms_ready, inv_ready, inv_diag, inv_wide, normed, n_hi, n_lo = (sem(n) for n in (
        "sq_ready", "acc_ready", "ss_ready", "ms_ready", "inv_ready", "inv_diag", "inv_wide", "normed", "n_hi", "n_lo"))
    dve_step, pool_set, x_ready, mix_ready = (sem(n) for n in ("dve_step", "pool_set", "x_ready", "mix_ready"))
    cmp_in_ready, cmp_hid_ready, cmp_ready, v_ready = (sem(n) for n in (
        "cmp_in_ready", "cmp_hid_ready", "cmp_ready", "v_ready"))
    ret_s, ret_p, ret_pv, ret_o = (sem(n) for n in ("ret_s", "ret_p", "ret_pv", "ret_o"))
    mx_ready, mx_done, negm_ready, negm_turned, shift_ready, s_ready, exp_done, pv_done = (sem(n) for n in (
        "mx_ready", "mx_done", "negm_ready", "negm_turned", "shift_ready", "s_ready", "exp_done", "pv_done"))
    o_out, den_ready, den_diag, den_wide, o_used = (sem(n) for n in (
        "o_out", "den_ready", "den_diag", "den_wide", "o_used"))
    conv_done, gelu_done, hid_ready, hid_hi_ready, hid_lo_ready = (sem(n) for n in (
        "conv_done", "gelu_done", "hid_ready", "hid_hi_ready", "hid_lo_ready"))
    gate_raw, gate_abs, gate_exp, gate_ln, scan_sum, scan_floor, floor_exp, a_ready, a_turned, a_col = (sem(n) for n in (
        "gate_raw", "gate_abs", "gate_exp", "gate_ln", "scan_sum", "scan_floor", "floor_exp", "a_ready", "a_turned",
        "a_col"))
    vb_ms, vb_inv, sgu_ready, sgu_read, qk_conv, qk_silu = (sem(n) for n in (
        "vb_ms", "vb_inv", "sgu_ready", "sgu_read", "qk_conv", "qk_silu"))
    row_wide, row_out, ml_s, ml_diag, ml_decay, ml_p, ml_pv, ml_read, ml_o = (sem(n) for n in (
        "row_wide", "row_out", "ml_s", "ml_diag", "ml_decay", "ml_p", "ml_pv", "ml_read", "ml_o"))
    ang_ready, trig_ready, proj_ready, head_ready = (sem(n) for n in (
        "ang_ready", "trig_ready", "proj_ready", "head_ready"))
    stored = sem("stored")

    units = []
    for t in range(4):
        for half in range(2):
            for s in range(3):
                r = slice(64 * half, 64 * half + 64)
                k = (kc_hi[r, :], kc_lo[r, :]) if s == 0 else (nk_hi[r, s - 1, :], nk_lo[r, s - 1, :])
                v = (lambda kt, half=half: vc[:, half, :]) if s == 0 else (
                    lambda kt, half=half, s=s: nv[:, kt, s - 1, half, :])
                units.append(dict(q=(nq_hi[r, t, :], nq_lo[r, t, :]), k=k, v=v, half=half, scale=0.125, at=at1, s=s, t=t,
                                  kind="cmp" if s == 0 else "causal", tiles=1 if s == 0 else NT, gate=s * 8 + half * 4 + t))
    NSA_UNITS = len(units)
    for u in range(HEADS):
        units.append(dict(q=(qf_hi[0:96, u % 2, :], qf_lo[0:96, u % 2, :]), k=(kf_hi[0:96, u % 2, :], kf_lo[0:96, u % 2, :]),
                          v=lambda kt, u=u: vh[:, u % 2, kt, :], half=u % 2, scale=96 ** -0.5, at=at2, s=0, t=u // 2,
                          kind="all", tiles=NT, gate=None))
    for n, w in enumerate(units):
        w["n"], w["first"] = n, sum(q["tiles"] for q in units[:n])
        w["num"] = slice(64 * w["half"], 64 * w["half"] + 64)
        w["den"] = 64 - 64 * w["half"]
    FF1_O, FF2_O, FF0_O = output_of(FF1), output_of(FF2), output_of(FF0)

    norm_source = {"mix_pre": x, "mix_post": y, "ffn_pre": x, "ffn_post": y, "ab": x, "ffn1": x, "c": x, "ffn2": x,
                   "final": x, "cq": c_raw[:, 0:3, :], "ckv": c_raw[:, 3:5, :]}
    for h in range(4):
        norm_source[f"ret{h}"] = at1["osb"][:, h % 2:h % 2 + 1, :]
        norm_source[f"head{h}"] = part[:, 1:2, :]
    norm_gain = {"mix_pre": "g_mix_pre", "mix_post": "g_mix_post", "ffn_pre": "g_ffn_pre", "ffn_post": "g_ffn_post",
                 "ab": "g_ab", "ffn1": "g_ffn1", "c": "g_c", "ffn2": "g_ffn2", "final": "g_final", "cq": "g_cq",
                 "ckv": "g_ckv"}
    norm_split = {name: (h_hi, h_lo) for name in SPLIT_NORMS}
    norm_split["cq"] = (cq_hi[:, 0:3, :], cq_lo[:, 0:3, :])
    norm_split["ckv"] = (cq_hi[:, 3:5, :], cq_lo[:, 3:5, :])
    X_WRITES = {}

    def down_tile(pe, dense, panel, i, tiles, hidden, c):
        dense(panel, i, moving=(hid_hi, hid_lo), tiles=tiles,
              **({} if hidden is None else dict(ready=hid_lo_ready, base=plus(hidden, c, 8))))

    def down(pe, dense, panel, tiles, hidden):
        for k in range(KD):
            down_tile(pe, dense, panel + k, None, tiles, hidden if k == 0 else None, None)

    block = ctx.enter_context(nc.Block())

    @block.sync
    def _(sp):
        for n in range(4):
            sp.dma_start(raw[:, n, :], A["panels"][n]).then_inc(raw_in[n], 16)
        with sp.Fori(1, PANELS // 4) as i:
            for n in range(4):
                sp.wait_ge(w_lo_ready, i * 4 + (n - 3))
                sp.dma_start(raw[:, n, :], A["panels"][i * 4 + n]).then_inc(raw_in[n], 16)
        first_norm = NORM["final"][1]
        for k in range(KD):
            sp.wait_ge(normed, first_norm + k + 1)
            sp.dma_start(A["out"][k], y[:, k, :]).then_inc(stored, 16)
        sp.wait_ge(stored, 16 * KD)

    @block.gpsimd
    def _(pool):
        nc.gpsimd.memset(ones_r[:].bitcast(F32), 1.0).then_inc(pool_set, 1)
        nc.gpsimd.memset(nv[:], 1.0).then_inc(pool_set, 1)
        nc.gpsimd.memset(vc[:], 1.0).then_inc(pool_set, 1)
        nc.gpsimd.memset(cv_hi[:].bitcast(F32), 0.0).then_inc(pool_set, 1)
        nc.gpsimd.memset(cv_lo[:].bitcast(F32), 0.0).then_inc(pool_set, 1)
        nc.gpsimd.memset(kc_hi[:].bitcast(F32), 0.0).then_inc(pool_set, 1)
        nc.gpsimd.memset(kc_lo[:].bitcast(F32), 0.0).then_inc(pool_set, 1)
        pool.wait_ge(consts_in, 32)

        def inverse_root(name):
            n = NORM[name][0]
            pool.wait_ge(ms_ready, n + 1)
            nc.gpsimd.tensor_tensor(r4[:, 1, :], r4[:, 0, :], col("minus_half", 0, 4), ALU.pow).then_inc(inv_ready, 1)

        for name, *_ in NORM_LIST[:9]:
            inverse_root(name)
        for t in range(NT):
            pool.wait_ge(vb_ms, t + 1)
            nc.gpsimd.tensor_tensor(r4[:, 3, :], r4[:, 2, :], col("minus_half", 0, 4), ALU.pow).then_inc(vb_inv, 1)
        for name, *_ in NORM_LIST[9:15]:
            inverse_root(name)
        pool.wait_ge(normed, NORM["c"][1] + KD)
        nc.gpsimd.memset(vh[:], 1.0).then_inc(pool_set, 1)
        for name, *_ in NORM_LIST[15:]:
            inverse_root(name)

    @block.tensor
    def _(pe):
        def product(out, a, b, start, stop):
            nc.tensor.matmul(out, a[0], b[0], start=start, stop=False)
            nc.tensor.matmul(out, a[0], b[1], start=False, stop=False)
            return nc.tensor.matmul(out, a[1], b[0], start=False, stop=stop)

        def w(panel, a, b):
            return w_hi[:, panel % 2, a:b], w_lo[:, panel % 2, a:b]

        def dense(panel, i=None, moving=(h_hi, h_lo), tiles=KD, ready=None, base=0, most=None):
            o = output_of(panel)
            pe.wait_ge(w_lo_ready, plus(panel + 1, i, 4))
            if o >= 4:
                pe.wait_ge(tile_out, plus(o - 3, i, 4))
            for k in range(tiles):
                if ready is not None:
                    pe.wait_ge(ready, base + k + 1 if most is None else min(base + k + 1, most))
                last = product(ps[:, o % 4, :], w(panel, k * P, (k + 1) * P), (moving[0][:, k, :], moving[1][:, k, :]),
                               k == 0, k == tiles - 1)
            last.then_inc(panel_read, 1)

        def token_major(panel, width):
            o = output_of(panel)
            pe.wait_ge(tile_out, o)
            for c in range(4):
                pe.wait_ge(w_lo_ready, panel + c + 1)
                for kk in range(2):
                    for t in range(NT):
                        kt = 2 * c + kk
                        at = slice(t * P, (t + 1) * P)
                        last = product(ps[:, (o + t) % 4, 0:width], (h_hi[:, kt, at], h_lo[:, kt, at]),
                                       w(panel + c, kk * 512, kk * 512 + width), kt == 0, kt == KD - 1)
                last.then_inc(panel_read, 1)

        def norm(name):
            n, before, tiles, width, _ = NORM[name]
            pe.wait_ge(acc_ready, before + tiles)
            for t in range(NT):
                last = nc.tensor.matmul(ps[:, 6, t:t + 1], tmp[:, 2, t * P:(t + 1) * P], ones[:, 0:1], start=True, stop=True)
            last.then_inc(ss_ready, 1)
            pe.wait_ge(inv_diag, n + 1)
            if before:
                pe.wait_ge(normed, before)
            nc.tensor.matmul(ps[:, 7, :], ones, tmp[:, 3, :], start=True, stop=True).then_inc(inv_wide, 1)

        def maxima(u):
            n, (q, _), (k, _) = u["n"], u["q"], u["k"]
            if u["kind"] == "cmp":
                if n:
                    pe.wait_ge(mx_done, 4 * n)
                for t in range(NT):
                    out = ps[:, 2, t * 32:(t + 1) * 32]
                    nc.tensor.matmul(out, mask("ident"), mask("cmp_q_k")[:, t * 32:(t + 1) * 32], start=True, stop=False)
                    last = nc.tensor.matmul(out, q[:, t * P:(t + 1) * P], k[:, 0:32], start=False, stop=True)
                last.then_inc(mx_ready, 4)
                return
            for t in range(NT):
                keys = (t + 1) * P if u["kind"] == "causal" else S
                out = ps[:, 2 + t % 2, :]
                if 4 * n + t >= 2:
                    pe.wait_ge(mx_done, 4 * n + t - 1)
                last = nc.tensor.matmul(out[:, 0:keys], q[:, t * P:(t + 1) * P], k[:, 0:keys], start=True,
                                        stop=u["kind"] != "causal")
                if u["kind"] == "causal":
                    last = nc.tensor.matmul(out[:, keys - P:keys], mask("ident"), mask("q_k"), start=False, stop=True)
                last.then_inc(mx_ready, 1)

        def turn(u):
            n = u["n"]
            pe.wait_ge(negm_ready, n + 1)
            if n:
                pe.wait_ge(shift_ready, n)
            nc.tensor.matmul(ps[0:4, 1, 0:P], u["at"]["negm"][:, n % 2, :], ident, start=True, stop=True).then_inc(negm_turned, 1)

        def scores(u, kt):
            n, m = u["n"], u["first"] + kt
            a = kt * P if u["kind"] == "causal" else 0
            out = ps[:, 4 + m % 2, :]
            pe.wait_ge(shift_ready, n + 1)
            if m >= 2:
                pe.wait_ge(exp_done, m - 1)
            nc.tensor.matmul(out[:, a:S], ones_r[:, :], u["at"]["shift"][:, n % 2, a:S], start=True, stop=False)
            if u["kind"] == "causal":
                nc.tensor.matmul(out[:, a:a + P], mask("ident"), mask("k_q"), start=False, stop=False)
            if u["kind"] == "cmp":
                nc.tensor.matmul(out[:, :], mask("ident"), mask("cmp_k_q"), start=False, stop=False)
            k = (u["k"][0][:, kt * P:(kt + 1) * P], u["k"][1][:, kt * P:(kt + 1) * P])
            product(out[:, a:S], k, (u["q"][0][:, a:S], u["q"][1][:, a:S]), False, True).then_inc(s_ready, 1)

        def values(u, kt):
            n, m = u["n"], u["first"] + kt
            a = kt * P if u["kind"] == "causal" else 0
            pe.wait_ge(exp_done, m + 1)
            if kt == 0 and n:
                pe.wait_ge(o_out, n)
            nc.tensor.matmul(ps[:, 6, a:S], u["v"](kt), u["at"]["pr"][:, m % 4, a:S], start=kt == 0,
                             stop=kt == u["tiles"] - 1).then_inc(pv_done, 1)

        def sums(u):
            n, d = u["n"], u["den"]
            pe.wait_ge(o_out, n + 1)
            if n:
                pe.wait_ge(den_diag, n)
            for t in range(NT):
                last = nc.tensor.matmul(ps[:, 1, 256 + t:257 + t], u["at"]["osb"][d:d + 1, n % 2, t * P:(t + 1) * P],
                                        ones[d:d + 1, 0:1], start=True, stop=True)
            last.then_inc(den_ready, 1)

        def widen(u):
            n = u["n"]
            pe.wait_ge(den_diag, n + 1)
            if n:
                pe.wait_ge(o_used, n)
            nc.tensor.matmul(ps[:, 7, :], ones, u["at"]["wd"][:, :], start=True, stop=True).then_inc(den_wide, 1)

        pe.wait_ge(consts_in, 32)
        pe.wait_ge(x_in, 16)
        norm("mix_pre")
        for panel in range(RET_Q, RET_V):
            dense(panel, ready=n_lo if panel == RET_Q else None)
        token_major(RET_V, 512)
        for panel in range(RET_G, NSA_V):
            dense(panel)
        token_major(NSA_V, 256)
        o = output_of(NSA_GATE)
        pe.wait_ge(w_lo_ready, NSA_GATE + 1)
        pe.wait_ge(tile_out, o - 3)
        for t in range(NT):
            for k in range(KD):
                at = slice(t * P, (t + 1) * P)
                last = product(ps[:, o % 4, t * 32:(t + 1) * 32], (h_hi[:, k, at], h_lo[:, k, at]),
                               w(NSA_GATE, k * 32, (k + 1) * 32), k == 0, k == KD - 1)
        last.then_inc(panel_read, 1)
        for kv in range(2):
            o = CMP_W1 + 2 * kv
            pe.wait_ge(tile_out, o - 2)
            pe.wait_ge(cmp_in_ready, kv + 1)
            for c in range(4):
                panel = CMP_W1 + 4 * kv + c
                pe.wait_ge(w_lo_ready, panel + 1)
                for kk in range(4):
                    for m in range(2):
                        kt = 4 * c + kk
                        last = product(ps[:, (o + m) % 4, 0:62], w(panel, kk * 256 + m * P, kk * 256 + (m + 1) * P),
                                       (xg_hi[:, kv, kt, :], xg_lo[:, kv, kt, :]), kt == 0, kt == 15)
                last.then_inc(panel_read, 1)
        pe.wait_ge(w_lo_ready, CMP_W2 + 1)
        pe.wait_ge(cmp_hid_ready, 4)
        o = CMP_W1 + 4
        pe.wait_ge(tile_out, o)
        for m in range(2):
            product(ps[:, o % 4, 0:62], w(CMP_W2, m * P, (m + 1) * P), (ch_hi[:, m, 0:62], ch_lo[:, m, 0:62]), m == 0, m == 1)
        for g in range(2):
            for m in range(2):
                last = product(ps[:, (o + 1 + g) % 4, 0:64], (cv_hi[:, m, g, :], cv_lo[:, m, g, :]),
                               w(CMP_W2, 256 + m * 64, 320 + m * 64), m == 0, m == 1)
        last.then_inc(panel_read, 1)

        pe.wait_ge(tile_out, CMP_W1 + 7)
        pe.wait_ge(ev_used, CMP_W1)
        for h in range(4):
            r = slice(64 * (h % 2), 64 * (h % 2) + 64)

            def ret_values(m, kt):
                pe.wait_ge(ret_p, m + 1)
                nc.tensor.matmul(ps[:, h % 2, kt * P:S], rv[:, kt, h * P:(h + 1) * P], at1["pr"][:, m % 4, kt * P:S],
                                 start=kt == 0, stop=kt == NT - 1).then_inc(ret_pv, 1)

            if h >= 2:
                pe.wait_ge(ret_o, h - 1)
            for kt in range(NT):
                m = 4 * h + kt
                if m >= 2:
                    pe.wait_ge(ret_p, m - 1)
                at = slice(kt * P, (kt + 1) * P)
                product(ps[:, 4 + m % 2, kt * P:S], (rk_hi[r, h // 2, at], rk_lo[r, h // 2, at]),
                        (rq_hi[r, h // 2, kt * P:S], rq_lo[r, h // 2, kt * P:S]), True, True).then_inc(ret_s, 1)
                if kt:
                    ret_values(m - 1, kt - 1)
            ret_values(4 * h + 3, 3)
            if h:
                norm(f"ret{h - 1}")
        norm("ret3")

        pe.wait_ge(pool_set, 7)
        pe.wait_ge(cmp_ready, 3)
        nsa = units[:NSA_UNITS]
        pe.wait_ge(mix_ready, 4)
        maxima(nsa[0])
        maxima(nsa[1])
        turn(nsa[0])
        for n, u in enumerate(nsa):
            scores(u, 0)
            if n:
                sums(nsa[n - 1])
            if u["tiles"] > 1:
                scores(u, 1)
            if n + 2 < NSA_UNITS:
                maxima(nsa[n + 2])
            values(u, 0)
            if n:
                widen(nsa[n - 1])
            for kt in range(2, u["tiles"]):
                scores(u, kt)
                values(u, kt - 1)
            if n + 1 < NSA_UNITS:
                turn(nsa[n + 1])
            if u["tiles"] > 1:
                values(u, u["tiles"] - 1)
        sums(nsa[-1])
        widen(nsa[-1])

        def dense_run(panel, count, **first):
            for j in range(4):
                dense(panel + j, **(first if j == 0 else {}))
            if count > 4:
                with pe.Fori(1, count // 4) as i:
                    for j in range(4):
                        dense(panel + j, i)

        dense_run(OUT1, KD, ready=mix_ready, base=0)
        norm("mix_post")
        norm("ffn_pre")
        panel, hidden = FF0, 0
        for c, tiles in enumerate(FF0_CHUNKS):
            dense_run(panel, 2 * tiles, **(dict(ready=n_lo, base=SPLITS_BEFORE["ffn_pre"]) if c == 0 else {}))
            panel += 2 * tiles
            down(pe, dense, panel, tiles, hidden)
            panel += KD
            hidden += tiles
        norm("ffn_post")

        norm("ab")
        dense(AB_GATE, ready=n_lo, base=SPLITS_BEFORE["ab"])
        for panel in range(AB_QK, AB_V):
            dense(panel)
        for t in range(NT):
            if t == 0:
                pe.wait_ge(a_ready, 1)
            last = nc.tensor.matmul(ps[:, 6, t * 64:(t + 1) * 64], la[:, t * P:(t + 1) * P], ident[0:64, 0:64],
                                    start=True, stop=True)
        last.then_inc(a_turned, 1)
        token_major(AB_V, 512)
        for panel in range(AB_O, AB_VB):
            dense(panel)
        token_major(AB_VB, 512)
        for panel in range(AB_U, OUT2):
            dense(panel)

        pe.wait_ge(tile_out, output_of(OUT2))
        pe.wait_ge(ev_used, output_of(OUT2))
        for g in range(4):
            for t in range(NT):
                last = nc.tensor.matmul(ps[:, g, t * P:(t + 1) * P], vb[:, t, g * P:(g + 1) * P],
                                        table(second, SECOND, "ws_t")[:, g * P:(g + 1) * P], start=True, stop=True)
            last.then_inc(sgu_ready, 1)
        pe.wait_ge(sgu_read, 4)

        pe.wait_ge(floor_exp, 1)

        def row(n, h, d, src):
            if n:
                pe.wait_ge(row_out, n)
            nc.tensor.matmul(ps[:, 7, :], ident[0:64, 32 * d + h:32 * d + h + 1].to_broadcast([64, P]), src[:, :],
                             start=True, stop=True).then_inc(row_wide, 1)

        for h in range(4):
            if h:
                pe.wait_ge(normed, NORM[f"head{h - 1}"][1] + 1)
            for d in range(2):
                row(4 * h + 2 * d, h, d, neg_m)
                row(4 * h + 2 * d + 1, h, d, floor_m)
            if h:
                pe.wait_ge(ml_read, 2 * h)

            def ml_values(m, kt, d, order):
                pe.wait_ge(ml_p, 8 * h + m + 1)
                a, b = (kt * P, S) if d == 0 else (0, (kt + 1) * P)
                begins, ends = kt == (0 if d == 0 else 3), kt == 2
                wt = weights[:, m % 4, a:b]
                nc.tensor.matmul(ps[:, 2 * d, a:b], av[:, kt, h * P:(h + 1) * P], wt, start=begins, stop=ends)
                nc.tensor.matmul(ps[:, 2 * d + 1, a:b], ones, wt, start=begins, stop=ends).then_inc(ml_pv, 1)

            def ml_scores(n, kt):
                if 4 * h + n >= 2:
                    pe.wait_ge(ml_p, 8 * h + 2 * n - 2)
                at = slice(kt * P, (kt + 1) * P)
                product(ps[:, 4 + n % 2, :], (aq_hi[:, 4 + h, at], aq_lo[:, 4 + h, at]), (aq_hi[:, h, :], aq_lo[:, h, :]),
                        True, True).then_inc(ml_s, 1)

            ml_scores(0, 0)
            ml_scores(1, 3)
            ml_values(0, 0, 0, 0)
            ml_values(3, 3, 1, 1)
            ml_values(1, 0, 1, 2)
            ml_scores(2, 1)
            ml_values(2, 3, 0, 3)
            ml_scores(3, 2)
            ml_values(4, 1, 0, 4)
            ml_values(5, 1, 1, 5)
            ml_values(6, 2, 0, 6)
            ml_values(7, 2, 1, 7)
            norm(f"head{h}")

        pe.wait_ge(ml_read, 8)
        dense_run(OUT2, KD, ready=mix_ready, base=12, most=16)

        def feed_forward(panel, base, hidden, name):
            norm(name)
            dense_run(panel, 8, ready=n_lo, base=SPLITS_BEFORE[name])
            down(pe, dense, panel + 8, 8, hidden)
            with pe.Fori(0, FF_CHUNKS - 1) as c:
                with pe.Fori(0, 2) as j:
                    for n in range(4):
                        dense(panel + 16 + n, c * 4 + j)
                for k in range(4):
                    down_tile(pe, dense, panel + 24 + k, c * 4, 8, hidden + 8 if k == 0 else None, c)
                for k in range(4):
                    down_tile(pe, dense, panel + 28 + k, c * 4, 8, None, None)

        feed_forward(FF1, 0, sum(FF0_CHUNKS), "ffn1")

        norm("c")
        for panel in range(C_IN, MLA):
            dense(panel, **(dict(ready=n_lo, base=SPLITS_BEFORE["c"]) if panel == C_IN else {}))
        norm("cq")
        norm("ckv")
        pe.wait_ge(n_lo, SPLITS_BEFORE["ckv"] + 2)
        pe.wait_ge(pool_set, 8)

        def project(n, part):
            panel, o = MLA + n, output_of(MLA) + 3 * n + part
            pe.wait_ge(w_lo_ready, panel + 1)
            pe.wait_ge(tile_out, o)
            if part < 2:
                for k in range(3 - part):
                    a = part * 384 + k * P
                    last = product(ps[:, 0, :], w(panel, a, a + P), (cq_hi[:, 3 * part + k, :], cq_lo[:, 3 * part + k, :]),
                                   k == 0, k == 2 - part)
                last.then_inc(proj_ready, 1)
                return
            for t in range(NT):
                for k in range(2):
                    at = slice(t * P, (t + 1) * P)
                    last = product(ps[:, 0, t * 64:(t + 1) * 64], (cq_hi[:, 3 + k, at], cq_lo[:, 3 + k, at]),
                                   w(panel, 640 + k * 64, 704 + k * 64), k == 0, k == 1)
            last.then_inc(panel_read, 1)

        mla = units[NSA_UNITS:]
        for k in range(3):
            project(0, k)
        pe.wait_ge(head_ready, 1)
        maxima(mla[0])
        turn(mla[0])
        for n, u in enumerate(mla):
            more = n + 1 < HEADS
            scores(u, 0)
            if n:
                sums(mla[n - 1])
            scores(u, 1)
            if more:
                project(n + 1, 0)
            values(u, 0)
            if n:
                widen(mla[n - 1])
            scores(u, 2)
            if more:
                project(n + 1, 1)
            values(u, 1)
            scores(u, 3)
            if more:
                project(n + 1, 2)
            values(u, 2)
            if more:
                pe.wait_ge(head_ready, n + 2)
                maxima(mla[n + 1])
            values(u, 3)
            if more:
                turn(mla[n + 1])
        sums(mla[-1])
        widen(mla[-1])

        dense_run(OUT3, KD, ready=mix_ready, base=16)
        feed_forward(FF2, 0, sum(FF0_CHUNKS) + 8 * FF_CHUNKS, "ffn2")
        norm("final")


    @block.scalar
    def _(act):
        def split(panel, i=None):
            act.wait_ge(raw_in[panel % 4], plus(16 * (panel // 4 + 1), i, 16))
            if panel >= 2:
                act.wait_ge(panel_read, plus(panel - 1, i, 4))
            nc.scalar.activation(w_hi[:, panel % 2, :], raw[:, panel % 4, :], ACT.Copy).then_inc(w_hi_ready, 1)

        def out(o, func, read, i=None, cols=S, bias=0.0, n=1):
            act.wait_ge(panel_read, plus(read, i, 4))
            if o >= 4:
                act.wait_ge(ev_used, plus(o - 3, i, 4))
            nc.scalar.activation(ev[:, o % 4, 0:cols], ps[:, o % 4, 0:cols], func, bias=bias).then_inc(tile_out, n)

        def step(panel, func=ACT.Copy, i=None, **more):
            act.wait_ge(panel_read, plus(panel + 1, i, 4))
            split(panel + 2, i)
            out(output_of(panel), func, panel + 1, i, **more)

        def token_major(panel, func, cols):
            for c in range(4):
                split(panel + c + 2)
            for t in range(NT):
                out(output_of(panel) + t, func, panel + 4, cols=cols)

        def step_run(panel, count, func=ACT.Copy):
            with act.Fori(0, count // 4) as i:
                for j in range(4):
                    step(panel + j, func, i)

        def squares(name, ready, value):
            _, before, tiles, _, _ = NORM[name]
            act.wait_ge(ready, value)
            for k in range(tiles):
                m = before + k
                if m >= 2:
                    act.wait_ge(acc_ready, m - 1)
                nc.scalar.activation(tmp[:, m % 2, :], norm_source[name][:, k, :], ACT.Square).then_inc(sq_ready, 1)

        def highs(name):
            _, before, tiles, _, _ = NORM[name]
            for k in range(tiles):
                act.wait_ge(normed, before + k + 1)
                nc.scalar.activation(norm_split[name][0][:, k, :], tmp[:, (before + k) % 2, :], ACT.Copy).then_inc(n_hi, 1)

        act.dma_start(small[:], A["small"]).then_inc(consts_in, 16)
        act.dma_start(masks[:], A["masks"]).then_inc(consts_in, 16)
        act.dma_start(x[:], A["x"].rearrange("k p s -> p k s")).then_inc(x_in, 16)
        act.dma_start(first[:], A["first"]).then_inc(first_in, 16)

        split(0)
        split(1)
        squares("mix_pre", x_in, 16)
        highs("mix_pre")
        for panel in range(RET_Q, RET_V):
            step(panel)
        token_major(RET_V, ACT.Copy, S)
        for panel in range(RET_G, CMP_IN):
            step(panel, ACT.Silu)
        for panel in range(CMP_IN, NSA_V):
            step(panel)
        token_major(NSA_V, ACT.Copy, 256)
        step(NSA_GATE, ACT.Sigmoid, cols=P)
        for kv in range(2):
            panel, o = CMP_W1 + 4 * kv, CMP_W1 + 2 * kv
            for c in range(4):
                split(panel + c + 2)
            for m in range(2):
                out(o + m, ACT.Gelu_apprx_tanh, panel + 4, cols=62)
        split(CMP_W2 + 2)
        out(CMP_W1 + 4, ACT.Copy, CMP_W2 + 1, cols=62)
        out(CMP_W1 + 5, ACT.Copy, CMP_W2 + 1, cols=64)
        out(CMP_W1 + 6, ACT.Copy, CMP_W2 + 1, cols=64)

        for h in range(4):
            act.wait_ge(ret_pv, 4 * (h + 1))
            if h >= 2:
                act.wait_ge(normed, NORM[f"ret{h - 2}"][1] + 1)
            nc.scalar.activation(at1["osb"][:, h % 2, :], ps[:, h % 2, :], ACT.Copy).then_inc(ret_o, 1)
            squares(f"ret{h}", ret_o, h + 1)

        def weights_of(u, kt):
            m = u["first"] + kt
            a = kt * P if u["kind"] == "causal" else 0
            act.wait_ge(s_ready, m + 1)
            if m >= 4:
                act.wait_ge(pv_done, m - 3)
            nc.scalar.activation(u["at"]["pr"][:, m % 4, a:S], ps[:, 4 + m % 2, a:S], ACT.Exp,
                                 scale=u["scale"]).then_inc(exp_done, 1)

        def result_of(u):
            n = u["n"]
            act.wait_ge(pv_done, u["first"] + u["tiles"])
            if n >= 2:
                act.wait_ge(o_used, n - 1)
            nc.scalar.activation(u["at"]["osb"][:, n % 2, :], ps[:, 6, :], ACT.Copy).then_inc(o_out, 1)

        act.wait_ge(normed, NORM["ret3"][1] + 1)
        nsa = units[:NSA_UNITS]
        for n, u in enumerate(nsa):
            if n:
                result_of(nsa[n - 1])
            for kt in range(u["tiles"]):
                weights_of(u, kt)
        result_of(nsa[-1])

        step_run(OUT1, KD)
        squares("mix_post", ev_used, FF0_O)
        squares("ffn_pre", x_ready, KD)
        highs("ffn_pre")

        def hidden_high(k, slot, ready, value):
            act.wait_ge(ready, value)
            nc.scalar.activation(hid_hi[:, k, :], hid_f[:, slot, :], ACT.Copy).then_inc(hid_hi_ready, 1)

        panel, hidden = FF0, 0
        for tiles in FF0_CHUNKS:
            def pair(j, i=None, skip=False):
                a = panel + 2 * j
                step(a, i=i)
                step(a + 1, i=i)
                act.wait_ge(ev_used, plus(output_of(a) + 1, i, 4))
                if hidden + j or i is not None:
                    act.wait_ge(hid_ready, plus(hidden + j, i, 2))
                nc.scalar.activation(act_t[:], conv_t[:, 0, :], ACT.Gelu_apprx_tanh).then_inc(gelu_done, 1)
                if not skip:
                    hidden_high(plus(j - 1, i, 2), (j - 1) % 2, hid_ready, plus(hidden + j, i, 2))

            pair(0, skip=True)
            pair(1)
            with act.Fori(1, tiles // 2) as i:
                pair(0, i)
                pair(1, i)
            hidden_high(tiles - 1, 1, hid_ready, hidden + tiles)
            step_run(panel + 2 * tiles, KD)
            panel += 2 * tiles + KD
            hidden += tiles
        squares("ffn_post", ev_used, output_of(AB_GATE))
        squares("ab", x_ready, 2 * KD)
        highs("ab")

        act.wait_ge(ev_used, output_of(AB_GATE))
        act.dma_start(second[:], A["second"]).then_inc(second_in, 16)
        step(AB_GATE)
        act.wait_ge(gate_raw, 2)
        nc.scalar.activation(gt[64:P, 1, :], gt[64:P, 0, :], ACT.Abs).then_inc(gate_abs, 1)
        act.wait_ge(gate_abs, 1)
        nc.scalar.activation(gt[64:P, 2, :], gt[64:P, 1, :], ACT.Exp, scale=-1.0).then_inc(gate_exp, 1)
        act.wait_ge(gate_exp, 1)
        nc.scalar.activation(gt[64:P, 1, :], gt[64:P, 2, :], ACT.Ln, bias=1.0).then_inc(gate_ln, 1)
        for n in range(8):
            step(AB_QK + n)
            act.wait_ge(qk_conv, n + 1)
            nc.scalar.activation(qk_f[:, 1, :], qk_f[:, 0, :], ACT.Silu).then_inc(qk_silu, 1)
        token_major(AB_V, ACT.Copy, S)
        for panel in range(AB_O, AB_VB):
            step(panel, ACT.Sigmoid)
        token_major(AB_VB, ACT.Gelu_apprx_tanh, S)
        for panel in range(AB_U, OUT2):
            step(panel, ACT.Gelu_apprx_tanh)

        act.wait_ge(scan_floor, 1)
        nc.scalar.activation(floor_m[:, :], floor_m[:, :], ACT.Exp, scale=-1.0).then_inc(floor_exp, 1)
        act.wait_ge(sgu_read, 4)
        for h in range(4):
            if h:
                act.wait_ge(ml_read, 2 * h)
            for n in range(4):
                act.wait_ge(row_wide, 4 * h + n + 1)
                nc.scalar.activation(rows[:, n, :], ps[:, 7, :], ACT.Copy).then_inc(row_out, 1)
            for n, kt in enumerate((0, 3, 1, 2)):
                for d in range(2):
                    m = 8 * h + 2 * n + d
                    at = slice(kt * P, (kt + 1) * P)
                    rest = slice((kt + 1) * P, S) if d == 0 else slice(0, kt * P)
                    bias = a_t[:, kt, 32 * d + h:32 * d + h + 1]
                    act.wait_ge(ml_diag, m + 1)
                    if m >= 2:
                        act.wait_ge(ml_p, m - 1)
                    last = nc.scalar.activation(decays[:, m % 2, at], diag[:, m % 2, :], ACT.Exp, bias=bias)
                    if rest.start < rest.stop:
                        last = nc.scalar.activation(decays[:, m % 2, rest], rows[:, 2 * d, rest], ACT.Exp, bias=bias)
                    last.then_inc(ml_decay, 1)
            squares(f"head{h}", ml_o, h + 1)

        def feed_forward(panel, name):
            squares(name, ev_used, output_of(panel))
            highs(name)

            def chunk(c):
                o = output_of(panel)

                def tile(k, i, skip=False):
                    step(panel + k, ACT.Relu, i)
                    if not skip:
                        hidden_high(k - 1, (k - 1) % 2, ev_used, plus(o + k, i, 4))

                i = None if c is None else c * 4
                for k in range(8):
                    tile(k, i, k == 0)
                hidden_high(7, 1, ev_used, plus(o + 8, i, 4))
                for k in range(8):
                    step(panel + 8 + k, ACT.Copy, i)

            with act.Fori(0, FF_CHUNKS) as c:
                chunk(c)

        step_run(OUT2, KD)
        feed_forward(FF1, "ffn1")

        squares("c", ev_used, output_of(C_IN))
        act.dma_start(pos_i[64:96, :], A["positions"]).then_inc(pos_in, 16)
        highs("c")
        for panel in range(C_IN, MLA):
            step(panel)
        for d in range(2):
            act.wait_ge(ang_ready, d + 1)
            nc.scalar.activation(trig[64:96, d, :], ang[64:96, 1 + d, :], ACT.Sin).then_inc(trig_ready, 1)
        squares("cq", ev_used, output_of(MLA))
        highs("cq")
        squares("ckv", n_lo, SPLITS_BEFORE["ckv"])
        highs("ckv")

        def project_out(n, part):
            o = output_of(MLA) + 3 * n + part
            if part == 0:
                split(MLA + n + 1) if n else None
            if part < 2:
                act.wait_ge(proj_ready, 2 * n + part + 1)
            else:
                act.wait_ge(panel_read, MLA + n + 1)
            act.wait_ge(ev_used, o - 3)
            nc.scalar.activation(ev[:, o % 4, 0:256 if part == 2 else S], ps[:, 0, 0:256 if part == 2 else S],
                                 ACT.Copy).then_inc(tile_out, 1)

        mla = units[NSA_UNITS:]
        for k in range(3):
            project_out(0, k)
        for n, u in enumerate(mla):
            if n:
                result_of(mla[n - 1])
            weights_of(u, 0)
            weights_of(u, 1)
            if n + 1 < HEADS:
                project_out(n + 1, 0)
            weights_of(u, 2)
            if n + 1 < HEADS:
                project_out(n + 1, 1)
            weights_of(u, 3)
            if n + 1 < HEADS:
                project_out(n + 1, 2)
        result_of(mla[-1])
        split(OUT3 + 1)

        step_run(OUT3, KD)
        feed_forward(FF2, "ffn2")
        squares("final", ev_used, output_of(PANELS_USED))

    @block.vector
    def _(dve):
        V = nc.vector
        so_far, loop = {}, {"i": None, "each": {}}

        def signal(ins, s, n=1, wait=True):
            so_far[s] = so_far.get(s, 0) + n
            ins.then_inc(s, n)
            if wait:
                dve.wait_ge(s, plus(so_far[s], loop["i"], loop["each"].get(s, 0)))

        def link(ins):
            signal(ins, dve_step)

        def enter(i, each, first=0):
            for s, k in each.items():
                so_far[s] = so_far.get(s, 0) - k * first
            loop["i"], loop["each"], loop["start"], loop["first"] = i, each, dict(so_far), first

        def leave(turns):
            for s, k in loop["each"].items():
                assert so_far.get(s, 0) - loop["start"].get(s, 0) == k, s
                so_far[s] += k * (turns - 1 + loop["first"])
            loop["i"], loop["each"] = None, {}

        def low(panel, i=None):
            dve.wait_ge(w_hi_ready, plus(panel + 1, i, 4))
            signal(V.tensor_tensor(w_lo[:, panel % 2, :], raw[:, panel % 4, :], w_hi[:, panel % 2, :].bitcast(F32),
                            ALU.subtract), w_lo_ready, wait=False)

        def take(panel, i=None, extra=0):
            low(panel + 2, i)
            o = output_of(panel)
            dve.wait_ge(tile_out, plus(o + 1, i, 4))
            return ev[:, o % 4, :]

        def take_four(panel):
            for c in range(4):
                low(panel + c + 2)
            for t in range(NT):
                dve.wait_ge(tile_out, output_of(panel) + t + 1)
                yield t, ev[:, (output_of(panel) + t) % 4, :]

        def used(ins):
            signal(ins, ev_used)

        def parts(hi, lo, src):
            link(V.tensor_copy(hi, src))
            return V.tensor_tensor(lo, src, hi.bitcast(F32), ALU.subtract)

        def wide(t4, n=P):
            return t4.unsqueeze(2).to_broadcast([t4.shape[0], 4, n])

        def fours(t):
            return t.rearrange("p (a b) -> p a b", a=4)

        def rope(src, dst, c, s, swapped):
            link(V.stream_shuffle(swapped, src, HALF_SWAP))
            link(V.tensor_tensor(swapped, swapped, s, ALU.mult))
            link(V.tensor_tensor(dst, src, c, ALU.mult))
            link(V.tensor_tensor(dst, dst, swapped, ALU.add))

        def inverse(name):
            n, before, tiles, width, eps = NORM[name]
            for k in range(tiles):
                m = before + k
                dve.wait_ge(sq_ready, m + 1)
                if k == 0:
                    signal(V.tensor_copy(tmp[:, 2, :], tmp[:, m % 2, :]), acc_ready)
                else:
                    dve.wait_ge(acc_ready, m)
                    signal(V.tensor_tensor(tmp[:, 2, :], tmp[:, 2, :], tmp[:, m % 2, :], ALU.add), acc_ready)
            dve.wait_ge(ss_ready, n + 1)
            signal(V.tensor_scalar(r4[:, 0, :], ps[:, 6, 0:4], 1.0 / width, eps, ALU.mult, ALU.add), ms_ready)
            dve.wait_ge(inv_ready, n + 1)
            signal(V.tensor_tensor(fours(tmp[:, 3, :]), ident.unsqueeze(1).to_broadcast([P, 4, P]), wide(r4[:, 1, :]),
                            ALU.mult), inv_diag)
            dve.wait_ge(inv_wide, n + 1)

        def scaled(name, k, gain, out=None):
            m = NORM[name][1] + k
            out = tmp[:, m % 2, :] if out is None else out
            signal(V.scalar_tensor_tensor(out, norm_source[name][:, k, :], gain, ps[:, 7, :], ALU.mult, ALU.mult), normed)

        def norm_split_of(name):
            _, before, tiles, _, _ = NORM[name]
            inverse(name)
            hi, lo = norm_split[name]
            at = SPLITS_BEFORE[name]

            def lower(k):
                dve.wait_ge(n_hi, at + k + 1)
                signal(V.tensor_tensor(lo[:, k, :], tmp[:, (before + k) % 2, :], hi[:, k, :].bitcast(F32), ALU.subtract), n_lo)

            for k in range(tiles):
                scaled(name, k, col(norm_gain[name], k))
                if k:
                    dve.wait_ge(normed, before + k)
                    lower(k - 1)
            dve.wait_ge(normed, before + tiles)
            lower(tiles - 1)

        def norm_add(name):
            inverse(name)
            _, before, tiles, _, _ = NORM[name]
            for k in range(tiles):
                scaled(name, k, col(norm_gain[name], k))
                dve.wait_ge(normed, before + k + 1)
                signal(V.tensor_tensor(x[:, k, :], x[:, k, :], tmp[:, (before + k) % 2, :], ALU.add), x_ready)

        def norm_head(name, gain, gate, k):
            inverse(name)
            before = NORM[name][1]
            t = tmp[:, before % 2, :]
            scaled(name, 0, gain)
            dve.wait_ge(normed, before + 1)
            link(V.tensor_tensor(t, t, gate, ALU.mult))
            signal(parts(h_hi[:, k, :], h_lo[:, k, :], t), mix_ready)

        def take_run(panel, n, each):
            with dve.Fori(0, n // 4) as i:
                enter(i, {ev_used: 4, w_lo_ready: 4})
                for j in range(4):
                    each(j, i, take(panel + j, i))
                leave(n // 4)

        dve.wait_ge(consts_in, 32)
        low(0)
        low(1)
        dve.wait_ge(x_in, 16)
        norm_split_of("mix_pre")
        dve.wait_ge(first_in, 16)
        c64, s64 = table(first, FIRST, "rope_c"), table(first, FIRST, "rope_s")

        def rope_parts(src, hi, lo):
            rope(src, tmp[:, 2, :], c64, s64, tmp[:, 3, :])
            used(parts(hi, lo, tmp[:, 2, :]))

        for panel in range(RET_Q, RET_V):
            t = panel % 2
            hi, lo = (rq_hi, rq_lo) if panel < RET_K else (rk_hi, rk_lo)
            rope_parts(take(panel), hi[:, t, :], lo[:, t, :])
        for t, src in take_four(RET_V):
            link(V.tensor_reduce(r4[:, 4, :], fours(src), AX.X, ALU.add))
            link(V.tensor_scalar(r4[:, 5, :], r4[:, 4, :], -1.0 / P, None, ALU.mult))
            used(V.tensor_tensor(fours(rv[:, t, :]), fours(src), wide(r4[:, 5, :]), ALU.add))
        for t in range(4):
            used(V.tensor_copy(rg[:, t, :], take(RET_G + t)))
        for kv in range(2):
            src = take(CMP_IN + kv)
            if kv:
                dve.wait_ge(cmp_in_ready, 1)
            for g in range(2):
                for odd in range(2):
                    r = slice(64 * odd, 64 * odd + 64)
                    by_block = src[64 * g:64 * g + 64, :].rearrange("p (n i two) -> p i n two", i=8, two=2)
                    for later in range(2):
                        out = xg_f[r, 8 * later:8 * later + 8, 31 * g:31 * g + 31]
                        pos = small[64 * g:64 * g + 64, SMALL["cmp_pos"][0]:SMALL["cmp_pos"][0] + 64]
                        pos = pos.rearrange("p (kv two i) -> p kv two i", kv=2, two=2)[:, kv, odd, 8 * later:8 * later + 8]
                        last = V.tensor_tensor(out, by_block[:, :, later:later + 31, odd],
                                               pos.unsqueeze(2).to_broadcast([64, 8, 31]), ALU.add)
            used(last)
            dve.wait_ge(ev_used, output_of(CMP_IN + kv) + 1)
            signal(parts(xg_hi[:, kv, :, :], xg_lo[:, kv, :, :], xg_f[:, :, :]), cmp_in_ready)
        for t in range(4):
            rope_parts(take(NSA_Q + t), nq_hi[:, t, :], nq_lo[:, t, :])
        for t in range(2):
            rope_parts(take(NSA_K + t), nk_hi[:, t, :], nk_lo[:, t, :])
        dve.wait_ge(pool_set, 7)
        for t, src in take_four(NSA_V):
            by = src[:, 0:256].rearrange("p (s g d) -> p s g d", s=2, g=2)
            V.tensor_copy(nv[:, t, :, 0, 0:64], by[:, :, 0, :])
            used(V.tensor_copy(nv[:, t, :, 1, 64:P], by[:, :, 1, :]))
        used(V.tensor_copy(gates[:, :, :], fours(take(NSA_GATE)[:, 0:P])))
        for kv in range(2):
            panel, o = CMP_W1 + 4 * kv, CMP_W1 + 2 * kv
            for c in range(4):
                low(panel + c + 2)
            for m in range(2):
                dve.wait_ge(tile_out, o + m + 1)
                src = ev[:, (o + m) % 4, :]
                if kv == 0:
                    link(V.tensor_copy(ch_hi[:, m, 0:62], src[:, 0:62]))
                    last = V.tensor_tensor(ch_lo[:, m, 0:62], src[:, 0:62], ch_hi[:, m, 0:62].bitcast(F32), ALU.subtract)
                else:
                    by = src[:, 0:62].rearrange("p (g n) -> p g n", g=2)
                    link(V.tensor_copy(cv_hi[:, m, :, 0:31], by))
                    last = V.tensor_tensor(cv_lo[:, m, :, 0:31], by, cv_hi[:, m, :, 0:31].bitcast(F32), ALU.subtract)
                used(last)
                dve.wait_ge(ev_used, o + m + 1)
                signal(V.memset(r4[:, 2, 0:1], 0.0), cmp_hid_ready)
        low(CMP_W2 + 2)
        dve.wait_ge(tile_out, CMP_W1 + 5)
        src = ev[:, (CMP_W1 + 4) % 4, :]
        V.tensor_copy(kc_f[0:64, 0, 0:31], src[0:64, 0:31])
        used(V.tensor_copy(kc_f[64:P, 0, 0:31], src[64:P, 31:62]))
        dve.wait_ge(ev_used, CMP_W1 + 5)
        rope(kc_f[:, 0, 0:31], kc_f[:, 1, 0:31], table(first, FIRST, "cmp_c")[:, 0:31],
             table(first, FIRST, "cmp_s")[:, 0:31], kc_f[:, 2, 0:31])
        signal(parts(kc_hi[:, 0:31], kc_lo[:, 0:31], kc_f[:, 1, 0:31]), cmp_ready)
        for g in range(2):
            dve.wait_ge(tile_out, CMP_W1 + 6 + g)
            used(V.tensor_copy(vc[:, g, 64 * g:64 * g + 64], ev[:, (CMP_W1 + 5 + g) % 4, 0:64]))
            dve.wait_ge(ev_used, CMP_W1 + 6 + g)
            signal(V.memset(r4[:, 2, 0:1], 0.0), cmp_ready)

        decay = table(first, FIRST, "decay")
        for h in range(4):
            for kt in range(NT):
                m = 4 * h + kt
                dve.wait_ge(ret_s, m + 1)
                if m >= 4:
                    dve.wait_ge(ret_pv, m - 3)
                signal(V.tensor_tensor(at1["pr"][:, m % 4, kt * P:S], ps[:, 4 + m % 2, kt * P:S],
                                decay[:, 512 * h:512 * h + S - kt * P], ALU.mult), ret_p)
            if h:
                norm_head(f"ret{h - 1}", col("gn", h - 1), rg[:, h - 1, :], h - 1)
        norm_head("ret3", col("gn", 3), rg[:, 3, :], 3)

        def largest(u):
            n, at = u["n"], u["at"]
            if u["kind"] == "cmp":
                dve.wait_ge(mx_ready, 4 * n + 4)
                signal(V.tensor_reduce(at["mx"][:, n % 2, :], ps[:, 2, 0:P].rearrange("p (a b) -> p a b", a=4), AX.X, ALU.max), mx_done, 4)
            else:
                for t in range(NT):
                    keys = (t + 1) * P if u["kind"] == "causal" else S
                    dve.wait_ge(mx_ready, 4 * n + t + 1)
                    signal(V.tensor_reduce(at["mx"][:, n % 2, t:t + 1], ps[:, 2 + t % 2, 0:keys], AX.X, ALU.max), mx_done)
            dve.wait_ge(mx_done, 4 * n + 4)
            signal(V.tensor_scalar(at["negm"][:, n % 2, :], at["mx"][:, n % 2, :], -1e20, -1.0, ALU.max, ALU.mult), negm_ready)

        def shift_of(u):
            n = u["n"]
            dve.wait_ge(negm_turned, n + 1)
            signal(V.tensor_tensor(fours(u["at"]["shift"][:, n % 2, :]), ps[0:4, 1, 0:P].unsqueeze(1).to_broadcast([4, 4, P]),
                            ident[0:4, 0:4].unsqueeze(2).to_broadcast([4, 4, P]), ALU.mult), shift_ready)

        def inverse_sums(u):
            n, at = u["n"], u["at"]
            dve.wait_ge(den_ready, n + 1)
            link(V.tensor_scalar(at["w4"][:], ps[:, 1, 256:260], 1e-30, None, ALU.max))
            link(V.reciprocal(at["w4"][:], at["w4"][:]))
            if u["gate"] is not None:
                link(V.tensor_tensor(at["w4"][:], at["w4"][:], gates[:, :, u["gate"]], ALU.mult))
            if n:
                dve.wait_ge(den_wide, n)
            signal(V.tensor_tensor(fours(at["wd"][:]), ident.unsqueeze(1).to_broadcast([P, 4, P]), wide(at["w4"][:]),
                            ALU.mult), den_diag)

        def result(u):
            n, r, at = u["n"], u["num"], u["at"]
            dve.wait_ge(den_wide, n + 1)
            o = at["macc"][r, :] if u["s"] == 0 else at["nt"][r, :]
            signal(V.tensor_tensor(o, at["osb"][r, n % 2, :], ps[r, 7, :], ALU.mult), o_used)
            dve.wait_ge(o_used, n + 1)
            if u["s"]:
                link(V.tensor_tensor(at["macc"][r, :], at["macc"][r, :], o, ALU.add))
            if u["half"] == 1 and (u["s"] == 2 or u["gate"] is None):
                k = u["t"] if u["gate"] is None else 4 + u["t"]
                signal(parts(h_hi[:, k, :], h_lo[:, k, :], at["macc"][:]), mix_ready)

        nsa = units[:NSA_UNITS]
        largest(nsa[0])
        largest(nsa[1])
        shift_of(nsa[0])
        for n, u in enumerate(nsa):
            if n:
                inverse_sums(nsa[n - 1])
            if n + 2 < NSA_UNITS:
                largest(nsa[n + 2])
            if n:
                result(nsa[n - 1])
            if n + 1 < NSA_UNITS:
                shift_of(nsa[n + 1])
        inverse_sums(nsa[-1])
        result(nsa[-1])

        take_run(OUT1, KD, lambda j, i, src: used(V.tensor_copy(y[:, plus(j, i, 4), :], src)))
        dve.wait_ge(ev_used, FF0_O)
        norm_add("mix_post")
        dve.wait_ge(x_ready, KD)
        norm_split_of("ffn_pre")
        conv0 = SMALL["conv0"][0]

        def hidden_low(k, slot, value):
            dve.wait_ge(hid_hi_ready, value)
            signal(V.tensor_tensor(hid_lo[:, k, :], hid_f[:, slot, :], hid_hi[:, k, :].bitcast(F32), ALU.subtract), hid_lo_ready)

        panel, hidden = FF0, 0
        for c, tiles in enumerate(FF0_CHUNKS):
            def pair(j, i=None, skip=False):
                q = hidden + j
                for side in range(2):
                    src = take(panel + 2 * j + side, i)
                    t = conv_t[:, side, :]

                    def tap(n):
                        at = plus(conv0 + (2 * q + side) * 3 + n, i, 12)
                        return small[:, at:at + 1] if i is None else small[:, bass.ds(at, 1)]

                    link(V.tensor_scalar(t, src, tap(2), None, ALU.mult))
                    link(V.scalar_tensor_tensor(t[:, 1:S], src[:, 0:S - 1], tap(1), t[:, 1:S], ALU.mult, ALU.add))
                    used(V.scalar_tensor_tensor(t[:, 2:S], src[:, 0:S - 2], tap(0), t[:, 2:S], ALU.mult, ALU.add))
                    dve.wait_ge(ev_used, plus(output_of(panel) + 2 * j + side + 1, i, 4))
                dve.wait_ge(gelu_done, plus(q + 1, i, 2))
                signal(V.tensor_tensor(hid_f[:, j % 2, :], act_t[:], conv_t[:, 1, :], ALU.mult), hid_ready)
                if not skip:
                    hidden_low(plus(j - 1, i, 2), (j - 1) % 2, plus(q, i, 2))

            pair(0, skip=True)
            pair(1)
            with dve.Fori(1, tiles // 2) as i:
                enter(i, {ev_used: 4, w_lo_ready: 4, dve_step: 4 * 2, hid_ready: 2, hid_lo_ready: 2}, first=1)
                pair(0, i)
                pair(1, i)
                leave(tiles // 2 - 1)
            hidden_low(tiles - 1, 1, hidden + tiles)
            down_panel = panel + 2 * tiles

            def gather(j, i, src):
                k = plus(j, i, 4)
                if c == 0:
                    used(V.tensor_copy(y[:, k, :], src))
                else:
                    used(V.tensor_tensor(y[:, k, :], y[:, k, :], src, ALU.add))

            take_run(down_panel, KD, gather)
            panel += 2 * tiles + KD
            hidden += tiles
        dve.wait_ge(ev_used, output_of(AB_GATE))
        norm_add("ffn_post")
        dve.wait_ge(x_ready, 2 * KD)
        norm_split_of("ab")

        src = take(AB_GATE)
        signal(V.tensor_scalar(gt[:, 0, :], src, col("gate_b"), None, ALU.add), gate_raw)
        dve.wait_ge(gate_raw, 1)
        used(V.tensor_scalar(li[:, :], src[0:64, :], col("gate_b")[0:64, :], None, ALU.add))
        dve.wait_ge(ev_used, output_of(AB_GATE) + 1)
        signal(V.memset(r4[:, 2, 0:1], 0.0), gate_raw)
        link(V.memset(scan[:, :, :], 0.0))
        dve.wait_ge(gate_ln, 1)
        mid = slice(256, 768)
        link(V.scalar_tensor_tensor(scan[:, 0, mid], gt[64:P, 0, :], 0.0, gt[64:P, 1, :], ALU.min, ALU.subtract))

        def scan_all(op):
            for n in range(9):
                a, b = n % 2, 1 - n % 2
                V.tensor_tensor(scan[0:32, b, mid], scan[0:32, a, mid], scan[0:32, a, 256 - 2 ** n:768 - 2 ** n], op)
                link(V.tensor_tensor(scan[32:64, b, mid], scan[32:64, a, mid], scan[32:64, a, 256 + 2 ** n:768 + 2 ** n], op))

        scan_all(ALU.add)
        link(V.tensor_copy(neg_m[:, :], scan[:, 1, mid]))
        signal(V.tensor_tensor(la[:, :], li[:, :], neg_m[:, :], ALU.subtract), a_ready)
        dve.wait_ge(a_ready, 1)
        link(V.memset(scan[:, :, :], NEG))
        link(V.tensor_copy(scan[:, 0, mid], la[:, :]))
        scan_all(ALU.max)
        link(V.tensor_scalar(scan[:, 0, mid], scan[:, 1, mid], 0.0, None, ALU.max))
        link(V.tensor_tensor(floor_m[:, :], neg_m[:, :], scan[:, 0, mid], ALU.add))
        signal(V.tensor_scalar(neg_m[:, :], scan[:, 0, mid], -1.0, None, ALU.mult), scan_floor)

        conv1 = SMALL["conv1"][0]
        for n in range(8):
            src = take(AB_QK + n)
            t = qk_f[:, 0, :]

            def tap(k):
                return small[:, conv1 + 5 * n + k:conv1 + 5 * n + k + 1]

            def add_tap(k, a, b):
                return V.scalar_tensor_tensor(t[:, a:b], src[:, a + k - 2:b + k - 2], tap(k), t[:, a:b], ALU.mult, ALU.add)

            link(V.tensor_scalar(t, src, tap(2), None, ALU.mult))
            link(add_tap(1, 1, S))
            link(add_tap(0, 2, S))
            link(add_tap(3, 0, S - 1))
            used(add_tap(4, 0, S - 2))
            dve.wait_ge(ev_used, output_of(AB_QK) + n + 1)
            signal(V.memset(r4[:, 2, 0:1], 0.0), qk_conv)
            dve.wait_ge(qk_silu, n + 1)
            link(parts(aq_hi[:, n, :], aq_lo[:, n, :], qk_f[:, 1, :]))
        dve.wait_ge(a_turned, 1)
        signal(V.tensor_copy(a_t[:, :, :], ps[:, 6, 0:256].rearrange("p (a b) -> p a b", a=4)), a_col)
        for t, src in take_four(AB_V):
            used(V.tensor_copy(av[:, t, :], src))
        for t in range(4):
            used(V.tensor_copy(ao[:, t, :], take(AB_O + t)))
        dve.wait_ge(second_in, 16)
        for t, src in take_four(AB_VB):
            link(V.tensor_tensor(tmp[:, 2, :], src, src, ALU.mult))
            link(V.tensor_reduce(r4[:, 4, :], fours(tmp[:, 2, :]), AX.X, ALU.add))
            signal(V.tensor_scalar(r4[:, 2, :], r4[:, 4, :], 1.0 / P, 1e-6, ALU.mult, ALU.add), vb_ms)
            dve.wait_ge(vb_inv, t + 1)
            link(V.tensor_tensor(fours(tmp[:, 3, :]), fours(src), wide(r4[:, 3, :]), ALU.mult))
            used(V.tensor_tensor(vb[:, t, :], tmp[:, 3, :], table(second, SECOND, "g_v"), ALU.mult))

        def gt_u(g):
            return gt[:, g, :] if g < 3 else qk_f[:, 0, :]

        for g in range(4):
            used(V.tensor_copy(gt_u(g), take(AB_U + g)))
        for g in range(4):
            dve.wait_ge(sgu_ready, g + 1)
            b = table(second, SECOND, "sgu_b")[:, g * P:(g + 1) * P].unsqueeze(1).to_broadcast([P, 4, P])
            signal(V.tensor_tensor(fours(tmp[:, 2, :]), fours(ps[:, g, :]), b, ALU.add), sgu_read)
            dve.wait_ge(sgu_read, g + 1)
            link(V.tensor_tensor(tmp[:, 2, :], tmp[:, 2, :], gt_u(g), ALU.mult))
            link(parts(h_hi[:, 4 + g, :], h_lo[:, 4 + g, :], tmp[:, 2, :]))
            signal(V.memset(r4[:, 2, 0:1], 0.0), mix_ready)

        for h in range(4):
            for n, kt in enumerate((0, 3, 1, 2)):
                at = slice(kt * P, (kt + 1) * P)
                for d in range(2):
                    m = 8 * h + 2 * n + d
                    dve.wait_ge(row_out, 4 * h + 2 * d + 1)
                    if m >= 2:
                        dve.wait_ge(ml_decay, m - 1)
                    signal(V.tensor_tensor(diag[:, m % 2, :], rows[:, 2 * d, at], mask("k_q" if d == 0 else "q_k"), ALU.add), ml_diag)
                dve.wait_ge(ml_s, 4 * h + n + 1)
                for d in range(2):
                    m = 8 * h + 2 * n + d
                    a, b = (kt * P, S) if d == 0 else (0, (kt + 1) * P)
                    dve.wait_ge(ml_decay, m + 1)
                    if m >= 4:
                        dve.wait_ge(ml_pv, m // 4 * 4)
                    signal(V.scalar_tensor_tensor(weights[:, m % 4, a:b], ps[:, 4 + n % 2, a:b], P ** -0.5, decays[:, m % 2, a:b],
                                           ALU.mult, ALU.mult), ml_p)
            dve.wait_ge(ml_pv, 8 * h + 8)
            dve.wait_ge(row_out, 4 * h + 4)
            for d in range(2):
                link(V.tensor_tensor(den[:, :], ps[:, 2 * d + 1, :], rows[:, 2 * d + 1, :], ALU.max))
                link(V.scalar_tensor_tensor(den[:, :], ps[:, 2 * d + 1, :], -1.0, den[:, :], ALU.mult, ALU.max))
                link(V.reciprocal(den[:, :], den[:, :]))
                signal(V.tensor_tensor(part[:, 1 - d, :], ps[:, 2 * d, :], den[:, :], ALU.mult), ml_read)
                dve.wait_ge(ml_read, 2 * h + d + 1)
            signal(V.tensor_tensor(part[:, 1, :], part[:, 1, :], part[:, 0, :], ALU.add), ml_o)
            norm_head(f"head{h}", col("g_head", h), ao[:, h, :], h)

        def feed_forward(panel, name, hidden):
            norm_split_of(name)
            o = output_of(panel)
            with dve.Fori(0, FF_CHUNKS) as c:
                enter(c, {ev_used: 16, w_lo_ready: 16, hid_lo_ready: 8})
                i = c * 4
                for k in range(8):
                    src = take(panel + k, i)
                    used(V.tensor_tensor(hid_f[:, k % 2, :], src, src, ALU.mult))
                    if k:
                        hidden_low(k - 1, (k - 1) % 2, plus(hidden + k, c, 8))
                hidden_low(7, 1, plus(hidden + 8, c, 8))
                for k in range(8):
                    src = take(panel + 8 + k, i)
                    used(V.tensor_tensor(x[:, k, :], x[:, k, :], src, ALU.add))
                leave(FF_CHUNKS)

        def add_to_x(j, i, src):
            used(V.tensor_tensor(x[:, plus(j, i, 4), :], x[:, plus(j, i, 4), :], src, ALU.add))

        take_run(OUT2, KD, add_to_x)
        dve.wait_ge(ev_used, FF1_O)
        feed_forward(FF1, "ffn1", sum(FF0_CHUNKS))

        dve.wait_ge(ev_used, output_of(C_IN))
        norm_split_of("c")
        rr = slice(64, 96)
        dve.wait_ge(pos_in, 16)
        TWO_PI, MAGIC = 2 * np.pi, 1.5 * 2.0 ** 23
        C1, C2 = 6.28125, 0.0019350051879882812
        C3 = TWO_PI - C1 - C2
        link(V.tensor_copy(ang[rr, 2, :], pos_i[rr, :]))
        link(V.tensor_scalar(ang[rr, 0, :], ang[rr, 2, :], col("freq")[rr, :], None, ALU.mult))
        for d in range(2):
            quarter = 0.25 * (1 - d)
            k, r = c_raw[rr, 0, :], ang[rr, 1 + d, :]
            link(V.tensor_scalar(k, ang[rr, 0, :], 1 / TWO_PI, quarter, ALU.mult, ALU.add))
            link(V.tensor_scalar(k, k, MAGIC, None, ALU.add))
            link(V.tensor_scalar(k, k, MAGIC, None, ALU.subtract))
            link(V.scalar_tensor_tensor(r, k, -C1, ang[rr, 0, :], ALU.mult, ALU.add))
            link(V.scalar_tensor_tensor(r, k, -C2, r, ALU.mult, ALU.add))
            link(V.scalar_tensor_tensor(r, k, -C3, r, ALU.mult, ALU.add))
            link(V.tensor_scalar(r, r, quarter * TWO_PI, None, ALU.add))
            signal(V.tensor_scalar(r, r, 3.1415925, -3.1415925, ALU.min, ALU.max), ang_ready)
            dve.wait_ge(ang_ready, d + 1)
        for k in range(5):
            used(V.tensor_copy(c_raw[:, k, :], take(C_IN + k)))
        src = take(C_IN + 5)
        dve.wait_ge(trig_ready, 2)
        link(V.tensor_scalar(trig[rr, 1, :], trig[rr, 1, :], col("rope_sign")[rr, :], None, ALU.mult))
        cos, sin = trig[rr, 0, :], trig[rr, 1, :]
        rope(src[rr, :], ang[rr, 0, :], cos, sin, ang[rr, 1, :])
        used(parts(kr_hi[rr, :], kr_lo[rr, :], ang[rr, 0, :]))
        dve.wait_ge(ev_used, output_of(MLA))
        norm_split_of("cq")
        norm_split_of("ckv")

        def projected(n):
            s, o = n % 2, output_of(MLA) + 3 * n
            low(MLA + n + 1) if n else None
            dve.wait_ge(tile_out, o + 1)
            src = ev[:, o % 4, :]
            rope(src[rr, :], ang[rr, 0, :], cos, sin, ang[rr, 1, :])
            V.tensor_copy(qf_hi[0:64, s, :], src[0:64, :])
            link(V.tensor_copy(qf_hi[rr, s, :], ang[rr, 0, :]))
            V.tensor_tensor(qf_lo[rr, s, :], ang[rr, 0, :], qf_hi[rr, s, :].bitcast(F32), ALU.subtract)
            used(V.tensor_tensor(qf_lo[0:64, s, :], src[0:64, :], qf_hi[0:64, s, :].bitcast(F32), ALU.subtract))
            V.tensor_copy(kf_hi[rr, s, :], kr_hi[rr, :])
            V.tensor_copy(kf_lo[rr, s, :], kr_lo[rr, :])
            dve.wait_ge(tile_out, o + 2)
            src = ev[:, (o + 1) % 4, :]
            link(V.tensor_copy(kf_hi[0:64, s, :], src[0:64, :]))
            used(V.tensor_tensor(kf_lo[0:64, s, :], src[0:64, :], kf_hi[0:64, s, :].bitcast(F32), ALU.subtract))
            dve.wait_ge(tile_out, o + 3)
            src = ev[:, (o + 2) % 4, 0:256]
            used(V.tensor_copy(vh[:, s, :, 64 * s:64 * s + 64], fours(src)))
            dve.wait_ge(ev_used, o + 3)
            signal(V.memset(r4[:, 2, 0:1], 0.0), head_ready)

        mla = units[NSA_UNITS:]
        dve.wait_ge(pool_set, 8)
        projected(0)
        largest(mla[0])
        shift_of(mla[0])
        for n, u in enumerate(mla):
            if n:
                inverse_sums(mla[n - 1])
                result(mla[n - 1])
            if n + 1 < HEADS:
                projected(n + 1)
                largest(mla[n + 1])
                shift_of(mla[n + 1])
        low(OUT3 + 1)
        inverse_sums(mla[-1])
        result(mla[-1])

        take_run(OUT3, KD, add_to_x)
        dve.wait_ge(ev_used, FF2_O)
        feed_forward(FF2, "ffn2", sum(FF0_CHUNKS) + 8 * FF_CHUNKS)
        dve.wait_ge(ev_used, output_of(PANELS_USED))
        inverse("final")
        for k in range(KD):
            scaled("final", k, col("g_final", k), out=y[:, k, :])


def swapped_order():
    return np.concatenate([np.arange(0, 16), np.arange(32, 48), np.arange(16, 32), np.arange(48, 64)])


def by_feature(w, cols):
    cols = np.asarray(cols)
    out = np.zeros((len(cols) // P, P, PANEL), np.float32)
    for n in range(len(cols) // P):
        c = cols[n * P:(n + 1) * P]
        block = np.zeros((w.shape[0], P), np.float32)
        block[:, c >= 0] = w[:, c[c >= 0]]
        kt = w.shape[0] // P
        out[n, :, :kt * P] = block.reshape(kt, P, P).transpose(1, 0, 2).reshape(P, kt * P)
    return out


def by_token(w, width):
    out = np.zeros((4, P, 2, 512), np.float32)
    out[:, :, :, :width] = w.reshape(4, 2, P, width).transpose(0, 2, 1, 3)
    return out.reshape(4, P, PANEL)


def lay_panels(a):
    order = swapped_order()
    w = a["w_in"][0]
    heads = lambda at, hs: np.concatenate([at + 64 * h + order for h in hs])
    out = [by_feature(w, heads(0, range(4))), by_feature(w, heads(256, range(4))), by_token(w[:, 512:1024], 512),
           by_feature(w, np.arange(1024, 1536)), by_feature(w, np.arange(2048, 2304)),
           by_feature(w, np.concatenate([heads(1536, (t, 4 + t)) for t in range(4)])),
           by_feature(w, heads(2304, range(2))), by_feature(w, heads(2560, range(2))),
           by_token(np.concatenate([w[:, 2432:2560], w[:, 2688:2816]], 1), 256)]
    gate = np.zeros((1, P, PANEL), np.float32)
    g = np.zeros((P, KD, 32), np.float32)
    g[:, :, :24] = w[:, 2816:2840].reshape(KD, P, 24).transpose(1, 0, 2)
    gate[0, :, :256] = g.reshape(P, 256)
    out.append(gate)
    for name in ("cmp_k_w1", "cmp_v_w1"):
        out.append(a[name][0].reshape(4, 4, P, 256).transpose(0, 2, 1, 3).reshape(4, P, PANEL))
    w2 = np.zeros((1, P, PANEL), np.float32)
    k2, v2 = a["cmp_k_w2"][0][:, order], a["cmp_v_w2"][0]
    for m in range(2):
        w2[0, :, m * P:m * P + 64] = k2[m * P:(m + 1) * P]
        w2[0, :, m * P + 64:(m + 1) * P] = k2[m * P:(m + 1) * P]
        w2[0, :, 256 + 64 * m:320 + 64 * m] = v2[m * P:(m + 1) * P]
    out.append(w2)
    rows = np.concatenate([np.arange(512)] + [512 + 64 * h + np.arange(64) for t in range(4) for h in (t, 4 + t)])
    out.append(by_feature(a["w_out"][0][rows], np.arange(D)))

    def down(w, at, tiles):
        part = w[at * P:(at + tiles) * P]
        return by_feature(part, np.arange(D))

    up, dn = a["ffn_w_up"][0], a["ffn_w_down"][0]
    half, at = up.shape[1] // 2, 0
    for tiles in FF0_CHUNKS:
        cols = np.concatenate([side * half + (at + t) * P + np.arange(P) for t in range(tiles) for side in range(2)])
        out += [by_feature(up, cols), down(dn, at, tiles)]
        at += tiles
    w = a["ab_w_in_2"][0]
    gates = -np.ones(P, int)
    for n, row in enumerate((0, 64, 32, 96)):
        gates[row:row + 4] = 2048 + 4 * n + np.arange(4)
    out += [by_feature(w, gates), by_feature(w, np.arange(1024)), by_token(w[:, 1024:1536], 512),
            by_feature(w, np.arange(1536, 2048)), by_token(w[:, 2576:3088], 512), by_feature(w, np.arange(2064, 2576)),
            by_feature(a["ab_w_out_2"][0], np.arange(D))]

    def feed_forward(n):
        for c in range(FF_CHUNKS):
            out.append(by_feature(a["ffn_w1_2"][n], np.arange(c * 1024, (c + 1) * 1024)))
            out.append(down(a["ffn_w2_2"][n], c * 8, 8))

    feed_forward(0)
    kr = -np.ones(P, int)
    kr[64:96] = 640 + np.arange(32)
    out.append(by_feature(a["c_w_in_2"][0], np.concatenate([np.arange(640), kr])))
    uq, ukv = a["c_w_uq_2"][0], a["c_w_ukv_2"][0]
    mla = np.zeros((HEADS, P, PANEL), np.float32)
    for h in range(HEADS):
        for k in range(3):
            mla[h, :, k * P:k * P + 96] = uq[k * P:(k + 1) * P, h * 96:(h + 1) * 96]
        for k in range(2):
            mla[h, :, 384 + k * P:448 + k * P] = ukv[k * P:(k + 1) * P, h * P:h * P + 64]
            mla[h, :, 640 + k * 64:704 + k * 64] = ukv[k * P:(k + 1) * P, h * P + 64:(h + 1) * P]
    out += [mla, by_feature(a["c_w_out_2"][0], np.arange(D))]
    feed_forward(1)
    out.append(np.zeros((PANELS - PANELS_USED, P, PANEL), np.float32))
    out = np.concatenate(out)
    assert out.shape == (PANELS, P, PANEL), out.shape
    return out


def lay_small(a):
    out = np.zeros((P, SMALL_N), np.float32)

    def put(name, value):
        at, n = SMALL[name]
        out[:, at:at + n] = value

    def columns_of(v):
        return np.asarray(v).reshape(-1, P).T

    put("ident", np.eye(P))
    put("ones", 1.0)
    for name, key in (("g_mix_pre", "norm_mix_pre"), ("g_mix_post", "norm_mix_post"), ("g_ffn_pre", "norm_ffn_pre"),
                      ("g_ffn_post", "norm_ffn_post"), ("gn", "ret_gn_w"), ("g_ab", "ab_norm_2"), ("g_head", "ab_head_g_2"),
                      ("g_c", "c_norm_2"), ("g_cq", "c_q_g_2"), ("g_ckv", "c_kv_g_2"), ("g_final", "final_norm_2")):
        put(name, columns_of(a[key]))
    put("g_ffn1", columns_of(a["ffn_norm_2"][0]))
    put("g_ffn2", columns_of(a["ffn_norm_2"][1]))
    pos = np.stack([a["cmp_k_pos"][0], a["cmp_v_pos"][0]])
    pos = pos.reshape(2, 16, 2, 64).transpose(3, 0, 2, 1).reshape(64, 64)
    put("cmp_pos", np.concatenate([pos, pos]))
    conv = a["ffn_conv"][0].reshape(3, 2, 22, P).transpose(3, 2, 1, 0)
    put("conv0", conv.reshape(P, 132))
    put("conv1", a["ab_conv_2"][0].reshape(5, 8, P).transpose(2, 1, 0).reshape(P, 40))
    at = SMALL["gate_b"][0]
    for n, row in enumerate((0, 64, 32, 96)):
        out[row:row + 4, at] = a["ab_gate_b_2"][0][4 * n:4 * n + 4]
    freq = (np.float32(10000.0) ** (-np.arange(16, dtype=np.float32) / np.float32(16))).astype(np.float32)
    put("freq", np.tile(freq, 8)[:, None])
    put("rope_sign", np.tile(np.repeat([-1.0, 1.0], 16), 4)[:, None])
    put("minus_half", -0.5)
    return out


def rope_tables(positions):
    inv = 1.0 / (np.float32(10000.0) ** (np.arange(0, 64, 2, dtype=np.float32) / np.float32(64)))
    ang = (positions.astype(np.float32)[:, None] * inv.astype(np.float32)[None, :]).astype(np.float64)
    p = np.arange(P)
    f = p % 16 + 16 * (p // 32 % 2)
    sign = np.where(p % 32 < 16, -1.0, 1.0)
    return np.cos(ang)[:, f].T, np.sin(ang)[:, f].T * sign[:, None]


def lay_first():
    out = np.zeros((P, FIRST_N), np.float32)

    def put(name, value):
        at = FIRST[name][0]
        out[:, at:at + value.shape[1]] = value

    c, s = rope_tables(np.arange(S))
    put("rope_c", c)
    put("rope_s", s)
    c, s = rope_tables(np.arange(31) * 16 + 31)
    put("cmp_c", c)
    put("cmp_s", s)
    diff = np.arange(S)[None, :] - np.arange(P)[:, None]
    decay = [np.where(diff >= 0, np.exp(np.log(1.0 - 2.0 ** (-5.0 - h)) * np.maximum(diff, 0)), 0.0) * 64 ** -0.5
             for h in range(4)]
    put("decay", np.concatenate(decay, 1))
    return out


def lay_second(a):
    out = np.zeros((P, SECOND_N), np.float32)
    out[:, 0:512] = a["ab_bs_2"][0].reshape(1, 512)
    out[:, 512:1024] = a["ab_v_g_2"][0][None, :]
    out[:, 1024:] = a["ab_ws_2"][0].transpose(2, 0, 1).reshape(P, 512)
    return out


def lay_masks(dtype):
    out = np.zeros((P, MASKS_N), np.float32)

    def put(name, value):
        out[:, MASKS[name][0]:MASKS[name][0] + value.shape[1]] = value

    r, c = np.arange(P)[:, None], np.arange(P)[None, :]
    put("ident", np.eye(P))
    put("q_k", np.where(c > r, NEG, 0.0))
    put("k_q", np.where(r > c, NEG, 0.0))
    key, query = np.arange(P), np.arange(S)
    bad = (key[:, None] * 16 + 31 > query[None, :]) | (key[:, None] >= 31)
    put("cmp_k_q", np.where(bad, NEG, 0.0))
    by_tile = np.where(bad, NEG, 0.0)[:32].reshape(32, NT, P).transpose(2, 1, 0).reshape(P, P)
    put("cmp_q_k", by_tile)
    return out.astype(dtype)


def kernel(**inputs):
    import concourse.bacc as bacc
    from concourse.bass_utils import run_bass_kernel_spmd

    a = {k: np.asarray(v) for k, v in inputs.items()}
    bf16 = mybir.dt.np(BF16)
    arrays = {
        "in_panels": lay_panels(a), "in_small": lay_small(a), "in_first": lay_first(), "in_second": lay_second(a),
        "in_masks": lay_masks(bf16), "in_x": np.ascontiguousarray(a["x"][0].T.reshape(KD, P, S)),
        "in_positions": np.ascontiguousarray(np.broadcast_to(a["positions_2"].astype(np.int32), (32, S))),
    }
    nc = bacc.Bacc("TRN2", target_bir_lowering=False, num_devices=1)
    dram = {name[3:]: nc.dram_tensor(name, v.shape, mybir.dt.from_np(v.dtype), kind="ExternalInput").ap()
            for name, v in arrays.items()}
    dram["out"] = nc.dram_tensor("out_0", (KD, P, S), F32, kind="ExternalOutput").ap()
    build(nc, dram)
    r = run_bass_kernel_spmd(nc, [arrays], core_ids=[0])
    return np.ascontiguousarray(np.asarray(r.results[0]["out_0"]).reshape(D, S).T)[None]
```

```python
from contextlib import ExitStack

import numpy as np

import concourse.bass as bass
from concourse import mybir

F32 = mybir.dt.float32
F32R = mybir.dt.float32r
BF16 = mybir.dt.bfloat16
I32 = mybir.dt.int32
ACT = mybir.ActivationFunctionType
ALU = mybir.AluOpType
AX = mybir.AxisListType

P = 128
S = 512
NT = S // P
D = 1024
KD = D // P
PANEL = 1024
NEG = -1e30
HALF_SWAP = [*range(16, 32), *range(16)]

RET_Q, RET_K, RET_V, RET_G = 0, 2, 4, 8
CMP_IN, NSA_Q, NSA_K, NSA_V, NSA_GATE = 12, 14, 18, 20, 24
CMP_W1, CMP_W2, OUT1 = 25, 33, 34
FF0 = 42
FF0_CHUNKS = [8, 8, 6]
AB_GATE = FF0 + sum(2 * c + KD for c in FF0_CHUNKS)
AB_QK = AB_GATE + 1
AB_V, AB_O, AB_VB, AB_U = AB_QK + 8, AB_QK + 12, AB_QK + 16, AB_QK + 20
OUT2 = AB_U + 4
FF1 = OUT2 + KD
FF_CHUNKS = 4
C_IN = FF1 + FF_CHUNKS * 16
MLA_V = C_IN + 6
MLA = MLA_V + 2
HEADS = 16
OUT3 = MLA + HEADS
FF2 = OUT3 + KD
PANELS_USED = FF2 + FF_CHUNKS * 16
PANELS = (PANELS_USED + 2 + 3) // 4 * 4


def columns(*parts):
    at, out = 0, {}
    for name, n in parts:
        out[name] = (at, n)
        at += n
    return out, at


SMALL, SMALL_N = columns(
    ("ident", 128), ("ones", 128), ("g_mix_pre", 8), ("g_mix_post", 8), ("g_ffn_pre", 8), ("g_ffn_post", 8),
    ("gn", 4), ("cmp_pos", 64), ("conv0", 132), ("g_ab", 8), ("conv1", 40), ("gate_b", 1), ("g_head", 4),
    ("g_c", 8), ("g_cq", 3), ("g_ckv", 2), ("g_ffn1", 8), ("g_ffn2", 8), ("g_final", 8), ("freq", 1),
    ("rope_sign", 1), ("minus_half", 4))
FIRST, FIRST_N = columns(("rope_c", 512), ("rope_s", 512), ("cmp_c", 32), ("cmp_s", 32), ("decay", 2048))
SECOND, SECOND_N = columns(("sgu_b", 512), ("g_v", 512), ("ws_t", 512))
MASKS, MASKS_N = columns(("ident", 128), ("q_k", 128), ("k_q", 128), ("cmp_q_k", 128), ("cmp_k_q", 512))


def plus(v, i, k):
    return v if i is None else i * k + v



NORM_LIST = (
    [("mix_pre", KD, D, 1e-6)] + [(f"ret{h}", 1, P, 1e-5) for h in range(4)]
    + [("mix_post", KD, D, 1e-6), ("ffn_pre", KD, D, 1e-6), ("ffn_post", KD, D, 1e-6), ("ab", KD, D, 1e-6)]
    + [(f"head{h}", 1, P, 1e-6) for h in range(4)]
    + [("ffn1", KD, D, 1e-6), ("c", KD, D, 1e-6), ("ckv", 2, 256, 1e-6), ("cq", 3, 384, 1e-6),
       ("ffn2", KD, D, 1e-6), ("final", KD, D, 1e-6)])
NORM = {}
for _n, (_name, _k, _d, _e) in enumerate(NORM_LIST):
    NORM[_name] = (_n, sum(q[1] for q in NORM_LIST[:_n]), _k, _d, _e)
SPLIT_NORMS = ("mix_pre", "ffn_pre", "ab", "ffn1", "c", "ckv", "cq", "ffn2")
SPLITS_BEFORE = {}
_at = 0
for _name in SPLIT_NORMS:
    SPLITS_BEFORE[_name] = _at
    _at += NORM[_name][2]


def output_of(panel):
    return panel if panel <= CMP_W1 else panel - 2 if panel <= MLA_V else panel - 2 - 2 - HEADS


def attention_memory(sb, c, tag="a"):
    return dict(
        pr=sb("pr" + tag, [P, 4, S], F32, c), shift=sb("shift" + tag, [4, 2, S], F32R, c),
        negm=sb("negm" + tag, [P, 2, 4], F32, c), mx=sb("mx" + tag, [P, 2, 4], F32, c), w4=sb("w4" + tag, [P, 4], F32, c),
        osb=sb("osb" + tag, [65, 2, S], F32, c), by_token=sb("by_token" + tag, [P, 2, NT, P], F32, c), term=sb("term" + tag, [P, NT, 64], F32, c))


def build(nc, A):
    with ExitStack() as ctx:
        build_in(nc, A, ctx)


def build_in(nc, A, ctx):
    def sb(name, shape, dt, c=ctx):
        return c.enter_context(nc.sbuf_tensor(name, shape, dt))

    def sem(name):
        return ctx.enter_context(nc.semaphore(name))

    x = sb("x", [P, KD, S], F32)
    small = sb("small", [P, SMALL_N], F32)
    masks = sb("masks", [P, MASKS_N], BF16)
    raw = sb("raw", [P, 4, PANEL], F32)
    w_hi = sb("w_hi", [P, 2, PANEL], F32R)
    w_lo = sb("w_lo", [P, 2, PANEL], F32R)
    ev = sb("ev", [P, 4, S], F32)
    h_hi = sb("h_hi", [P, KD, S], F32R)
    h_lo = sb("h_lo", [P, KD, S], F32R)
    tmp = sb("tmp", [P, 4, S], F32)
    r4 = sb("r4", [P, 6, 4], F32)
    ones_r = sb("ones_r", [4, P], F32R)
    ps = ctx.enter_context(nc.psum_tensor("ps", [P, 8, S], F32))

    with ExitStack() as c:
        first = sb("first", [P, FIRST_N], F32, c)
        rq_hi, rq_lo = sb("rq_hi", [P, 2, S], F32R, c), sb("rq_lo", [P, 2, S], F32R, c)
        rk_hi, rk_lo = sb("rk_hi", [P, 2, S], F32R, c), sb("rk_lo", [P, 2, S], F32R, c)
        nq_hi, nq_lo = sb("nq_hi", [P, 4, S], F32R, c), sb("nq_lo", [P, 4, S], F32R, c)
        nk_hi, nk_lo = sb("nk_hi", [P, 2, S], F32R, c), sb("nk_lo", [P, 2, S], F32R, c)
        rv = sb("rv", [P, NT, 512], F32, c)
        rg = sb("rg", [P, 4, S], F32, c)
        nv = sb("nv", [P, NT, 2, 2, 65], F32, c)
        vc = sb("vc", [P, 2, 65], F32, c)
        gates = sb("gates", [P, NT, 32], F32, c)
        kc_hi, kc_lo = sb("kc_hi", [P, P], F32R, c), sb("kc_lo", [P, P], F32R, c)
        ch_hi, ch_lo = sb("ch_hi", [P, 2, 64], F32R, c), sb("ch_lo", [P, 2, 64], F32R, c)
        cv_hi, cv_lo = sb("cv_hi", [P, 2, 2, P], F32R, c), sb("cv_lo", [P, 2, 2, P], F32R, c)
        kc_f = sb("kc_f", [P, 4, 32], F32, c)
        with ExitStack() as cc:
            xg_f = sb("xg_f", [P, 16, 62], F32, cc)
            xg_hi, xg_lo = sb("xg_hi", [P, 2, 16, 62], F32R, cc), sb("xg_lo", [P, 2, 16, 62], F32R, cc)
        with ExitStack() as cc:
            at1 = attention_memory(sb, cc)
            ret_out = sb("ret_out", [P, 2, S], F32, cc)
        del cc
    with ExitStack() as c:
        hid_hi, hid_lo = sb("hid_hi", [P, 8, S], F32R, c), sb("hid_lo", [P, 8, S], F32R, c)
        hid_f = sb("hid_f", [P, 2, S], F32, c)
        conv_t = sb("conv_t", [P, 2, S], F32, c)
        act_t = sb("act_t", [P, S], F32, c)
        y = sb("y", [P, KD, S], F32, c)
    with ExitStack() as c:
        second = sb("second", [P, SECOND_N], F32, c)
        aq_hi, aq_lo = sb("aq_hi", [P, 8, S], F32R, c), sb("aq_lo", [P, 8, S], F32R, c)
        av = sb("av", [P, NT, 512], F32, c)
        ao = sb("ao", [P, 4, S], F32, c)
        a_t = sb("a_t", [P, NT, 64], F32, c)
        neg_m, floor_m = sb("neg_m", [64, S], F32, c), sb("floor_m", [64, S], F32, c)
        with ExitStack() as cc:
            gt = sb("gt", [P, 3, S], F32, cc)
            scan = sb("scan", [64, 2, 2 * S], F32, cc)
            li, la = sb("li", [64, S], F32, cc), sb("la", [64, S], F32, cc)
            vb = sb("vb", [P, NT, 512], F32, cc)
            qk_f = sb("qk_f", [P, 2, S], F32, cc)
        with ExitStack() as cc:
            rows = sb("rows", [P, 4, S], F32, cc)
            decays = sb("decays", [P, 2, S], F32, cc)
            diag = sb("diag", [P, 2, P], F32, cc)
            weights = sb("weights", [P, 4, S], F32, cc)
            den = sb("den", [P, S], F32, cc)
            part = sb("part", [P, 2, S], F32, cc)
    with ExitStack() as c:
        c_raw = sb("c_raw", [P, 5, S], F32, c)
        cq_hi, cq_lo = sb("cq_hi", [P, 5, S], F32R, c), sb("cq_lo", [P, 5, S], F32R, c)
        kr_hi, kr_lo = sb("kr_hi", [P, S], F32R, c), sb("kr_lo", [P, S], F32R, c)
        qf_hi, qf_lo = sb("qf_hi", [P, 2, S], F32R, c), sb("qf_lo", [P, 2, S], F32R, c)
        kf_hi, kf_lo = sb("kf_hi", [P, 2, S], F32R, c), sb("kf_lo", [P, 2, S], F32R, c)
        q_f = sb("q_f", [P, S], F32, c)
        q_turn = sb("q_turn", [P, S], F32, c)
        mla_v = sb("mla_v", [P, NT, HEADS, 65], F32, c)
        trig = sb("trig", [P, 2, S], F32, c)
        ang = sb("ang", [P, 3, S], F32, c)
        pos_i = ang[:, 0, :].bitcast(I32)
        at2 = attention_memory(sb, c, "b")

    ones = small[:, SMALL["ones"][0]:SMALL["ones"][0] + P]
    ident = small[:, SMALL["ident"][0]:SMALL["ident"][0] + P]

    def col(name, n=0, k=1):
        return small[:, SMALL[name][0] + n:SMALL[name][0] + n + k]

    def mask(name):
        return masks[:, MASKS[name][0]:MASKS[name][0] + MASKS[name][1]]

    def table(t, where, name):
        return t[:, where[name][0]:where[name][0] + where[name][1]]

    raw_in = [sem(f"raw_in{n}") for n in range(4)]
    consts_in, x_in, first_in, second_in, pos_in = (sem(n) for n in (
        "consts_in", "x_in", "first_in", "second_in", "pos_in"))
    w_hi_ready, w_lo_ready, panel_read, tile_out, ev_used = (sem(n) for n in (
        "w_hi_ready", "w_lo_ready", "panel_read", "tile_out", "ev_used"))
    sq_ready, acc_ready, ss_ready, ms_ready, inv_ready, inv_diag, inv_wide, normed, n_hi, n_lo = (sem(n) for n in (
        "sq_ready", "acc_ready", "ss_ready", "ms_ready", "inv_ready", "inv_diag", "inv_wide", "normed", "n_hi", "n_lo"))
    dve_step, pool_set, x_ready, mix_ready = (sem(n) for n in ("dve_step", "pool_set", "x_ready", "mix_ready"))
    cmp_in_ready, cmp_hid_ready, cmp_ready, v_ready = (sem(n) for n in (
        "cmp_in_ready", "cmp_hid_ready", "cmp_ready", "v_ready"))
    turned, turned_high = sem("turned"), sem("turned_high")
    v_copied, q_proj, q_scaled, q_high, q_low, k_proj, k_high, k_low = (sem(n) for n in (
        "v_copied", "q_proj", "q_scaled", "q_high", "q_low", "k_proj", "k_high", "k_low"))
    ret_s, ret_p, ret_pv, ret_o = (sem(n) for n in ("ret_s", "ret_p", "ret_pv", "ret_o"))
    mx_ready, mx_done, negm_ready, negm_turned, shift_ready, s_ready, exp_done, pv_done = (sem(n) for n in (
        "mx_ready", "mx_done", "negm_ready", "negm_turned", "shift_ready", "s_ready", "exp_done", "pv_done"))
    o_used, o_out, o_turned = sem("o_used"), sem("o_out"), sem("o_turned")
    conv_done, gelu_done, hid_ready, hid_hi_ready, hid_lo_ready = (sem(n) for n in (
        "conv_done", "gelu_done", "hid_ready", "hid_hi_ready", "hid_lo_ready"))
    gate_raw, gate_abs, gate_exp, gate_ln, scan_sum, scan_floor, floor_exp, a_ready, a_turned, a_col = (sem(n) for n in (
        "gate_raw", "gate_abs", "gate_exp", "gate_ln", "scan_sum", "scan_floor", "floor_exp", "a_ready", "a_turned",
        "a_col"))
    vb_ms, vb_inv, sgu_ready, sgu_read, qk_conv, qk_silu = (sem(n) for n in (
        "vb_ms", "vb_inv", "sgu_ready", "sgu_read", "qk_conv", "qk_silu"))
    row_wide, row_out, ml_s, ml_diag, ml_decay, ml_p, ml_pv, ml_read, ml_o = (sem(n) for n in (
        "row_wide", "row_out", "ml_s", "ml_diag", "ml_decay", "ml_p", "ml_pv", "ml_read", "ml_o"))
    ang_ready, trig_ready = sem("ang_ready"), sem("trig_ready")
    stored = sem("stored")

    units = []
    for t in range(4):
        for half in range(2):
            for s in range(3):
                r = slice(64 * half, 64 * half + 64)
                k = (kc_hi[r, :], kc_lo[r, :]) if s == 0 else (nk_hi[r, s - 1, :], nk_lo[r, s - 1, :])
                v = (lambda kt, half=half: vc[:, half, :]) if s == 0 else (
                    lambda kt, half=half, s=s: nv[:, kt, s - 1, half, :])
                units.append(dict(q=(nq_hi[r, t, :], nq_lo[r, t, :]), k=k, v=v, half=half, scale=0.125, at=at1, s=s, t=t,
                                  kind="cmp" if s == 0 else "causal", tiles=1 if s == 0 else NT, gate=s * 8 + half * 4 + t,
                                  pair=t, last=half == 1 and s == 2))
    NSA_UNITS = len(units)
    for u in range(HEADS):
        units.append(dict(q=(qf_hi[:, u % 2, :], qf_lo[:, u % 2, :]), k=(kf_hi[:, u % 2, :], kf_lo[:, u % 2, :]),
                          v=lambda kt, u=u: mla_v[:, kt, u, :], half=u % 2, scale=96 ** -0.5, at=at2, s=0, t=u // 2,
                          kind="all", tiles=NT, gate=None, pair=4 + u // 2, last=u % 2 == 1))
    for n, w in enumerate(units):
        w["n"], w["first"] = n, sum(q["tiles"] for q in units[:n])
        w["k_mix"] = w["t"] + (4 if w["gate"] is not None else 0)
    MIX_BEFORE = [4 + p if p < 4 else 16 + p - 4 for p in range(12)]
    FF1_O, FF2_O, FF0_O = output_of(FF1), output_of(FF2), output_of(FF0)

    norm_source = {"mix_pre": x, "mix_post": y, "ffn_pre": x, "ffn_post": y, "ab": x, "ffn1": x, "c": x, "ffn2": x,
                   "final": x, "cq": c_raw[:, 0:3, :], "ckv": c_raw[:, 3:5, :]}
    for h in range(4):
        norm_source[f"ret{h}"] = ret_out[:, h % 2:h % 2 + 1, :]
        norm_source[f"head{h}"] = part[:, 1:2, :]
    norm_gain = {"mix_pre": "g_mix_pre", "mix_post": "g_mix_post", "ffn_pre": "g_ffn_pre", "ffn_post": "g_ffn_post",
                 "ab": "g_ab", "ffn1": "g_ffn1", "c": "g_c", "ffn2": "g_ffn2", "final": "g_final", "cq": "g_cq",
                 "ckv": "g_ckv"}
    norm_split = {name: (h_hi, h_lo) for name in SPLIT_NORMS}
    norm_split["cq"] = (cq_hi[:, 0:3, :], cq_lo[:, 0:3, :])
    norm_split["ckv"] = (cq_hi[:, 3:5, :], cq_lo[:, 3:5, :])
    X_WRITES = {}

    def down_tile(pe, dense, panel, i, tiles, hidden, c):
        dense(panel, i, moving=(hid_hi, hid_lo), tiles=tiles,
              **({} if hidden is None else dict(ready=hid_lo_ready, base=plus(hidden, c, 8))))

    def down(pe, dense, panel, tiles, hidden):
        for k in range(KD):
            down_tile(pe, dense, panel + k, None, tiles, hidden if k == 0 else None, None)

    block = ctx.enter_context(nc.Block())

    @block.sync
    def _(sp):
        for n in range(4):
            sp.dma_start(raw[:, n, :], A["panels"][n]).then_inc(raw_in[n], 16)
        with sp.Fori(1, PANELS // 4) as i:
            for n in range(4):
                sp.wait_ge(w_lo_ready, i * 4 + (n - 3))
                sp.dma_start(raw[:, n, :], A["panels"][i * 4 + n]).then_inc(raw_in[n], 16)
        first_norm = NORM["final"][1]
        for k in range(KD):
            sp.wait_ge(normed, first_norm + k + 1)
            sp.dma_start(A["out"][k], y[:, k, :]).then_inc(stored, 16)
        sp.wait_ge(stored, 16 * KD)

    @block.gpsimd
    def _(pool):
        nc.gpsimd.memset(ones_r[:].bitcast(F32), 1.0).then_inc(pool_set, 1)
        nc.gpsimd.memset(nv[:], 1.0).then_inc(pool_set, 1)
        nc.gpsimd.memset(vc[:], 1.0).then_inc(pool_set, 1)
        nc.gpsimd.memset(cv_hi[:].bitcast(F32), 0.0).then_inc(pool_set, 1)
        nc.gpsimd.memset(cv_lo[:].bitcast(F32), 0.0).then_inc(pool_set, 1)
        nc.gpsimd.memset(kc_hi[:].bitcast(F32), 0.0).then_inc(pool_set, 1)
        nc.gpsimd.memset(kc_lo[:].bitcast(F32), 0.0).then_inc(pool_set, 1)
        pool.wait_ge(consts_in, 32)

        def inverse_root(name):
            n = NORM[name][0]
            pool.wait_ge(ms_ready, n + 1)
            nc.gpsimd.tensor_tensor(r4[:, 1, :], r4[:, 0, :], col("minus_half", 0, 4), ALU.pow).then_inc(inv_ready, 1)

        for name, *_ in NORM_LIST[:9]:
            inverse_root(name)
        for t in range(NT):
            pool.wait_ge(vb_ms, t + 1)
            nc.gpsimd.tensor_tensor(r4[:, 3, :], r4[:, 2, :], col("minus_half", 0, 4), ALU.pow).then_inc(vb_inv, 1)
        for name, *_ in NORM_LIST[9:15]:
            inverse_root(name)
        pool.wait_ge(normed, NORM["c"][1] + KD)
        nc.gpsimd.memset(mla_v[:, :, :, 64:65], 1.0).then_inc(pool_set, 1)
        nc.gpsimd.memset(q_turn[0:64, :], 1.0).then_inc(pool_set, 1)
        for name, *_ in NORM_LIST[15:]:
            inverse_root(name)

    @block.tensor
    def _(pe):
        def product(out, a, b, start, stop):
            nc.tensor.matmul(out, a[0], b[0], start=start, stop=False)
            nc.tensor.matmul(out, a[0], b[1], start=False, stop=False)
            return nc.tensor.matmul(out, a[1], b[0], start=False, stop=stop)

        def w(panel, a, b):
            return w_hi[:, panel % 2, a:b], w_lo[:, panel % 2, a:b]

        def dense(panel, i=None, moving=(h_hi, h_lo), tiles=KD, ready=None, base=0, most=None):
            o = output_of(panel)
            pe.wait_ge(w_lo_ready, plus(panel + 1, i, 4))
            if o >= 4:
                pe.wait_ge(tile_out, plus(o - 3, i, 4))
            for k in range(tiles):
                if ready is not None:
                    pe.wait_ge(ready, base + k + 1 if most is None else min(base + k + 1, most))
                last = product(ps[:, o % 4, :], w(panel, k * P, (k + 1) * P), (moving[0][:, k, :], moving[1][:, k, :]),
                               k == 0, k == tiles - 1)
            last.then_inc(panel_read, 1)

        def token_major(panel, width):
            o = output_of(panel)
            pe.wait_ge(tile_out, o)
            for c in range(4):
                pe.wait_ge(w_lo_ready, panel + c + 1)
                for kk in range(2):
                    for t in range(NT):
                        kt = 2 * c + kk
                        at = slice(t * P, (t + 1) * P)
                        last = product(ps[:, (o + t) % 4, 0:width], (h_hi[:, kt, at], h_lo[:, kt, at]),
                                       w(panel + c, kk * 512, kk * 512 + width), kt == 0, kt == KD - 1)
                last.then_inc(panel_read, 1)

        def norm(name):
            n, before, tiles, width, _ = NORM[name]
            pe.wait_ge(acc_ready, before + tiles)
            for t in range(NT):
                last = nc.tensor.matmul(ps[:, 6, t:t + 1], tmp[:, 2, t * P:(t + 1) * P], ones[:, 0:1], start=True, stop=True)
            last.then_inc(ss_ready, 1)
            pe.wait_ge(inv_diag, n + 1)
            if before:
                pe.wait_ge(normed, before)
            nc.tensor.matmul(ps[:, 7, :], ones, tmp[:, 3, :], start=True, stop=True).then_inc(inv_wide, 1)

        def maxima(u, tiles=range(NT)):
            n, (q, _), (k, _) = u["n"], u["q"], u["k"]
            if u["kind"] == "cmp":
                if n:
                    pe.wait_ge(mx_done, 4 * n)
                for t in range(NT):
                    out = ps[:, 2, t * 32:(t + 1) * 32]
                    nc.tensor.matmul(out, mask("ident"), mask("cmp_q_k")[:, t * 32:(t + 1) * 32], start=True, stop=False)
                    last = nc.tensor.matmul(out, q[:, t * P:(t + 1) * P], k[:, 0:32], start=False, stop=True)
                last.then_inc(mx_ready, 4)
                return
            for t in tiles:
                keys = (t + 1) * P if u["kind"] == "causal" else S
                out = ps[:, 2 + t % 2, :]
                if 4 * n + t >= 2:
                    pe.wait_ge(mx_done, 4 * n + t - 1)
                last = nc.tensor.matmul(out[:, 0:keys], q[:, t * P:(t + 1) * P], k[:, 0:keys], start=True,
                                        stop=u["kind"] != "causal")
                if u["kind"] == "causal":
                    last = nc.tensor.matmul(out[:, keys - P:keys], mask("ident"), mask("q_k"), start=False, stop=True)
                last.then_inc(mx_ready, 1)

        def turn(u):
            n = u["n"]
            pe.wait_ge(negm_ready, n + 1)
            if n:
                pe.wait_ge(shift_ready, n)
            if n >= 2:
                pe.wait_ge(o_used, n - 1)
            nc.tensor.matmul(ps[0:4, 7, 384:512], u["at"]["negm"][:, n % 2, :], ident, start=True,
                             stop=True).then_inc(negm_turned, 1)

        def scores(u, kt):
            n, m = u["n"], u["first"] + kt
            a = kt * P if u["kind"] == "causal" else 0
            out = ps[:, 4 + m % 2, :]
            pe.wait_ge(shift_ready, n + 1)
            if m >= 2:
                pe.wait_ge(exp_done, m - 1)
            nc.tensor.matmul(out[:, a:S], ones_r[:, :], u["at"]["shift"][:, n % 2, a:S], start=True, stop=False)
            if u["kind"] == "causal":
                nc.tensor.matmul(out[:, a:a + P], mask("ident"), mask("k_q"), start=False, stop=False)
            if u["kind"] == "cmp":
                nc.tensor.matmul(out[:, :], mask("ident"), mask("cmp_k_q"), start=False, stop=False)
            k = (u["k"][0][:, kt * P:(kt + 1) * P], u["k"][1][:, kt * P:(kt + 1) * P])
            product(out[:, a:S], k, (u["q"][0][:, a:S], u["q"][1][:, a:S]), False, True).then_inc(s_ready, 1)

        def values(u, kt):
            n, m = u["n"], u["first"] + kt
            a = kt * P if u["kind"] == "causal" else 0
            pe.wait_ge(exp_done, m + 1)
            if kt == 0 and n:
                pe.wait_ge(o_out, n)
            nc.tensor.matmul(ps[0:65, 6, a:S], u["v"](kt), u["at"]["pr"][:, m % 4, a:S], start=kt == 0,
                             stop=kt == u["tiles"] - 1).then_inc(pv_done, 1)

        def turn_result(u):
            n = u["n"]
            pe.wait_ge(o_out, n + 1)
            if n:
                pe.wait_ge(o_used, n)
            for t in range(NT):
                last = nc.tensor.transpose(ps[:, 7, t * 65:(t + 1) * 65], u["at"]["osb"][:, n % 2, t * P:(t + 1) * P],
                                           ident[0:65, 0:65])
            last.then_inc(o_turned, 1)

        def turn_pair(u):
            pe.wait_ge(o_used, u["n"] + 1)
            if u["k_mix"] % 8:
                pe.wait_ge(mix_ready, MIX_BEFORE[u["pair"]])
            for t in range(NT):
                last = nc.tensor.transpose(ps[:, 1, t * P:(t + 1) * P], u["at"]["by_token"][:, u["pair"] % 2, t, :], ident)
            last.then_inc(turned, 1)

        pe.wait_ge(consts_in, 32)
        pe.wait_ge(x_in, 16)
        norm("mix_pre")
        for panel in range(RET_Q, RET_V):
            dense(panel, ready=n_lo if panel == RET_Q else None)
        token_major(RET_V, 512)
        for panel in range(RET_G, NSA_V):
            dense(panel)
        token_major(NSA_V, 256)
        o = output_of(NSA_GATE)
        pe.wait_ge(w_lo_ready, NSA_GATE + 1)
        pe.wait_ge(tile_out, o - 3)
        for t in range(NT):
            for k in range(KD):
                at = slice(t * P, (t + 1) * P)
                last = product(ps[:, o % 4, t * 32:(t + 1) * 32], (h_hi[:, k, at], h_lo[:, k, at]),
                               w(NSA_GATE, k * 32, (k + 1) * 32), k == 0, k == KD - 1)
        last.then_inc(panel_read, 1)
        for kv in range(2):
            o = CMP_W1 + 2 * kv
            pe.wait_ge(tile_out, o - 2)
            pe.wait_ge(cmp_in_ready, kv + 1)
            for c in range(4):
                panel = CMP_W1 + 4 * kv + c
                pe.wait_ge(w_lo_ready, panel + 1)
                for kk in range(4):
                    for m in range(2):
                        kt = 4 * c + kk
                        last = product(ps[:, (o + m) % 4, 0:62], w(panel, kk * 256 + m * P, kk * 256 + (m + 1) * P),
                                       (xg_hi[:, kv, kt, :], xg_lo[:, kv, kt, :]), kt == 0, kt == 15)
                last.then_inc(panel_read, 1)
        pe.wait_ge(w_lo_ready, CMP_W2 + 1)
        pe.wait_ge(cmp_hid_ready, 4)
        o = CMP_W1 + 4
        pe.wait_ge(tile_out, o)
        for m in range(2):
            product(ps[:, o % 4, 0:62], w(CMP_W2, m * P, (m + 1) * P), (ch_hi[:, m, 0:62], ch_lo[:, m, 0:62]), m == 0, m == 1)
        for g in range(2):
            for m in range(2):
                last = product(ps[:, (o + 1 + g) % 4, 0:64], (cv_hi[:, m, g, :], cv_lo[:, m, g, :]),
                               w(CMP_W2, 256 + m * 64, 320 + m * 64), m == 0, m == 1)
        last.then_inc(panel_read, 1)

        pe.wait_ge(tile_out, CMP_W1 + 7)
        pe.wait_ge(ev_used, CMP_W1)
        for h in range(4):
            r = slice(64 * (h % 2), 64 * (h % 2) + 64)

            def ret_values(m, kt):
                pe.wait_ge(ret_p, m + 1)
                nc.tensor.matmul(ps[:, h % 2, kt * P:S], rv[:, kt, h * P:(h + 1) * P], at1["pr"][:, m % 4, kt * P:S],
                                 start=kt == 0, stop=kt == NT - 1).then_inc(ret_pv, 1)

            if h >= 2:
                pe.wait_ge(ret_o, h - 1)
            for kt in range(NT):
                m = 4 * h + kt
                if m >= 2:
                    pe.wait_ge(ret_p, m - 1)
                at = slice(kt * P, (kt + 1) * P)
                product(ps[:, 4 + m % 2, kt * P:S], (rk_hi[r, h // 2, at], rk_lo[r, h // 2, at]),
                        (rq_hi[r, h // 2, kt * P:S], rq_lo[r, h // 2, kt * P:S]), True, True).then_inc(ret_s, 1)
                if kt:
                    ret_values(m - 1, kt - 1)
            ret_values(4 * h + 3, 3)
            if h:
                norm(f"ret{h - 1}")
        norm("ret3")

        pe.wait_ge(pool_set, 7)
        pe.wait_ge(cmp_ready, 3)
        nsa = units[:NSA_UNITS]
        pe.wait_ge(mix_ready, 4)
        maxima(nsa[0])
        maxima(nsa[1])
        turn(nsa[0])
        for n, u in enumerate(nsa):
            ahead = nsa[n + 2] if n + 2 < NSA_UNITS else None
            apart = ahead is not None and ahead["kind"] != "cmp"
            scores(u, 0)
            if u["tiles"] > 1:
                scores(u, 1)
            if n:
                turn_result(nsa[n - 1])
            if ahead is not None:
                maxima(ahead, range(0, 1))
            values(u, 0)
            if apart:
                maxima(ahead, range(1, 2))
            if n + 1 < NSA_UNITS:
                turn(nsa[n + 1])
            if n and nsa[n - 1]["last"]:
                turn_pair(nsa[n - 1])
            if u["tiles"] > 1:
                scores(u, 2)
                values(u, 1)
            if apart:
                maxima(ahead, range(2, 3))
            if u["tiles"] > 1:
                scores(u, 3)
                values(u, 2)
            if apart:
                maxima(ahead, range(3, 4))
            if u["tiles"] > 1:
                values(u, 3)
        turn_result(nsa[-1])
        turn_pair(nsa[-1])

        def dense_run(panel, count, **first):
            for j in range(4):
                dense(panel + j, **(first if j == 0 else {}))
            if count > 4:
                with pe.Fori(1, count // 4) as i:
                    for j in range(4):
                        dense(panel + j, i)

        dense_run(OUT1, KD, ready=mix_ready, base=0)
        norm("mix_post")
        norm("ffn_pre")
        panel, hidden = FF0, 0
        for c, tiles in enumerate(FF0_CHUNKS):
            dense_run(panel, 2 * tiles, **(dict(ready=n_lo, base=SPLITS_BEFORE["ffn_pre"]) if c == 0 else {}))
            panel += 2 * tiles
            down(pe, dense, panel, tiles, hidden)
            panel += KD
            hidden += tiles
        norm("ffn_post")

        norm("ab")
        dense(AB_GATE, ready=n_lo, base=SPLITS_BEFORE["ab"])
        for panel in range(AB_QK, AB_V):
            dense(panel)
        for t in range(NT):
            if t == 0:
                pe.wait_ge(a_ready, 1)
            last = nc.tensor.matmul(ps[:, 6, t * 64:(t + 1) * 64], la[:, t * P:(t + 1) * P], ident[0:64, 0:64],
                                    start=True, stop=True)
        last.then_inc(a_turned, 1)
        token_major(AB_V, 512)
        for panel in range(AB_O, AB_VB):
            dense(panel)
        token_major(AB_VB, 512)
        for panel in range(AB_U, OUT2):
            dense(panel)

        pe.wait_ge(tile_out, output_of(OUT2))
        pe.wait_ge(ev_used, output_of(OUT2))
        for g in range(4):
            for t in range(NT):
                last = nc.tensor.matmul(ps[:, g, t * P:(t + 1) * P], vb[:, t, g * P:(g + 1) * P],
                                        table(second, SECOND, "ws_t")[:, g * P:(g + 1) * P], start=True, stop=True)
            last.then_inc(sgu_ready, 1)
        pe.wait_ge(sgu_read, 4)

        pe.wait_ge(floor_exp, 1)

        def row(n, h, d, src):
            if n:
                pe.wait_ge(row_out, n)
            nc.tensor.matmul(ps[:, 7, :], ident[0:64, 32 * d + h:32 * d + h + 1].to_broadcast([64, P]), src[:, :],
                             start=True, stop=True).then_inc(row_wide, 1)

        for h in range(4):
            if h:
                pe.wait_ge(normed, NORM[f"head{h - 1}"][1] + 1)
            for d in range(2):
                row(4 * h + 2 * d, h, d, neg_m)
                row(4 * h + 2 * d + 1, h, d, floor_m)
            if h:
                pe.wait_ge(ml_read, 2 * h)

            def ml_values(m, kt, d, order):
                pe.wait_ge(ml_p, 8 * h + m + 1)
                a, b = (kt * P, S) if d == 0 else (0, (kt + 1) * P)
                begins, ends = kt == (0 if d == 0 else 3), kt == 2
                wt = weights[:, m % 4, a:b]
                nc.tensor.matmul(ps[:, 2 * d, a:b], av[:, kt, h * P:(h + 1) * P], wt, start=begins, stop=ends)
                nc.tensor.matmul(ps[:, 2 * d + 1, a:b], ones, wt, start=begins, stop=ends).then_inc(ml_pv, 1)

            def ml_scores(n, kt):
                if 4 * h + n >= 2:
                    pe.wait_ge(ml_p, 8 * h + 2 * n - 2)
                at = slice(kt * P, (kt + 1) * P)
                product(ps[:, 4 + n % 2, :], (aq_hi[:, 4 + h, at], aq_lo[:, 4 + h, at]), (aq_hi[:, h, :], aq_lo[:, h, :]),
                        True, True).then_inc(ml_s, 1)

            ml_scores(0, 0)
            ml_scores(1, 3)
            ml_values(0, 0, 0, 0)
            ml_values(3, 3, 1, 1)
            ml_values(1, 0, 1, 2)
            ml_scores(2, 1)
            ml_values(2, 3, 0, 3)
            ml_scores(3, 2)
            ml_values(4, 1, 0, 4)
            ml_values(5, 1, 1, 5)
            ml_values(6, 2, 0, 6)
            ml_values(7, 2, 1, 7)
            norm(f"head{h}")

        pe.wait_ge(ml_read, 8)
        dense_run(OUT2, KD, ready=mix_ready, base=12, most=16)

        def feed_forward(panel, base, hidden, name):
            norm(name)
            dense_run(panel, 8, ready=n_lo, base=SPLITS_BEFORE[name])
            down(pe, dense, panel + 8, 8, hidden)
            with pe.Fori(0, FF_CHUNKS - 1) as c:
                with pe.Fori(0, 2) as j:
                    for n in range(4):
                        dense(panel + 16 + n, c * 4 + j)
                for k in range(4):
                    down_tile(pe, dense, panel + 24 + k, c * 4, 8, hidden + 8 if k == 0 else None, c)
                for k in range(4):
                    down_tile(pe, dense, panel + 28 + k, c * 4, 8, None, None)

        feed_forward(FF1, 0, sum(FF0_CHUNKS), "ffn1")

        norm("c")
        for panel in range(C_IN, MLA_V):
            dense(panel, **(dict(ready=n_lo, base=SPLITS_BEFORE["c"]) if panel == C_IN else {}))
        norm("ckv")
        norm("cq")
        pe.wait_ge(n_lo, SPLITS_BEFORE["ckv"] + 2)
        pe.wait_ge(w_lo_ready, MLA_V + 2)
        pe.wait_ge(tile_out, output_of(MLA_V))
        for j in range(8):
            t, half = j % 4, j // 4
            at = slice(t * P, (t + 1) * P)
            if j >= 4:
                pe.wait_ge(v_copied, j - 3)
            for k in range(2):
                last = product(ps[:, j % 4, :], (cq_hi[:, 3 + k, at], cq_lo[:, 3 + k, at]),
                               w(MLA_V + k, half * 512, half * 512 + 512), k == 0, k == 1)
            last.then_inc(*((v_ready, 1) if j < 7 else (panel_read, 2)))
        pe.wait_ge(v_copied, 8)
        pe.wait_ge(pool_set, 9)
        pe.wait_ge(n_lo, SPLITS_BEFORE["cq"] + 3)

        def project_q(n):
            pe.wait_ge(w_lo_ready, MLA + n + 1)
            if n:
                pe.wait_ge(k_low, n)
            for k in range(3):
                last = product(ps[:, 0, :], w(MLA + n, k * P, (k + 1) * P), (cq_hi[:, k, :], cq_lo[:, k, :]), k == 0, k == 2)
            last.then_inc(q_proj, 1)

        def project_k(n):
            pe.wait_ge(q_scaled, n + 1)
            for k in range(2):
                a = 384 + k * P
                last = product(ps[0:64, 0, :], w(MLA + n, a, a + 64), (cq_hi[:, 3 + k, :], cq_lo[:, 3 + k, :]), k == 0, k == 1)
            last.then_inc(panel_read, 1)

        mla = units[NSA_UNITS:]
        project_q(0)
        project_k(0)
        project_q(1)
        project_k(1)
        pe.wait_ge(k_low, 1)
        maxima(mla[0])
        turn(mla[0])
        for n, u in enumerate(mla):
            more = n + 1 < HEADS
            scores(u, 0)
            scores(u, 1)
            if n:
                turn_result(mla[n - 1])
            if more:
                pe.wait_ge(k_low, n + 2)
                maxima(mla[n + 1], range(0, 2))
            values(u, 0)
            scores(u, 2)
            if more:
                maxima(mla[n + 1], range(2, 4))
            values(u, 1)
            scores(u, 3)
            if n + 2 < HEADS:
                project_q(n + 2)
            values(u, 2)
            if more:
                turn(mla[n + 1])
            if n and mla[n - 1]["last"]:
                turn_pair(mla[n - 1])
            if n + 2 < HEADS:
                project_k(n + 2)
            values(u, 3)
        turn_result(mla[-1])
        turn_pair(mla[-1])

        dense_run(OUT3, KD, ready=mix_ready, base=16)
        feed_forward(FF2, 0, sum(FF0_CHUNKS) + 8 * FF_CHUNKS, "ffn2")
        norm("final")


    @block.scalar
    def _(act):
        def split(panel, i=None):
            act.wait_ge(raw_in[panel % 4], plus(16 * (panel // 4 + 1), i, 16))
            if panel >= 2:
                act.wait_ge(panel_read, plus(panel - 1, i, 4))
            nc.scalar.activation(w_hi[:, panel % 2, :], raw[:, panel % 4, :], ACT.Copy).then_inc(w_hi_ready, 1)

        def out(o, func, read, i=None, cols=S, bias=0.0, n=1):
            act.wait_ge(panel_read, plus(read, i, 4))
            if o >= 4:
                act.wait_ge(ev_used, plus(o - 3, i, 4))
            nc.scalar.activation(ev[:, o % 4, 0:cols], ps[:, o % 4, 0:cols], func, bias=bias).then_inc(tile_out, n)

        def step(panel, func=ACT.Copy, i=None, **more):
            act.wait_ge(panel_read, plus(panel + 1, i, 4))
            split(panel + 2, i)
            out(output_of(panel), func, panel + 1, i, **more)

        def token_major(panel, func, cols):
            for c in range(4):
                split(panel + c + 2)
            for t in range(NT):
                out(output_of(panel) + t, func, panel + 4, cols=cols)

        def step_run(panel, count, func=ACT.Copy):
            with act.Fori(0, count // 4) as i:
                for j in range(4):
                    step(panel + j, func, i)

        def squares(name, ready, value):
            _, before, tiles, _, _ = NORM[name]
            act.wait_ge(ready, value)
            for k in range(tiles):
                m = before + k
                if m >= 2:
                    act.wait_ge(acc_ready, m - 1)
                nc.scalar.activation(tmp[:, m % 2, :], norm_source[name][:, k, :], ACT.Square).then_inc(sq_ready, 1)

        def highs(name):
            _, before, tiles, _, _ = NORM[name]
            for k in range(tiles):
                act.wait_ge(normed, before + k + 1)
                nc.scalar.activation(norm_split[name][0][:, k, :], tmp[:, (before + k) % 2, :], ACT.Copy).then_inc(n_hi, 1)

        act.dma_start(small[:], A["small"]).then_inc(consts_in, 16)
        act.dma_start(masks[:], A["masks"]).then_inc(consts_in, 16)
        act.dma_start(x[:], A["x"].rearrange("k p s -> p k s")).then_inc(x_in, 16)
        act.dma_start(first[:], A["first"]).then_inc(first_in, 16)

        split(0)
        split(1)
        squares("mix_pre", x_in, 16)
        highs("mix_pre")
        for panel in range(RET_Q, RET_V):
            step(panel)
        token_major(RET_V, ACT.Copy, S)
        for panel in range(RET_G, CMP_IN):
            step(panel, ACT.Silu)
        for panel in range(CMP_IN, NSA_V):
            step(panel)
        token_major(NSA_V, ACT.Copy, 256)
        step(NSA_GATE, ACT.Sigmoid, cols=P)
        for kv in range(2):
            panel, o = CMP_W1 + 4 * kv, CMP_W1 + 2 * kv
            for c in range(4):
                split(panel + c + 2)
            for m in range(2):
                out(o + m, ACT.Gelu_apprx_tanh, panel + 4, cols=62)
        split(CMP_W2 + 2)
        out(CMP_W1 + 4, ACT.Copy, CMP_W2 + 1, cols=62)
        out(CMP_W1 + 5, ACT.Copy, CMP_W2 + 1, cols=64)
        out(CMP_W1 + 6, ACT.Copy, CMP_W2 + 1, cols=64)

        for h in range(4):
            act.wait_ge(ret_pv, 4 * (h + 1))
            if h >= 2:
                act.wait_ge(normed, NORM[f"ret{h - 2}"][1] + 1)
            nc.scalar.activation(ret_out[:, h % 2, :], ps[:, h % 2, :], ACT.Copy).then_inc(ret_o, 1)
            squares(f"ret{h}", ret_o, h + 1)

        def weights_of(u, kt):
            m = u["first"] + kt
            a = kt * P if u["kind"] == "causal" else 0
            act.wait_ge(s_ready, m + 1)
            if m >= 4:
                act.wait_ge(pv_done, m - 3)
            nc.scalar.activation(u["at"]["pr"][:, m % 4, a:S], ps[:, 4 + m % 2, a:S], ACT.Exp,
                                 scale=u["scale"]).then_inc(exp_done, 1)

        def result_of(u):
            n = u["n"]
            act.wait_ge(pv_done, u["first"] + u["tiles"])
            if n >= 2:
                act.wait_ge(o_turned, n - 1)
            nc.scalar.activation(u["at"]["osb"][:, n % 2, :], ps[0:65, 6, :], ACT.Copy).then_inc(o_out, 1)

        def pair_high(u):
            act.wait_ge(turned, u["pair"] + 1)
            nc.scalar.activation(h_hi[:, u["k_mix"], :], ps[:, 1, :], ACT.Copy).then_inc(turned_high, 1)

        act.wait_ge(normed, NORM["ret3"][1] + 1)
        nsa = units[:NSA_UNITS]
        for n, u in enumerate(nsa):
            for kt in range(u["tiles"]):
                weights_of(u, kt)
                if kt == 0 and n:
                    result_of(nsa[n - 1])
                if kt == 0 and n and nsa[n - 1]["last"]:
                    pair_high(nsa[n - 1])
        result_of(nsa[-1])
        pair_high(nsa[-1])

        step_run(OUT1, KD)
        squares("mix_post", ev_used, FF0_O)
        squares("ffn_pre", x_ready, KD)
        highs("ffn_pre")

        def hidden_high(k, slot, ready, value):
            act.wait_ge(ready, value)
            nc.scalar.activation(hid_hi[:, k, :], hid_f[:, slot, :], ACT.Copy).then_inc(hid_hi_ready, 1)

        panel, hidden = FF0, 0
        for tiles in FF0_CHUNKS:
            def pair(j, i=None, skip=False):
                a = panel + 2 * j
                step(a, i=i)
                step(a + 1, i=i)
                act.wait_ge(ev_used, plus(output_of(a) + 1, i, 4))
                if hidden + j or i is not None:
                    act.wait_ge(hid_ready, plus(hidden + j, i, 2))
                nc.scalar.activation(act_t[:], conv_t[:, 0, :], ACT.Gelu_apprx_tanh).then_inc(gelu_done, 1)
                if not skip:
                    hidden_high(plus(j - 1, i, 2), (j - 1) % 2, hid_ready, plus(hidden + j, i, 2))

            pair(0, skip=True)
            pair(1)
            with act.Fori(1, tiles // 2) as i:
                pair(0, i)
                pair(1, i)
            hidden_high(tiles - 1, 1, hid_ready, hidden + tiles)
            step_run(panel + 2 * tiles, KD)
            panel += 2 * tiles + KD
            hidden += tiles
        squares("ffn_post", ev_used, output_of(AB_GATE))
        squares("ab", x_ready, 2 * KD)
        highs("ab")

        act.wait_ge(ev_used, output_of(AB_GATE))
        act.dma_start(second[:], A["second"]).then_inc(second_in, 16)
        step(AB_GATE)
        act.wait_ge(gate_raw, 2)
        nc.scalar.activation(gt[64:P, 1, :], gt[64:P, 0, :], ACT.Abs).then_inc(gate_abs, 1)
        act.wait_ge(gate_abs, 1)
        nc.scalar.activation(gt[64:P, 2, :], gt[64:P, 1, :], ACT.Exp, scale=-1.0).then_inc(gate_exp, 1)
        act.wait_ge(gate_exp, 1)
        nc.scalar.activation(gt[64:P, 1, :], gt[64:P, 2, :], ACT.Ln, bias=1.0).then_inc(gate_ln, 1)
        for n in range(8):
            step(AB_QK + n)
            act.wait_ge(qk_conv, n + 1)
            nc.scalar.activation(qk_f[:, 1, :], qk_f[:, 0, :], ACT.Silu).then_inc(qk_silu, 1)
        token_major(AB_V, ACT.Copy, S)
        for panel in range(AB_O, AB_VB):
            step(panel, ACT.Sigmoid)
        token_major(AB_VB, ACT.Gelu_apprx_tanh, S)
        for panel in range(AB_U, OUT2):
            step(panel, ACT.Gelu_apprx_tanh)

        act.wait_ge(scan_floor, 1)
        nc.scalar.activation(floor_m[:, :], floor_m[:, :], ACT.Exp, scale=-1.0).then_inc(floor_exp, 1)
        act.wait_ge(sgu_read, 4)
        for h in range(4):
            if h:
                act.wait_ge(ml_read, 2 * h)
            for n in range(4):
                act.wait_ge(row_wide, 4 * h + n + 1)
                nc.scalar.activation(rows[:, n, :], ps[:, 7, :], ACT.Copy).then_inc(row_out, 1)
            for n, kt in enumerate((0, 3, 1, 2)):
                for d in range(2):
                    m = 8 * h + 2 * n + d
                    at = slice(kt * P, (kt + 1) * P)
                    rest = slice((kt + 1) * P, S) if d == 0 else slice(0, kt * P)
                    bias = a_t[:, kt, 32 * d + h:32 * d + h + 1]
                    act.wait_ge(ml_diag, m + 1)
                    if m >= 2:
                        act.wait_ge(ml_p, m - 1)
                    last = nc.scalar.activation(decays[:, m % 2, at], diag[:, m % 2, :], ACT.Exp, bias=bias)
                    if rest.start < rest.stop:
                        last = nc.scalar.activation(decays[:, m % 2, rest], rows[:, 2 * d, rest], ACT.Exp, bias=bias)
                    last.then_inc(ml_decay, 1)
            squares(f"head{h}", ml_o, h + 1)

        def feed_forward(panel, name):
            squares(name, ev_used, output_of(panel))
            highs(name)

            def chunk(c):
                o = output_of(panel)

                def tile(k, i, skip=False):
                    step(panel + k, ACT.Relu, i)
                    if not skip:
                        hidden_high(k - 1, (k - 1) % 2, ev_used, plus(o + k, i, 4))

                i = None if c is None else c * 4
                for k in range(8):
                    tile(k, i, k == 0)
                hidden_high(7, 1, ev_used, plus(o + 8, i, 4))
                for k in range(8):
                    step(panel + 8 + k, ACT.Copy, i)

            with act.Fori(0, FF_CHUNKS) as c:
                chunk(c)

        step_run(OUT2, KD)
        feed_forward(FF1, "ffn1")

        squares("c", ev_used, output_of(C_IN))
        act.dma_start(pos_i[64:P, :], A["positions"]).then_inc(pos_in, 16)
        highs("c")
        for panel in range(C_IN, MLA_V):
            step(panel)
        for d in range(2):
            act.wait_ge(ang_ready, d + 1)
            nc.scalar.activation(trig[64:P, d, :], ang[64:P, 1 + d, :], ACT.Sin).then_inc(trig_ready, 1)
        squares("ckv", ev_used, output_of(MLA_V))
        highs("ckv")
        squares("cq", n_lo, SPLITS_BEFORE["cq"])
        highs("cq")
        for j in range(8):
            t, half = j % 4, j // 4
            act.wait_ge(*((v_ready, j + 1) if j < 7 else (panel_read, MLA)))
            nc.scalar.activation(mla_v[:, t, 8 * half:8 * half + 8, 0:64], ps[:, j % 4, :].rearrange("p (h d) -> p h d", h=8),
                                 ACT.Copy).then_inc(v_copied, 1)

        def q_of(n):
            act.wait_ge(q_scaled, n + 1)
            nc.scalar.activation(qf_hi[:, n % 2, :], q_f[:, :], ACT.Copy).then_inc(q_high, 1)

        def k_of(n):
            act.wait_ge(panel_read, MLA + n + 1)
            nc.scalar.activation(kf_hi[0:64, n % 2, :], ps[0:64, 0, :], ACT.Copy).then_inc(k_high, 1)
            split(MLA + n + 2)

        mla = units[NSA_UNITS:]
        split(MLA)
        split(MLA + 1)
        for n in range(2):
            q_of(n)
            k_of(n)
        for n, u in enumerate(mla):
            for kt in range(4):
                weights_of(u, kt)
                if kt == 0 and n:
                    result_of(mla[n - 1])
            if n + 2 < HEADS:
                q_of(n + 2)
            if n and mla[n - 1]["last"]:
                pair_high(mla[n - 1])
            if n + 2 < HEADS:
                k_of(n + 2)
        result_of(mla[-1])
        pair_high(mla[-1])

        step_run(OUT3, KD)
        feed_forward(FF2, "ffn2")
        squares("final", ev_used, output_of(PANELS_USED))

    @block.vector
    def _(dve):
        V = nc.vector
        so_far, loop = {}, {"i": None, "each": {}}

        def signal(ins, s, n=1, wait=True):
            so_far[s] = so_far.get(s, 0) + n
            ins.then_inc(s, n)
            if wait:
                dve.wait_ge(s, plus(so_far[s], loop["i"], loop["each"].get(s, 0)))

        def link(ins):
            signal(ins, dve_step)

        def enter(i, each, first=0):
            for s, k in each.items():
                so_far[s] = so_far.get(s, 0) - k * first
            loop["i"], loop["each"], loop["start"], loop["first"] = i, each, dict(so_far), first

        def leave(turns):
            for s, k in loop["each"].items():
                assert so_far.get(s, 0) - loop["start"].get(s, 0) == k, s
                so_far[s] += k * (turns - 1 + loop["first"])
            loop["i"], loop["each"] = None, {}

        def low(panel, i=None):
            dve.wait_ge(w_hi_ready, plus(panel + 1, i, 4))
            signal(V.tensor_tensor(w_lo[:, panel % 2, :], raw[:, panel % 4, :], w_hi[:, panel % 2, :].bitcast(F32),
                            ALU.subtract), w_lo_ready, wait=False)

        def take(panel, i=None, extra=0):
            low(panel + 2, i)
            o = output_of(panel)
            dve.wait_ge(tile_out, plus(o + 1, i, 4))
            return ev[:, o % 4, :]

        def take_four(panel):
            for c in range(4):
                low(panel + c + 2)
            for t in range(NT):
                dve.wait_ge(tile_out, output_of(panel) + t + 1)
                yield t, ev[:, (output_of(panel) + t) % 4, :]

        def used(ins):
            signal(ins, ev_used)

        def parts(hi, lo, src):
            link(V.tensor_copy(hi, src))
            return V.tensor_tensor(lo, src, hi.bitcast(F32), ALU.subtract)

        def wide(t4, n=P):
            return t4.unsqueeze(2).to_broadcast([t4.shape[0], 4, n])

        def fours(t):
            return t.rearrange("p (a b) -> p a b", a=4)

        def rope(src, dst, c, s, swapped):
            link(V.stream_shuffle(swapped, src, HALF_SWAP))
            link(V.tensor_tensor(swapped, swapped, s, ALU.mult))
            link(V.tensor_tensor(dst, src, c, ALU.mult))
            link(V.tensor_tensor(dst, dst, swapped, ALU.add))

        def inverse(name):
            n, before, tiles, width, eps = NORM[name]
            for k in range(tiles):
                m = before + k
                dve.wait_ge(sq_ready, m + 1)
                if k == 0:
                    signal(V.tensor_copy(tmp[:, 2, :], tmp[:, m % 2, :]), acc_ready)
                else:
                    dve.wait_ge(acc_ready, m)
                    signal(V.tensor_tensor(tmp[:, 2, :], tmp[:, 2, :], tmp[:, m % 2, :], ALU.add), acc_ready)
            dve.wait_ge(ss_ready, n + 1)
            signal(V.tensor_scalar(r4[:, 0, :], ps[:, 6, 0:4], 1.0 / width, eps, ALU.mult, ALU.add), ms_ready)
            dve.wait_ge(inv_ready, n + 1)
            signal(V.tensor_tensor(fours(tmp[:, 3, :]), ident.unsqueeze(1).to_broadcast([P, 4, P]), wide(r4[:, 1, :]),
                            ALU.mult), inv_diag)
            dve.wait_ge(inv_wide, n + 1)

        def scaled(name, k, gain, out=None):
            m = NORM[name][1] + k
            out = tmp[:, m % 2, :] if out is None else out
            signal(V.scalar_tensor_tensor(out, norm_source[name][:, k, :], gain, ps[:, 7, :], ALU.mult, ALU.mult), normed)

        def norm_split_of(name):
            _, before, tiles, _, _ = NORM[name]
            inverse(name)
            hi, lo = norm_split[name]
            at = SPLITS_BEFORE[name]

            def lower(k):
                dve.wait_ge(n_hi, at + k + 1)
                signal(V.tensor_tensor(lo[:, k, :], tmp[:, (before + k) % 2, :], hi[:, k, :].bitcast(F32), ALU.subtract), n_lo)

            for k in range(tiles):
                scaled(name, k, col(norm_gain[name], k))
                if k:
                    dve.wait_ge(normed, before + k)
                    lower(k - 1)
            dve.wait_ge(normed, before + tiles)
            lower(tiles - 1)

        def norm_add(name):
            inverse(name)
            _, before, tiles, _, _ = NORM[name]
            for k in range(tiles):
                scaled(name, k, col(norm_gain[name], k))
                dve.wait_ge(normed, before + k + 1)
                signal(V.tensor_tensor(x[:, k, :], x[:, k, :], tmp[:, (before + k) % 2, :], ALU.add), x_ready)

        def norm_head(name, gain, gate, k):
            inverse(name)
            before = NORM[name][1]
            t = tmp[:, before % 2, :]
            scaled(name, 0, gain)
            dve.wait_ge(normed, before + 1)
            link(V.tensor_tensor(t, t, gate, ALU.mult))
            signal(parts(h_hi[:, k, :], h_lo[:, k, :], t), mix_ready)

        def take_run(panel, n, each):
            with dve.Fori(0, n // 4) as i:
                enter(i, {ev_used: 4, w_lo_ready: 4})
                for j in range(4):
                    each(j, i, take(panel + j, i))
                leave(n // 4)

        dve.wait_ge(consts_in, 32)
        low(0)
        low(1)
        dve.wait_ge(x_in, 16)
        norm_split_of("mix_pre")
        dve.wait_ge(first_in, 16)
        c64, s64 = table(first, FIRST, "rope_c"), table(first, FIRST, "rope_s")

        def rope_parts(src, hi, lo):
            rope(src, tmp[:, 2, :], c64, s64, tmp[:, 3, :])
            used(parts(hi, lo, tmp[:, 2, :]))

        for panel in range(RET_Q, RET_V):
            t = panel % 2
            hi, lo = (rq_hi, rq_lo) if panel < RET_K else (rk_hi, rk_lo)
            rope_parts(take(panel), hi[:, t, :], lo[:, t, :])
        for t, src in take_four(RET_V):
            link(V.tensor_reduce(r4[:, 4, :], fours(src), AX.X, ALU.add))
            link(V.tensor_scalar(r4[:, 5, :], r4[:, 4, :], -1.0 / P, None, ALU.mult))
            used(V.tensor_tensor(fours(rv[:, t, :]), fours(src), wide(r4[:, 5, :]), ALU.add))
        for t in range(4):
            used(V.tensor_copy(rg[:, t, :], take(RET_G + t)))
        for kv in range(2):
            src = take(CMP_IN + kv)
            if kv:
                dve.wait_ge(cmp_in_ready, 1)
            for g in range(2):
                for odd in range(2):
                    r = slice(64 * odd, 64 * odd + 64)
                    by_block = src[64 * g:64 * g + 64, :].rearrange("p (n i two) -> p i n two", i=8, two=2)
                    for later in range(2):
                        out = xg_f[r, 8 * later:8 * later + 8, 31 * g:31 * g + 31]
                        pos = small[64 * g:64 * g + 64, SMALL["cmp_pos"][0]:SMALL["cmp_pos"][0] + 64]
                        pos = pos.rearrange("p (kv two i) -> p kv two i", kv=2, two=2)[:, kv, odd, 8 * later:8 * later + 8]
                        last = V.tensor_tensor(out, by_block[:, :, later:later + 31, odd],
                                               pos.unsqueeze(2).to_broadcast([64, 8, 31]), ALU.add)
            used(last)
            dve.wait_ge(ev_used, output_of(CMP_IN + kv) + 1)
            signal(parts(xg_hi[:, kv, :, :], xg_lo[:, kv, :, :], xg_f[:, :, :]), cmp_in_ready)
        for t in range(4):
            rope_parts(take(NSA_Q + t), nq_hi[:, t, :], nq_lo[:, t, :])
        for t in range(2):
            rope_parts(take(NSA_K + t), nk_hi[:, t, :], nk_lo[:, t, :])
        dve.wait_ge(pool_set, 7)
        for t, src in take_four(NSA_V):
            by = src[:, 0:256].rearrange("p (s g d) -> p s g d", s=2, g=2)
            used(V.tensor_copy(nv[:, t, :, :, 0:64], by))
        used(V.tensor_copy(gates[:, :, :], fours(take(NSA_GATE)[:, 0:P])))
        for kv in range(2):
            panel, o = CMP_W1 + 4 * kv, CMP_W1 + 2 * kv
            for c in range(4):
                low(panel + c + 2)
            for m in range(2):
                dve.wait_ge(tile_out, o + m + 1)
                src = ev[:, (o + m) % 4, :]
                if kv == 0:
                    link(V.tensor_copy(ch_hi[:, m, 0:62], src[:, 0:62]))
                    last = V.tensor_tensor(ch_lo[:, m, 0:62], src[:, 0:62], ch_hi[:, m, 0:62].bitcast(F32), ALU.subtract)
                else:
                    by = src[:, 0:62].rearrange("p (g n) -> p g n", g=2)
                    link(V.tensor_copy(cv_hi[:, m, :, 0:31], by))
                    last = V.tensor_tensor(cv_lo[:, m, :, 0:31], by, cv_hi[:, m, :, 0:31].bitcast(F32), ALU.subtract)
                used(last)
                dve.wait_ge(ev_used, o + m + 1)
                signal(V.memset(r4[:, 2, 0:1], 0.0), cmp_hid_ready)
        low(CMP_W2 + 2)
        dve.wait_ge(tile_out, CMP_W1 + 5)
        src = ev[:, (CMP_W1 + 4) % 4, :]
        V.tensor_copy(kc_f[0:64, 0, 0:31], src[0:64, 0:31])
        used(V.tensor_copy(kc_f[64:P, 0, 0:31], src[64:P, 31:62]))
        dve.wait_ge(ev_used, CMP_W1 + 5)
        rope(kc_f[:, 0, 0:31], kc_f[:, 1, 0:31], table(first, FIRST, "cmp_c")[:, 0:31],
             table(first, FIRST, "cmp_s")[:, 0:31], kc_f[:, 2, 0:31])
        signal(parts(kc_hi[:, 0:31], kc_lo[:, 0:31], kc_f[:, 1, 0:31]), cmp_ready)
        for g in range(2):
            dve.wait_ge(tile_out, CMP_W1 + 6 + g)
            used(V.tensor_copy(vc[:, g, 0:64], ev[:, (CMP_W1 + 5 + g) % 4, 0:64]))
            dve.wait_ge(ev_used, CMP_W1 + 6 + g)
            signal(V.memset(r4[:, 2, 0:1], 0.0), cmp_ready)

        decay = table(first, FIRST, "decay")
        for h in range(4):
            for kt in range(NT):
                m = 4 * h + kt
                dve.wait_ge(ret_s, m + 1)
                if m >= 4:
                    dve.wait_ge(ret_pv, m - 3)
                signal(V.tensor_tensor(at1["pr"][:, m % 4, kt * P:S], ps[:, 4 + m % 2, kt * P:S],
                                decay[:, 512 * h:512 * h + S - kt * P], ALU.mult), ret_p)
            if h:
                norm_head(f"ret{h - 1}", col("gn", h - 1), rg[:, h - 1, :], h - 1)
        norm_head("ret3", col("gn", 3), rg[:, 3, :], 3)

        def largest(u, tiles=range(NT)):
            n, at = u["n"], u["at"]
            if u["kind"] == "cmp":
                if tiles.start == 0:
                    dve.wait_ge(mx_ready, 4 * n + 4)
                    signal(V.tensor_reduce(at["mx"][:, n % 2, :], ps[:, 2, 0:P].rearrange("p (a b) -> p a b", a=4), AX.X,
                                           ALU.max), mx_done, 4, wait=False)
            else:
                for t in tiles:
                    keys = (t + 1) * P if u["kind"] == "causal" else S
                    dve.wait_ge(mx_ready, 4 * n + t + 1)
                    signal(V.tensor_reduce(at["mx"][:, n % 2, t:t + 1], ps[:, 2 + t % 2, 0:keys], AX.X, ALU.max), mx_done,
                           wait=False)
            if tiles.stop < NT:
                return
            dve.wait_ge(mx_done, 4 * n + 4)
            signal(V.tensor_scalar(at["negm"][:, n % 2, :], at["mx"][:, n % 2, :], -1e20, -1.0, ALU.max, ALU.mult), negm_ready,
                   wait=False)

        def shift_of(u):
            n = u["n"]
            dve.wait_ge(negm_turned, n + 1)
            signal(V.tensor_tensor(fours(u["at"]["shift"][:, n % 2, :]),
                                   ps[0:4, 7, 384:512].unsqueeze(1).to_broadcast([4, 4, P]),
                                   ident[0:4, 0:4].unsqueeze(2).to_broadcast([4, 4, P]), ALU.mult), shift_ready, wait=False)

        def result(u):
            n, at = u["n"], u["at"]
            dve.wait_ge(o_turned, n + 1)
            if u["pair"] % 4 >= 2 and u["half"] == 0 and u["s"] == 0:
                dve.wait_ge(turned, u["pair"] - 1)
            by = ps[:, 7, 0:NT * 65].rearrange("p (t d) -> p t d", t=NT)
            w4 = at["w4"][:].unsqueeze(2)
            if u["gate"] is None:
                link(V.reciprocal(w4, by[:, :, 64:65]))
            else:
                link(V.tensor_scalar(w4, by[:, :, 64:65], 1e-30, None, ALU.max))
                link(V.reciprocal(at["w4"][:], at["w4"][:]))
                link(V.tensor_tensor(at["w4"][:], at["w4"][:], gates[:, :, u["gate"]], ALU.mult))
            total = at["by_token"][:, u["pair"] % 2, :, 64 * u["half"]:64 * u["half"] + 64]
            if u["s"] == 0:
                signal(V.tensor_tensor(total, by[:, :, 0:64], wide(at["w4"][:], 64), ALU.mult), o_used)
            else:
                link(V.tensor_tensor(at["term"][:], by[:, :, 0:64], wide(at["w4"][:], 64), ALU.mult))
                signal(V.tensor_tensor(total, total, at["term"][:], ALU.add), o_used)

        def pair_low(u):
            dve.wait_ge(turned_high, u["pair"] + 1)
            k = u["k_mix"]
            signal(V.tensor_tensor(h_lo[:, k, :], ps[:, 1, :], h_hi[:, k, :].bitcast(F32), ALU.subtract), mix_ready, wait=False)

        nsa = units[:NSA_UNITS]
        largest(nsa[0])
        largest(nsa[1])
        shift_of(nsa[0])
        for n, u in enumerate(nsa):
            if n:
                result(nsa[n - 1])
            if n + 2 < NSA_UNITS:
                largest(nsa[n + 2], range(0, 2))
            if n + 1 < NSA_UNITS:
                shift_of(nsa[n + 1])
            if n and nsa[n - 1]["last"]:
                pair_low(nsa[n - 1])
            if n + 2 < NSA_UNITS:
                largest(nsa[n + 2], range(2, 4))
        result(nsa[-1])
        pair_low(nsa[-1])

        take_run(OUT1, KD, lambda j, i, src: used(V.tensor_copy(y[:, plus(j, i, 4), :], src)))
        dve.wait_ge(ev_used, FF0_O)
        norm_add("mix_post")
        dve.wait_ge(x_ready, KD)
        norm_split_of("ffn_pre")
        conv0 = SMALL["conv0"][0]

        def hidden_low(k, slot, value):
            dve.wait_ge(hid_hi_ready, value)
            signal(V.tensor_tensor(hid_lo[:, k, :], hid_f[:, slot, :], hid_hi[:, k, :].bitcast(F32), ALU.subtract), hid_lo_ready)

        panel, hidden = FF0, 0
        for c, tiles in enumerate(FF0_CHUNKS):
            def pair(j, i=None, skip=False):
                q = hidden + j
                for side in range(2):
                    src = take(panel + 2 * j + side, i)
                    t = conv_t[:, side, :]

                    def tap(n):
                        at = plus(conv0 + (2 * q + side) * 3 + n, i, 12)
                        return small[:, at:at + 1] if i is None else small[:, bass.ds(at, 1)]

                    link(V.tensor_scalar(t, src, tap(2), None, ALU.mult))
                    link(V.scalar_tensor_tensor(t[:, 1:S], src[:, 0:S - 1], tap(1), t[:, 1:S], ALU.mult, ALU.add))
                    used(V.scalar_tensor_tensor(t[:, 2:S], src[:, 0:S - 2], tap(0), t[:, 2:S], ALU.mult, ALU.add))
                    dve.wait_ge(ev_used, plus(output_of(panel) + 2 * j + side + 1, i, 4))
                dve.wait_ge(gelu_done, plus(q + 1, i, 2))
                signal(V.tensor_tensor(hid_f[:, j % 2, :], act_t[:], conv_t[:, 1, :], ALU.mult), hid_ready)
                if not skip:
                    hidden_low(plus(j - 1, i, 2), (j - 1) % 2, plus(q, i, 2))

            pair(0, skip=True)
            pair(1)
            with dve.Fori(1, tiles // 2) as i:
                enter(i, {ev_used: 4, w_lo_ready: 4, dve_step: 4 * 2, hid_ready: 2, hid_lo_ready: 2}, first=1)
                pair(0, i)
                pair(1, i)
                leave(tiles // 2 - 1)
            hidden_low(tiles - 1, 1, hidden + tiles)
            down_panel = panel + 2 * tiles

            def gather(j, i, src):
                k = plus(j, i, 4)
                if c == 0:
                    used(V.tensor_copy(y[:, k, :], src))
                else:
                    used(V.tensor_tensor(y[:, k, :], y[:, k, :], src, ALU.add))

            take_run(down_panel, KD, gather)
            panel += 2 * tiles + KD
            hidden += tiles
        dve.wait_ge(ev_used, output_of(AB_GATE))
        norm_add("ffn_post")
        dve.wait_ge(x_ready, 2 * KD)
        norm_split_of("ab")

        src = take(AB_GATE)
        signal(V.tensor_scalar(gt[:, 0, :], src, col("gate_b"), None, ALU.add), gate_raw)
        dve.wait_ge(gate_raw, 1)
        used(V.tensor_scalar(li[:, :], src[0:64, :], col("gate_b")[0:64, :], None, ALU.add))
        dve.wait_ge(ev_used, output_of(AB_GATE) + 1)
        signal(V.memset(r4[:, 2, 0:1], 0.0), gate_raw)
        link(V.memset(scan[:, :, :], 0.0))
        dve.wait_ge(gate_ln, 1)
        mid = slice(256, 768)
        link(V.scalar_tensor_tensor(scan[:, 0, mid], gt[64:P, 0, :], 0.0, gt[64:P, 1, :], ALU.min, ALU.subtract))

        def scan_all(op):
            for n in range(9):
                a, b = n % 2, 1 - n % 2
                V.tensor_tensor(scan[0:32, b, mid], scan[0:32, a, mid], scan[0:32, a, 256 - 2 ** n:768 - 2 ** n], op)
                link(V.tensor_tensor(scan[32:64, b, mid], scan[32:64, a, mid], scan[32:64, a, 256 + 2 ** n:768 + 2 ** n], op))

        scan_all(ALU.add)
        link(V.tensor_copy(neg_m[:, :], scan[:, 1, mid]))
        signal(V.tensor_tensor(la[:, :], li[:, :], neg_m[:, :], ALU.subtract), a_ready)
        dve.wait_ge(a_ready, 1)
        link(V.memset(scan[:, :, :], NEG))
        link(V.tensor_copy(scan[:, 0, mid], la[:, :]))
        scan_all(ALU.max)
        link(V.tensor_scalar(scan[:, 0, mid], scan[:, 1, mid], 0.0, None, ALU.max))
        link(V.tensor_tensor(floor_m[:, :], neg_m[:, :], scan[:, 0, mid], ALU.add))
        signal(V.tensor_scalar(neg_m[:, :], scan[:, 0, mid], -1.0, None, ALU.mult), scan_floor)

        conv1 = SMALL["conv1"][0]
        for n in range(8):
            src = take(AB_QK + n)
            t = qk_f[:, 0, :]

            def tap(k):
                return small[:, conv1 + 5 * n + k:conv1 + 5 * n + k + 1]

            def add_tap(k, a, b):
                return V.scalar_tensor_tensor(t[:, a:b], src[:, a + k - 2:b + k - 2], tap(k), t[:, a:b], ALU.mult, ALU.add)

            link(V.tensor_scalar(t, src, tap(2), None, ALU.mult))
            link(add_tap(1, 1, S))
            link(add_tap(0, 2, S))
            link(add_tap(3, 0, S - 1))
            used(add_tap(4, 0, S - 2))
            dve.wait_ge(ev_used, output_of(AB_QK) + n + 1)
            signal(V.memset(r4[:, 2, 0:1], 0.0), qk_conv)
            dve.wait_ge(qk_silu, n + 1)
            link(parts(aq_hi[:, n, :], aq_lo[:, n, :], qk_f[:, 1, :]))
        dve.wait_ge(a_turned, 1)
        signal(V.tensor_copy(a_t[:, :, :], ps[:, 6, 0:256].rearrange("p (a b) -> p a b", a=4)), a_col)
        for t, src in take_four(AB_V):
            used(V.tensor_copy(av[:, t, :], src))
        for t in range(4):
            used(V.tensor_copy(ao[:, t, :], take(AB_O + t)))
        dve.wait_ge(second_in, 16)
        for t, src in take_four(AB_VB):
            link(V.tensor_tensor(tmp[:, 2, :], src, src, ALU.mult))
            link(V.tensor_reduce(r4[:, 4, :], fours(tmp[:, 2, :]), AX.X, ALU.add))
            signal(V.tensor_scalar(r4[:, 2, :], r4[:, 4, :], 1.0 / P, 1e-6, ALU.mult, ALU.add), vb_ms)
            dve.wait_ge(vb_inv, t + 1)
            link(V.tensor_tensor(fours(tmp[:, 3, :]), fours(src), wide(r4[:, 3, :]), ALU.mult))
            used(V.tensor_tensor(vb[:, t, :], tmp[:, 3, :], table(second, SECOND, "g_v"), ALU.mult))

        def gt_u(g):
            return gt[:, g, :] if g < 3 else qk_f[:, 0, :]

        for g in range(4):
            used(V.tensor_copy(gt_u(g), take(AB_U + g)))
        for g in range(4):
            dve.wait_ge(sgu_ready, g + 1)
            b = table(second, SECOND, "sgu_b")[:, g * P:(g + 1) * P].unsqueeze(1).to_broadcast([P, 4, P])
            signal(V.tensor_tensor(fours(tmp[:, 2, :]), fours(ps[:, g, :]), b, ALU.add), sgu_read)
            dve.wait_ge(sgu_read, g + 1)
            link(V.tensor_tensor(tmp[:, 2, :], tmp[:, 2, :], gt_u(g), ALU.mult))
            link(parts(h_hi[:, 4 + g, :], h_lo[:, 4 + g, :], tmp[:, 2, :]))
            signal(V.memset(r4[:, 2, 0:1], 0.0), mix_ready)

        for h in range(4):
            for n, kt in enumerate((0, 3, 1, 2)):
                at = slice(kt * P, (kt + 1) * P)
                for d in range(2):
                    m = 8 * h + 2 * n + d
                    dve.wait_ge(row_out, 4 * h + 2 * d + 1)
                    if m >= 2:
                        dve.wait_ge(ml_decay, m - 1)
                    signal(V.tensor_tensor(diag[:, m % 2, :], rows[:, 2 * d, at], mask("k_q" if d == 0 else "q_k"), ALU.add), ml_diag)
                dve.wait_ge(ml_s, 4 * h + n + 1)
                for d in range(2):
                    m = 8 * h + 2 * n + d
                    a, b = (kt * P, S) if d == 0 else (0, (kt + 1) * P)
                    dve.wait_ge(ml_decay, m + 1)
                    if m >= 4:
                        dve.wait_ge(ml_pv, m // 4 * 4)
                    signal(V.scalar_tensor_tensor(weights[:, m % 4, a:b], ps[:, 4 + n % 2, a:b], P ** -0.5, decays[:, m % 2, a:b],
                                           ALU.mult, ALU.mult), ml_p)
            dve.wait_ge(ml_pv, 8 * h + 8)
            dve.wait_ge(row_out, 4 * h + 4)
            for d in range(2):
                link(V.tensor_tensor(den[:, :], ps[:, 2 * d + 1, :], rows[:, 2 * d + 1, :], ALU.max))
                link(V.scalar_tensor_tensor(den[:, :], ps[:, 2 * d + 1, :], -1.0, den[:, :], ALU.mult, ALU.max))
                link(V.reciprocal(den[:, :], den[:, :]))
                signal(V.tensor_tensor(part[:, 1 - d, :], ps[:, 2 * d, :], den[:, :], ALU.mult), ml_read)
                dve.wait_ge(ml_read, 2 * h + d + 1)
            signal(V.tensor_tensor(part[:, 1, :], part[:, 1, :], part[:, 0, :], ALU.add), ml_o)
            norm_head(f"head{h}", col("g_head", h), ao[:, h, :], h)

        def feed_forward(panel, name, hidden):
            norm_split_of(name)
            o = output_of(panel)
            with dve.Fori(0, FF_CHUNKS) as c:
                enter(c, {ev_used: 16, w_lo_ready: 16, hid_lo_ready: 8})
                i = c * 4
                for k in range(8):
                    src = take(panel + k, i)
                    used(V.tensor_tensor(hid_f[:, k % 2, :], src, src, ALU.mult))
                    if k:
                        hidden_low(k - 1, (k - 1) % 2, plus(hidden + k, c, 8))
                hidden_low(7, 1, plus(hidden + 8, c, 8))
                for k in range(8):
                    src = take(panel + 8 + k, i)
                    used(V.tensor_tensor(x[:, k, :], x[:, k, :], src, ALU.add))
                leave(FF_CHUNKS)

        def add_to_x(j, i, src):
            used(V.tensor_tensor(x[:, plus(j, i, 4), :], x[:, plus(j, i, 4), :], src, ALU.add))

        take_run(OUT2, KD, add_to_x)
        dve.wait_ge(ev_used, FF1_O)
        feed_forward(FF1, "ffn1", sum(FF0_CHUNKS))

        dve.wait_ge(ev_used, output_of(C_IN))
        norm_split_of("c")
        rr = slice(64, P)
        dve.wait_ge(pos_in, 16)
        TWO_PI, MAGIC = 2 * np.pi, 1.5 * 2.0 ** 23
        C1, C2 = 6.28125, 0.0019350051879882812
        C3 = TWO_PI - C1 - C2
        link(V.tensor_copy(ang[rr, 2, :], pos_i[rr, :]))
        link(V.tensor_scalar(ang[rr, 0, :], ang[rr, 2, :], col("freq")[rr, :], None, ALU.mult))
        for d in range(2):
            quarter = 0.25 * (1 - d)
            k, r = c_raw[rr, 0, :], ang[rr, 1 + d, :]
            link(V.tensor_scalar(k, ang[rr, 0, :], 1 / TWO_PI, quarter, ALU.mult, ALU.add))
            link(V.tensor_scalar(k, k, MAGIC, None, ALU.add))
            link(V.tensor_scalar(k, k, MAGIC, None, ALU.subtract))
            link(V.scalar_tensor_tensor(r, k, -C1, ang[rr, 0, :], ALU.mult, ALU.add))
            link(V.scalar_tensor_tensor(r, k, -C2, r, ALU.mult, ALU.add))
            link(V.scalar_tensor_tensor(r, k, -C3, r, ALU.mult, ALU.add))
            link(V.tensor_scalar(r, r, quarter * TWO_PI, None, ALU.add))
            signal(V.tensor_scalar(r, r, 3.1415925, -3.1415925, ALU.min, ALU.max), ang_ready)
            dve.wait_ge(ang_ready, d + 1)
        for k in range(5):
            used(V.tensor_copy(c_raw[:, k, :], take(C_IN + k)))
        src = take(C_IN + 5)
        dve.wait_ge(trig_ready, 2)
        link(V.tensor_scalar(trig[rr, 1, :], trig[rr, 1, :], col("rope_sign")[rr, :], None, ALU.mult))
        rope(src[rr, :], ang[rr, 0, :], trig[rr, 0, :], trig[rr, 1, :], ang[rr, 1, :])
        link(V.tensor_copy(q_turn[64:96, :], trig[64:96, 0, :]))
        link(V.tensor_copy(q_turn[96:P, :], trig[96:P, 1, :]))
        link(V.tensor_copy(kf_hi[rr, 0, :], ang[rr, 0, :]))
        link(V.tensor_tensor(kf_lo[rr, 0, :], ang[rr, 0, :], kf_hi[rr, 0, :].bitcast(F32), ALU.subtract))
        link(V.tensor_copy(kf_hi[rr, 1, :], kf_hi[rr, 0, :]))
        used(V.tensor_copy(kf_lo[rr, 1, :], kf_lo[rr, 0, :]))
        dve.wait_ge(ev_used, output_of(MLA_V))
        norm_split_of("ckv")
        norm_split_of("cq")
        dve.wait_ge(pool_set, 9)

        def q_scale(n):
            dve.wait_ge(q_proj, n + 1)
            if n:
                dve.wait_ge(q_low, n)
            signal(V.tensor_tensor(q_f[:, :], ps[:, 0, :], q_turn[:, :], ALU.mult), q_scaled, wait=False)

        def q_lower(n):
            dve.wait_ge(q_high, n + 1)
            signal(V.tensor_tensor(qf_lo[:, n % 2, :], q_f[:, :], qf_hi[:, n % 2, :].bitcast(F32), ALU.subtract), q_low,
                   wait=False)

        def k_lower(n):
            dve.wait_ge(k_high, n + 1)
            dve.wait_ge(q_low, n + 1)
            signal(V.tensor_tensor(kf_lo[0:64, n % 2, :], ps[0:64, 0, :], kf_hi[0:64, n % 2, :].bitcast(F32), ALU.subtract),
                   k_low, wait=False)
            low(MLA + n + 2)

        mla = units[NSA_UNITS:]
        low(MLA)
        low(MLA + 1)
        for n in range(2):
            q_scale(n)
            q_lower(n)
            k_lower(n)
        largest(mla[0])
        shift_of(mla[0])
        for n, u in enumerate(mla):
            more = n + 1 < HEADS
            if n:
                result(mla[n - 1])
            if more:
                largest(mla[n + 1])
            if n + 2 < HEADS:
                q_scale(n + 2)
            if more:
                shift_of(mla[n + 1])
            if n + 2 < HEADS:
                q_lower(n + 2)
            if n and mla[n - 1]["last"]:
                pair_low(mla[n - 1])
            if n + 2 < HEADS:
                k_lower(n + 2)
        result(mla[-1])
        pair_low(mla[-1])

        take_run(OUT3, KD, add_to_x)
        dve.wait_ge(ev_used, FF2_O)
        feed_forward(FF2, "ffn2", sum(FF0_CHUNKS) + 8 * FF_CHUNKS)
        dve.wait_ge(ev_used, output_of(PANELS_USED))
        inverse("final")
        for k in range(KD):
            scaled("final", k, col("g_final", k), out=y[:, k, :])


def swapped_order():
    return np.concatenate([np.arange(0, 16), np.arange(32, 48), np.arange(16, 32), np.arange(48, 64)])


def by_feature(w, cols):
    cols = np.asarray(cols)
    out = np.zeros((len(cols) // P, P, PANEL), np.float32)
    for n in range(len(cols) // P):
        c = cols[n * P:(n + 1) * P]
        block = np.zeros((w.shape[0], P), np.float32)
        block[:, c >= 0] = w[:, c[c >= 0]]
        kt = w.shape[0] // P
        out[n, :, :kt * P] = block.reshape(kt, P, P).transpose(1, 0, 2).reshape(P, kt * P)
    return out


def by_token(w, width):
    out = np.zeros((4, P, 2, 512), np.float32)
    out[:, :, :, :width] = w.reshape(4, 2, P, width).transpose(0, 2, 1, 3)
    return out.reshape(4, P, PANEL)


def lay_panels(a):
    order = swapped_order()
    w = a["w_in"][0]
    heads = lambda at, hs: np.concatenate([at + 64 * h + order for h in hs])
    out = [by_feature(w, heads(0, range(4))), by_feature(w, heads(256, range(4))), by_token(w[:, 512:1024], 512),
           by_feature(w, np.arange(1024, 1536)), by_feature(w, np.arange(2048, 2304)),
           by_feature(w, np.concatenate([heads(1536, (t, 4 + t)) for t in range(4)])),
           by_feature(w, heads(2304, range(2))), by_feature(w, heads(2560, range(2))),
           by_token(np.concatenate([w[:, 2432:2560], w[:, 2688:2816]], 1), 256)]
    gate = np.zeros((1, P, PANEL), np.float32)
    g = np.zeros((P, KD, 32), np.float32)
    g[:, :, :24] = w[:, 2816:2840].reshape(KD, P, 24).transpose(1, 0, 2)
    gate[0, :, :256] = g.reshape(P, 256)
    out.append(gate)
    for name in ("cmp_k_w1", "cmp_v_w1"):
        out.append(a[name][0].reshape(4, 4, P, 256).transpose(0, 2, 1, 3).reshape(4, P, PANEL))
    w2 = np.zeros((1, P, PANEL), np.float32)
    k2, v2 = a["cmp_k_w2"][0][:, order], a["cmp_v_w2"][0]
    for m in range(2):
        w2[0, :, m * P:m * P + 64] = k2[m * P:(m + 1) * P]
        w2[0, :, m * P + 64:(m + 1) * P] = k2[m * P:(m + 1) * P]
        w2[0, :, 256 + 64 * m:320 + 64 * m] = v2[m * P:(m + 1) * P]
    out.append(w2)
    rows = np.concatenate([np.arange(512)] + [512 + 64 * h + np.arange(64) for t in range(4) for h in (t, 4 + t)])
    out.append(by_feature(a["w_out"][0][rows], np.arange(D)))

    def down(w, at, tiles):
        part = w[at * P:(at + tiles) * P]
        return by_feature(part, np.arange(D))

    up, dn = a["ffn_w_up"][0], a["ffn_w_down"][0]
    half, at = up.shape[1] // 2, 0
    for tiles in FF0_CHUNKS:
        cols = np.concatenate([side * half + (at + t) * P + np.arange(P) for t in range(tiles) for side in range(2)])
        out += [by_feature(up, cols), down(dn, at, tiles)]
        at += tiles
    w = a["ab_w_in_2"][0]
    gates = -np.ones(P, int)
    for n, row in enumerate((0, 64, 32, 96)):
        gates[row:row + 4] = 2048 + 4 * n + np.arange(4)
    out += [by_feature(w, gates), by_feature(w, np.arange(1024)), by_token(w[:, 1024:1536], 512),
            by_feature(w, np.arange(1536, 2048)), by_token(w[:, 2576:3088], 512), by_feature(w, np.arange(2064, 2576)),
            by_feature(a["ab_w_out_2"][0], np.arange(D))]

    def feed_forward(n):
        for c in range(FF_CHUNKS):
            out.append(by_feature(a["ffn_w1_2"][n], np.arange(c * 1024, (c + 1) * 1024)))
            out.append(down(a["ffn_w2_2"][n], c * 8, 8))

    feed_forward(0)
    kr = -np.ones(P, int)
    kr[64:96] = kr[96:P] = 640 + np.arange(32)
    out.append(by_feature(a["c_w_in_2"][0], np.concatenate([np.arange(640), kr])))
    uq, ukv = a["c_w_uq_2"][0], a["c_w_ukv_2"][0]
    mla = np.zeros((HEADS, P, PANEL), np.float32)
    for h in range(HEADS):
        for k in range(3):
            block = uq[k * P:(k + 1) * P, h * 96:(h + 1) * 96]
            mla[h, :, k * P:k * P + 96] = block
            mla[h, :, k * P + 96:(k + 1) * P] = block[:, 64 + np.array(HALF_SWAP)]
        for k in range(2):
            mla[h, :, 384 + k * P:448 + k * P] = ukv[k * P:(k + 1) * P, h * P:h * P + 64]
    out += [ukv.reshape(2, P, HEADS, 2, 64)[:, :, :, 1, :].reshape(2, P, PANEL), mla, by_feature(a["c_w_out_2"][0], np.arange(D))]
    feed_forward(1)
    out.append(np.zeros((PANELS - PANELS_USED, P, PANEL), np.float32))
    out = np.concatenate(out)
    assert out.shape == (PANELS, P, PANEL), out.shape
    return out


def lay_small(a):
    out = np.zeros((P, SMALL_N), np.float32)

    def put(name, value):
        at, n = SMALL[name]
        out[:, at:at + n] = value

    def columns_of(v):
        return np.asarray(v).reshape(-1, P).T

    put("ident", np.eye(P))
    put("ones", 1.0)
    for name, key in (("g_mix_pre", "norm_mix_pre"), ("g_mix_post", "norm_mix_post"), ("g_ffn_pre", "norm_ffn_pre"),
                      ("g_ffn_post", "norm_ffn_post"), ("gn", "ret_gn_w"), ("g_ab", "ab_norm_2"), ("g_head", "ab_head_g_2"),
                      ("g_c", "c_norm_2"), ("g_cq", "c_q_g_2"), ("g_ckv", "c_kv_g_2"), ("g_final", "final_norm_2")):
        put(name, columns_of(a[key]))
    put("g_ffn1", columns_of(a["ffn_norm_2"][0]))
    put("g_ffn2", columns_of(a["ffn_norm_2"][1]))
    pos = np.stack([a["cmp_k_pos"][0], a["cmp_v_pos"][0]])
    pos = pos.reshape(2, 16, 2, 64).transpose(3, 0, 2, 1).reshape(64, 64)
    put("cmp_pos", np.concatenate([pos, pos]))
    conv = a["ffn_conv"][0].reshape(3, 2, 22, P).transpose(3, 2, 1, 0)
    put("conv0", conv.reshape(P, 132))
    put("conv1", a["ab_conv_2"][0].reshape(5, 8, P).transpose(2, 1, 0).reshape(P, 40))
    at = SMALL["gate_b"][0]
    for n, row in enumerate((0, 64, 32, 96)):
        out[row:row + 4, at] = a["ab_gate_b_2"][0][4 * n:4 * n + 4]
    freq = (np.float32(10000.0) ** (-np.arange(16, dtype=np.float32) / np.float32(16))).astype(np.float32)
    put("freq", np.tile(freq, 8)[:, None])
    put("rope_sign", np.tile(np.repeat([-1.0, 1.0], 16), 4)[:, None])
    put("minus_half", -0.5)
    return out


def rope_tables(positions):
    inv = 1.0 / (np.float32(10000.0) ** (np.arange(0, 64, 2, dtype=np.float32) / np.float32(64)))
    ang = (positions.astype(np.float32)[:, None] * inv.astype(np.float32)[None, :]).astype(np.float64)
    p = np.arange(P)
    f = p % 16 + 16 * (p // 32 % 2)
    sign = np.where(p % 32 < 16, -1.0, 1.0)
    return np.cos(ang)[:, f].T, np.sin(ang)[:, f].T * sign[:, None]


def lay_first():
    out = np.zeros((P, FIRST_N), np.float32)

    def put(name, value):
        at = FIRST[name][0]
        out[:, at:at + value.shape[1]] = value

    c, s = rope_tables(np.arange(S))
    put("rope_c", c)
    put("rope_s", s)
    c, s = rope_tables(np.arange(31) * 16 + 31)
    put("cmp_c", c)
    put("cmp_s", s)
    diff = np.arange(S)[None, :] - np.arange(P)[:, None]
    decay = [np.where(diff >= 0, np.exp(np.log(1.0 - 2.0 ** (-5.0 - h)) * np.maximum(diff, 0)), 0.0) * 64 ** -0.5
             for h in range(4)]
    put("decay", np.concatenate(decay, 1))
    return out


def lay_second(a):
    out = np.zeros((P, SECOND_N), np.float32)
    out[:, 0:512] = a["ab_bs_2"][0].reshape(1, 512)
    out[:, 512:1024] = a["ab_v_g_2"][0][None, :]
    out[:, 1024:] = a["ab_ws_2"][0].transpose(2, 0, 1).reshape(P, 512)
    return out


def lay_masks(dtype):
    out = np.zeros((P, MASKS_N), np.float32)

    def put(name, value):
        out[:, MASKS[name][0]:MASKS[name][0] + value.shape[1]] = value

    r, c = np.arange(P)[:, None], np.arange(P)[None, :]
    put("ident", np.eye(P))
    put("q_k", np.where(c > r, NEG, 0.0))
    put("k_q", np.where(r > c, NEG, 0.0))
    key, query = np.arange(P), np.arange(S)
    bad = (key[:, None] * 16 + 31 > query[None, :]) | (key[:, None] >= 31)
    put("cmp_k_q", np.where(bad, NEG, 0.0))
    by_tile = np.where(bad, NEG, 0.0)[:32].reshape(32, NT, P).transpose(2, 1, 0).reshape(P, P)
    put("cmp_q_k", by_tile)
    return out.astype(dtype)


def kernel(**inputs):
    import concourse.bacc as bacc
    from concourse.bass_utils import run_bass_kernel_spmd

    a = {k: np.asarray(v) for k, v in inputs.items()}
    bf16 = mybir.dt.np(BF16)
    arrays = {
        "in_panels": lay_panels(a), "in_small": lay_small(a), "in_first": lay_first(), "in_second": lay_second(a),
        "in_masks": lay_masks(bf16), "in_x": np.ascontiguousarray(a["x"][0].T.reshape(KD, P, S)),
        "in_positions": np.ascontiguousarray(np.broadcast_to(a["positions_2"].astype(np.int32), (64, S))),
    }
    nc = bacc.Bacc("TRN2", target_bir_lowering=False, num_devices=1)
    dram = {name[3:]: nc.dram_tensor(name, v.shape, mybir.dt.from_np(v.dtype), kind="ExternalInput").ap()
            for name, v in arrays.items()}
    dram["out"] = nc.dram_tensor("out_0", (KD, P, S), F32, kind="ExternalOutput").ap()
    build(nc, dram)
    r = run_bass_kernel_spmd(nc, [arrays], core_ids=[0])
    return np.ascontiguousarray(np.asarray(r.results[0]["out_0"]).reshape(D, S).T)[None]
```

```python
from contextlib import ExitStack

import numpy as np

import concourse.bass as bass
from concourse import mybir

F32 = mybir.dt.float32
F32R = mybir.dt.float32r
BF16 = mybir.dt.bfloat16
I32 = mybir.dt.int32
ACT = mybir.ActivationFunctionType
ALU = mybir.AluOpType
AX = mybir.AxisListType

P = 128
S = 512
NT = S // P
D = 1024
KD = D // P
PANEL = 1024
NEG = -1e30
HALF_SWAP = [*range(16, 32), *range(16)]

RET_Q, RET_K, RET_V, RET_G = 0, 2, 4, 8
CMP_IN, NSA_Q, NSA_K, NSA_V, NSA_GATE = 12, 14, 18, 20, 24
CMP_W1, CMP_W2, OUT1 = 25, 33, 34
FF0 = 42
FF0_CHUNKS = [8, 8, 6]
AB_GATE = FF0 + sum(2 * c + KD for c in FF0_CHUNKS)
AB_QK = AB_GATE + 1
AB_V, AB_O, AB_VB, AB_U = AB_QK + 8, AB_QK + 12, AB_QK + 16, AB_QK + 20
OUT2 = AB_U + 4
FF1 = OUT2 + KD
FF_CHUNKS = 4
C_IN = FF1 + FF_CHUNKS * 16
MLA_V = C_IN + 6
MLA = MLA_V + 2
HEADS = 16
OUT3 = MLA + HEADS
FF2 = OUT3 + KD
PANELS_USED = FF2 + FF_CHUNKS * 16
PANELS = (PANELS_USED + 2 + 3) // 4 * 4


def columns(*parts):
    at, out = 0, {}
    for name, n in parts:
        out[name] = (at, n)
        at += n
    return out, at


SMALL, SMALL_N = columns(
    ("ident", 128), ("ones", 128), ("g_mix_pre", 8), ("g_mix_post", 8), ("g_ffn_pre", 8), ("g_ffn_post", 8),
    ("gn", 4), ("cmp_pos", 64), ("conv0", 132), ("g_ab", 8), ("conv1", 40), ("gate_b", 1), ("g_head", 4),
    ("g_c", 8), ("g_cq", 3), ("g_ckv", 2), ("g_ffn1", 8), ("g_ffn2", 8), ("g_final", 8), ("freq", 1),
    ("rope_sign", 1), ("minus_half", 16))
FIRST, FIRST_N = columns(("rope_c", 512), ("rope_s", 512), ("cmp_c", 32), ("cmp_s", 32), ("decay", 2048))
SECOND, SECOND_N = columns(("sgu_b", 512), ("g_v", 512), ("ws_t", 512))
MASKS, MASKS_N = columns(("ident", 128), ("q_k", 128), ("k_q", 128), ("cmp_q_k", 128), ("cmp_k_q", 512))


def plus(v, i, k):
    return v if i is None else i * k + v


NORM_LIST = (
    [("mix_pre", KD, D, 1e-6), ("mix_post", KD, D, 1e-6), ("ffn_pre", KD, D, 1e-6), ("ffn_post", KD, D, 1e-6), ("ab", KD, D, 1e-6)]
    + [("ffn1", KD, D, 1e-6), ("c", KD, D, 1e-6), ("ckv", 2, 256, 1e-6), ("cq", 3, 384, 1e-6),
       ("ffn2", KD, D, 1e-6), ("final", KD, D, 1e-6)])
NORM = {}
for _n, (_name, _k, _d, _e) in enumerate(NORM_LIST):
    NORM[_name] = (_n, sum(q[1] for q in NORM_LIST[:_n]), _k, _d, _e)
SPLIT_NORMS = ("mix_pre", "ffn_pre", "ab", "ffn1", "c", "ckv", "cq", "ffn2")
SPLITS_BEFORE = {}
_at = 0
for _name in SPLIT_NORMS:
    SPLITS_BEFORE[_name] = _at
    _at += NORM[_name][2]


def output_of(panel):
    return panel if panel <= CMP_W1 else panel - 2 if panel <= MLA_V else panel - 2 - 2 - HEADS


def attention_memory(sb, c, tag="a"):
    return dict(
        pr=sb("pr" + tag, [P, 4, S], F32, c), shift=sb("shift" + tag, [4, 2, S], F32R, c),
        negm=sb("negm" + tag, [P, 2, 4], F32, c), mx=sb("mx" + tag, [P, 2, 4], F32, c), w4=sb("w4" + tag, [P, 4], F32, c),
        osb=sb("osb" + tag, [65, 2, S], F32, c), by_token=sb("by_token" + tag, [P, 2, NT, P], F32, c), term=sb("term" + tag, [P, NT, 64], F32, c))


def build(nc, A):
    with ExitStack() as ctx:
        build_in(nc, A, ctx)


def build_in(nc, A, ctx):
    def sb(name, shape, dt, c=ctx):
        return c.enter_context(nc.sbuf_tensor(name, shape, dt))

    def sem(name):
        return ctx.enter_context(nc.semaphore(name))

    x = sb("x", [P, KD, S], F32)
    small = sb("small", [P, SMALL_N], F32)
    masks = sb("masks", [P, MASKS_N], BF16)
    raw = sb("raw", [P, 4, PANEL], F32)
    w_hi = sb("w_hi", [P, 2, PANEL], F32R)
    w_lo = sb("w_lo", [P, 2, PANEL], F32R)
    ev = sb("ev", [P, 4, S], F32)
    h_hi = sb("h_hi", [P, KD, S], F32R)
    h_lo = sb("h_lo", [P, KD, S], F32R)
    tmp = sb("tmp", [P, 4, S], F32)
    sq = sb("sq", [P, 2, S], F32)
    r4 = sb("r4", [P, 6, 4], F32)
    ones_r = sb("ones_r", [4, P], F32R)
    ps = ctx.enter_context(nc.psum_tensor("ps", [P, 8, S], F32))

    with ExitStack() as c:
        first = sb("first", [P, FIRST_N], F32, c)
        rq_hi, rq_lo = sb("rq_hi", [P, 2, S], F32R, c), sb("rq_lo", [P, 2, S], F32R, c)
        rk_hi, rk_lo = sb("rk_hi", [P, 2, S], F32R, c), sb("rk_lo", [P, 2, S], F32R, c)
        nq_hi, nq_lo = sb("nq_hi", [P, 4, S], F32R, c), sb("nq_lo", [P, 4, S], F32R, c)
        nk_hi, nk_lo = sb("nk_hi", [P, 2, S], F32R, c), sb("nk_lo", [P, 2, S], F32R, c)
        rv = sb("rv", [P, NT, 512], F32, c)
        rg = sb("rg", [P, 4, S], F32, c)
        nv = sb("nv", [P, NT, 2, 2, 65], F32, c)
        vc = sb("vc", [P, 2, 65], F32, c)
        gates = sb("gates", [P, NT, 32], F32, c)
        kc_hi, kc_lo = sb("kc_hi", [P, P], F32R, c), sb("kc_lo", [P, P], F32R, c)
        ch_hi, ch_lo = sb("ch_hi", [P, 2, 64], F32R, c), sb("ch_lo", [P, 2, 64], F32R, c)
        cv_hi, cv_lo = sb("cv_hi", [P, 2, 2, P], F32R, c), sb("cv_lo", [P, 2, 2, P], F32R, c)
        kc_f = sb("kc_f", [P, 4, 32], F32, c)
        with ExitStack() as cc:
            xg_f = sb("xg_f", [P, 16, 62], F32, cc)
            xg_hi, xg_lo = sb("xg_hi", [P, 2, 16, 62], F32R, cc), sb("xg_lo", [P, 2, 16, 62], F32R, cc)
        with ExitStack() as cc:
            at1 = attention_memory(sb, cc)
            ret16 = sb("ret16", [P, 2, 16], F32, cc)
        del cc
    with ExitStack() as c:
        hid_hi, hid_lo = sb("hid_hi", [P, 8, S], F32R, c), sb("hid_lo", [P, 8, S], F32R, c)
        hid_f = sb("hid_f", [P, 2, S], F32, c)
        conv_t = sb("conv_t", [P, 2, S], F32, c)
        act_t = sb("act_t", [P, S], F32, c)
        y = sb("y", [P, KD, S], F32, c)
    with ExitStack() as c:
        second = sb("second", [P, SECOND_N], F32, c)
        aq_hi, aq_lo = sb("aq_hi", [P, 8, S], F32R, c), sb("aq_lo", [P, 8, S], F32R, c)
        av = sb("av", [P, NT, 4, 129], F32, c)
        ao = sb("ao", [P, 4, S], F32, c)
        a_t = sb("a_t", [P, 2, NT, 64], F32, c)
        neg_m, floor_m = sb("neg_m", [64, S], F32, c), sb("floor_m", [64, S], F32, c)
        with ExitStack() as cc:
            gt = sb("gt", [P, 3, S], F32, cc)
            scan = sb("scan", [64, 2, 2 * S], F32, cc)
            li, la = sb("li", [64, S], F32, cc), sb("la", [64, S], F32, cc)
            vb = sb("vb", [P, NT, 512], F32, cc)
            qk_c = sb("qk_c", [P, 2, S], F32, cc)
            qk_s = sb("qk_s", [P, 2, S], F32, cc)
        with ExitStack() as cc:
            rows = sb("rows", [P, 4, S], F32, cc)
            decays = sb("decays", [P, 2, S], F32, cc)
            diag = sb("diag", [P, 2, P], F32, cc)
            weights = sb("weights", [P, 4, S], F32, cc)
            head_sq = sb("head_sq", [P, S], F32, cc)
            den = sb("den", [P, 2, NT], F32, cc)
            part = sb("part", [P, 2, S], F32, cc)
    with ExitStack() as c:
        c_raw = sb("c_raw", [P, 5, S], F32, c)
        cq_hi, cq_lo = sb("cq_hi", [P, 5, S], F32R, c), sb("cq_lo", [P, 5, S], F32R, c)
        kr_hi, kr_lo = sb("kr_hi", [P, S], F32R, c), sb("kr_lo", [P, S], F32R, c)
        qf_hi, qf_lo = sb("qf_hi", [P, 2, S], F32R, c), sb("qf_lo", [P, 2, S], F32R, c)
        kf_hi, kf_lo = sb("kf_hi", [P, 2, S], F32R, c), sb("kf_lo", [P, 2, S], F32R, c)
        q_f = sb("q_f", [P, S], F32, c)
        q_turn = sb("q_turn", [P, S], F32, c)
        mla_v = sb("mla_v", [P, NT, HEADS, 65], F32, c)
        trig = sb("trig", [P, 2, S], F32, c)
        ang = sb("ang", [P, 3, S], F32, c)
        pos_i = ang[:, 0, :].bitcast(I32)
        at2 = attention_memory(sb, c, "b")

    ones = small[:, SMALL["ones"][0]:SMALL["ones"][0] + P]
    ident = small[:, SMALL["ident"][0]:SMALL["ident"][0] + P]

    def col(name, n=0, k=1):
        return small[:, SMALL[name][0] + n:SMALL[name][0] + n + k]

    def mask(name):
        return masks[:, MASKS[name][0]:MASKS[name][0] + MASKS[name][1]]

    def table(t, where, name):
        return t[:, where[name][0]:where[name][0] + where[name][1]]

    raw_in = [sem(f"raw_in{n}") for n in range(4)]
    consts_in, x_in, first_in, second_in, pos_in = (sem(n) for n in (
        "consts_in", "x_in", "first_in", "second_in", "pos_in"))
    w_hi_ready, w_lo_ready, panel_read, tile_out, ev_used = (sem(n) for n in (
        "w_hi_ready", "w_lo_ready", "panel_read", "tile_out", "ev_used"))
    sq_ready, acc_ready, ss_ready, ms_ready, inv_ready, inv_diag, inv_wide, normed, n_hi, n_lo = (sem(n) for n in (
        "sq_ready", "acc_ready", "ss_ready", "ms_ready", "inv_ready", "inv_diag", "inv_wide", "normed", "n_hi", "n_lo"))
    dve_step, pool_set, x_ready, mix_ready = (sem(n) for n in ("dve_step", "pool_set", "x_ready", "mix_ready"))
    gates_turned, cmp_in_ready, cmp_turned, cmp_ready, v_ready = (sem(n) for n in (
        "gates_turned", "cmp_in_ready", "cmp_turned", "cmp_ready", "v_ready"))
    ret_sum, ret_ms, ret_inv, ret_diag, ret_wide = (sem(n) for n in (
        "ret_sum", "ret_ms", "ret_inv", "ret_diag", "ret_wide"))
    turned, turned_high = sem("turned"), sem("turned_high")
    v_copied, q_proj, q_scaled, q_high, q_low, k_proj, k_high, k_low = (sem(n) for n in (
        "v_copied", "q_proj", "q_scaled", "q_high", "q_low", "k_proj", "k_high", "k_low"))
    ret_s, ret_p, ret_pv, ret_o = (sem(n) for n in ("ret_s", "ret_p", "ret_pv", "ret_o"))
    mx_ready, mx_done, negm_ready, negm_turned, shift_ready, s_ready, exp_done, pv_done = (sem(n) for n in (
        "mx_ready", "mx_done", "negm_ready", "negm_turned", "shift_ready", "s_ready", "exp_done", "pv_done"))
    o_used, o_out, o_turned = sem("o_used"), sem("o_out"), sem("o_turned")
    conv_done, gelu_done, hid_ready, hid_hi_ready, hid_lo_ready = (sem(n) for n in (
        "conv_done", "gelu_done", "hid_ready", "hid_hi_ready", "hid_lo_ready"))
    gate_raw, gate_abs, gate_exp, gate_ln, scan_floor, floor_exp, a_ready, a_turned = (sem(n) for n in (
        "gate_raw", "gate_abs", "gate_exp", "gate_ln", "scan_floor", "floor_exp", "a_ready", "a_turned"))
    vb_ms, vb_inv, sgu_ready, sgu_read, qk_mid, qk_silu, qk_high, qk_low = (sem(n) for n in (
        "vb_ms", "vb_inv", "sgu_ready", "sgu_read", "qk_mid", "qk_silu", "qk_high", "qk_low"))
    row_wide, row_out, ml_s, ml_diag, ml_decay, ml_p, ml_pv, ml_o = (sem(n) for n in (
        "row_wide", "row_out", "ml_s", "ml_diag", "ml_decay", "ml_p", "ml_pv", "ml_o"))
    head_square, head_ms, head_inv, head_scaled, head_turned = (sem(n) for n in (
        "head_square", "head_ms", "head_inv", "head_scaled", "head_turned"))
    ang_ready, trig_ready = sem("ang_ready"), sem("trig_ready")
    stored = sem("stored")

    units = []
    for t in range(4):
        for half in range(2):
            for s in range(3):
                r = slice(64 * half, 64 * half + 64)
                k = (kc_hi[r, :], kc_lo[r, :]) if s == 0 else (nk_hi[r, s - 1, :], nk_lo[r, s - 1, :])
                v = (lambda kt, half=half: vc[:, half, :]) if s == 0 else (
                    lambda kt, half=half, s=s: nv[:, kt, s - 1, half, :])
                units.append(dict(q=(nq_hi[r, t, :], nq_lo[r, t, :]), k=k, v=v, half=half, scale=0.125, at=at1, s=s, t=t,
                                  kind="cmp" if s == 0 else "causal", tiles=1 if s == 0 else NT, gate=s * 8 + half * 4 + t,
                                  pair=t, last=half == 1 and s == 2))
    NSA_UNITS = len(units)
    for u in range(HEADS):
        units.append(dict(q=(qf_hi[:, u % 2, :], qf_lo[:, u % 2, :]), k=(kf_hi[:, u % 2, :], kf_lo[:, u % 2, :]),
                          v=lambda kt, u=u: mla_v[:, kt, u, :], half=u % 2, scale=96 ** -0.5, at=at2, s=0, t=u // 2,
                          kind="all", tiles=NT, gate=None, pair=4 + u // 2, last=u % 2 == 1))
    for n, w in enumerate(units):
        w["n"], w["first"] = n, sum(q["tiles"] for q in units[:n])
        w["k_mix"] = w["t"] + (4 if w["gate"] is not None else 0)
    MIX_BEFORE = [4 + p if p < 4 else 16 + p - 4 for p in range(12)]

    norm_source = {"mix_pre": x, "mix_post": y, "ffn_pre": x, "ffn_post": y, "ab": x, "ffn1": x, "c": x, "ffn2": x,
                   "final": x, "cq": c_raw[:, 0:3, :], "ckv": c_raw[:, 3:5, :]}
    norm_gain = {"mix_pre": "g_mix_pre", "mix_post": "g_mix_post", "ffn_pre": "g_ffn_pre", "ffn_post": "g_ffn_post",
                 "ab": "g_ab", "ffn1": "g_ffn1", "c": "g_c", "ffn2": "g_ffn2", "final": "g_final", "cq": "g_cq",
                 "ckv": "g_ckv"}
    norm_split = {name: (h_hi, h_lo) for name in SPLIT_NORMS}
    norm_split["cq"] = (cq_hi[:, 0:3, :], cq_lo[:, 0:3, :])
    norm_split["ckv"] = (cq_hi[:, 3:5, :], cq_lo[:, 3:5, :])

    def down_tile(pe, dense, panel, i, tiles, hidden, c):
        dense(panel, i, moving=(hid_hi, hid_lo), tiles=tiles,
              **({} if hidden is None else dict(ready=hid_lo_ready, base=plus(hidden, c, 8))))

    def down(pe, dense, panel, tiles, hidden):
        for k in range(KD):
            down_tile(pe, dense, panel + k, None, tiles, hidden if k == 0 else None, None)

    block = ctx.enter_context(nc.Block())

    @block.sync
    def _(sp):
        for n in range(4):
            sp.dma_start(raw[:, n, :], A["panels"][n]).then_inc(raw_in[n], 16)
        with sp.Fori(1, PANELS // 4) as i:
            for n in range(4):
                sp.wait_ge(w_lo_ready, i * 4 + (n - 3))
                sp.dma_start(raw[:, n, :], A["panels"][i * 4 + n]).then_inc(raw_in[n], 16)
        first_norm = NORM["final"][1]
        for k in range(KD):
            sp.wait_ge(normed, first_norm + k + 1)
            sp.dma_start(A["out"][k], y[:, k, :]).then_inc(stored, 16)
        sp.wait_ge(stored, 16 * KD)

    @block.gpsimd
    def _(pool):
        nc.gpsimd.memset(ones_r[:].bitcast(F32), 1.0).then_inc(pool_set, 1)
        nc.gpsimd.memset(nv[:], 1.0).then_inc(pool_set, 1)
        nc.gpsimd.memset(vc[:], 1.0).then_inc(pool_set, 1)
        nc.gpsimd.memset(cv_hi[:].bitcast(F32), 0.0).then_inc(pool_set, 1)
        nc.gpsimd.memset(cv_lo[:].bitcast(F32), 0.0).then_inc(pool_set, 1)
        nc.gpsimd.memset(kc_hi[:].bitcast(F32), 0.0).then_inc(pool_set, 1)
        nc.gpsimd.memset(kc_lo[:].bitcast(F32), 0.0).then_inc(pool_set, 1)
        pool.wait_ge(consts_in, 32)

        def inverse_root(name):
            n = NORM[name][0]
            pool.wait_ge(ms_ready, n + 1)
            nc.gpsimd.tensor_tensor(r4[:, 1, :], r4[:, 0, :], col("minus_half", 0, 4), ALU.pow).then_inc(inv_ready, 1)

        inverse_root("mix_pre")
        pool.wait_ge(ret_ms, 1)
        nc.gpsimd.tensor_tensor(ret16[:, 1, :], ret16[:, 0, :], col("minus_half", 0, 16), ALU.pow).then_inc(ret_inv, 1)
        for turn, (post, pre) in enumerate((("mix_post", "ffn_pre"), ("ffn_post", "ab"))):
            inverse_root(post)
            for k in range(KD):
                pool.wait_ge(normed, NORM[post][1] + k + 1)
                nc.gpsimd.tensor_tensor(x[:, k, :], x[:, k, :], tmp[:, (NORM[post][1] + k) % 2, :], ALU.add).then_inc(x_ready, 1)
            inverse_root(pre)
        for t in range(NT):
            pool.wait_ge(vb_ms, t + 1)
            nc.gpsimd.tensor_tensor(r4[:, 3, :], r4[:, 2, :], col("minus_half", 0, 4), ALU.pow).then_inc(vb_inv, 1)
        for h in range(4):
            pool.wait_ge(head_ms, h + 1)
            nc.gpsimd.tensor_tensor(r4[:, 5, :], r4[:, 4, :], col("minus_half", 0, 4), ALU.pow).then_inc(head_inv, 1)
        for name, *_ in NORM_LIST[5:7]:
            inverse_root(name)
        pool.wait_ge(normed, NORM["c"][1] + KD)
        nc.gpsimd.memset(mla_v[:, :, :, 64:65], 1.0).then_inc(pool_set, 1)
        nc.gpsimd.memset(q_turn[0:64, :], 1.0).then_inc(pool_set, 1)
        for name, *_ in NORM_LIST[7:]:
            inverse_root(name)

    @block.tensor
    def _(pe):
        def product(out, a, b, start, stop):
            nc.tensor.matmul(out, a[0], b[0], start=start, stop=False)
            nc.tensor.matmul(out, a[0], b[1], start=False, stop=False)
            return nc.tensor.matmul(out, a[1], b[0], start=False, stop=stop)

        def w(panel, a, b):
            return w_hi[:, panel % 2, a:b], w_lo[:, panel % 2, a:b]

        def dense(panel, i=None, moving=(h_hi, h_lo), tiles=KD, ready=None, base=0, most=None):
            o = output_of(panel)
            pe.wait_ge(w_lo_ready, plus(panel + 1, i, 4))
            if o >= 4:
                pe.wait_ge(tile_out, plus(o - 3, i, 4))
            for k in range(tiles):
                if ready is not None:
                    pe.wait_ge(ready, base + k + 1 if most is None else min(base + k + 1, most))
                last = product(ps[:, o % 4, :], w(panel, k * P, (k + 1) * P), (moving[0][:, k, :], moving[1][:, k, :]),
                               k == 0, k == tiles - 1)
            last.then_inc(panel_read, 1)

        def token_major(panel, width):
            o = output_of(panel)
            pe.wait_ge(tile_out, o)
            for c in range(4):
                pe.wait_ge(w_lo_ready, panel + c + 1)
                for kk in range(2):
                    for t in range(NT):
                        kt = 2 * c + kk
                        at = slice(t * P, (t + 1) * P)
                        last = product(ps[:, (o + t) % 4, 0:width], (h_hi[:, kt, at], h_lo[:, kt, at]),
                                       w(panel + c, kk * 512, kk * 512 + width), kt == 0, kt == KD - 1)
                last.then_inc(panel_read, 1)

        def norm(name):
            n, before, tiles, width, _ = NORM[name]
            pe.wait_ge(acc_ready, before + tiles)
            for t in range(NT):
                last = nc.tensor.matmul(ps[:, 6, t:t + 1], tmp[:, 2, t * P:(t + 1) * P], ones[:, 0:1], start=True, stop=True)
            last.then_inc(ss_ready, 1)
            pe.wait_ge(inv_diag, n + 1)
            if before:
                pe.wait_ge(normed, before)
            nc.tensor.matmul(ps[:, 7, :], ones, tmp[:, 3, :], start=True, stop=True).then_inc(inv_wide, 1)

        def maxima(u, tiles=range(NT)):
            n, (q, _), (k, _) = u["n"], u["q"], u["k"]
            if u["kind"] == "cmp":
                if n:
                    pe.wait_ge(mx_done, 4 * n)
                for t in range(NT):
                    out = ps[:, 2, t * 32:(t + 1) * 32]
                    nc.tensor.matmul(out, mask("ident"), mask("cmp_q_k")[:, t * 32:(t + 1) * 32], start=True, stop=False)
                    last = nc.tensor.matmul(out, q[:, t * P:(t + 1) * P], k[:, 0:32], start=False, stop=True)
                last.then_inc(mx_ready, 4)
                return
            for t in tiles:
                keys = (t + 1) * P if u["kind"] == "causal" else S
                out = ps[:, 2 + t % 2, :]
                if 4 * n + t >= 2:
                    pe.wait_ge(mx_done, 4 * n + t - 1)
                last = nc.tensor.matmul(out[:, 0:keys], q[:, t * P:(t + 1) * P], k[:, 0:keys], start=True,
                                        stop=u["kind"] != "causal")
                if u["kind"] == "causal":
                    last = nc.tensor.matmul(out[:, keys - P:keys], mask("ident"), mask("q_k"), start=False, stop=True)
                last.then_inc(mx_ready, 1)

        def turn(u):
            n = u["n"]
            pe.wait_ge(negm_ready, n + 1)
            if n:
                pe.wait_ge(shift_ready, n)
            if n >= 2:
                pe.wait_ge(o_used, n - 1)
            nc.tensor.matmul(ps[0:4, 7, 384:512], u["at"]["negm"][:, n % 2, :], ident, start=True,
                             stop=True).then_inc(negm_turned, 1)

        def scores(u, kt):
            n, m = u["n"], u["first"] + kt
            a = kt * P if u["kind"] == "causal" else 0
            out = ps[:, 4 + m % 2, :]
            pe.wait_ge(shift_ready, n + 1)
            if m >= 2:
                pe.wait_ge(exp_done, m - 1)
            nc.tensor.matmul(out[:, a:S], ones_r[:, :], u["at"]["shift"][:, n % 2, a:S], start=True, stop=False)
            if u["kind"] == "causal":
                nc.tensor.matmul(out[:, a:a + P], mask("ident"), mask("k_q"), start=False, stop=False)
            if u["kind"] == "cmp":
                nc.tensor.matmul(out[:, :], mask("ident"), mask("cmp_k_q"), start=False, stop=False)
            k = (u["k"][0][:, kt * P:(kt + 1) * P], u["k"][1][:, kt * P:(kt + 1) * P])
            product(out[:, a:S], k, (u["q"][0][:, a:S], u["q"][1][:, a:S]), False, True).then_inc(s_ready, 1)

        def values(u, kt):
            n, m = u["n"], u["first"] + kt
            a = kt * P if u["kind"] == "causal" else 0
            pe.wait_ge(exp_done, m + 1)
            if kt == 0 and n:
                pe.wait_ge(o_out, n)
            nc.tensor.matmul(ps[0:65, 6, a:S], u["v"](kt), u["at"]["pr"][:, m % 4, a:S], start=kt == 0,
                             stop=kt == u["tiles"] - 1).then_inc(pv_done, 1)

        def turn_result(u):
            n = u["n"]
            pe.wait_ge(o_out, n + 1)
            if n:
                pe.wait_ge(o_used, n)
            for t in range(NT):
                last = nc.tensor.transpose(ps[:, 7, t * 65:(t + 1) * 65], u["at"]["osb"][:, n % 2, t * P:(t + 1) * P],
                                           ident[0:65, 0:65])
            last.then_inc(o_turned, 1)

        def turn_pair(u):
            pe.wait_ge(o_used, u["n"] + 1)
            if u["k_mix"] % 8:
                pe.wait_ge(mix_ready, MIX_BEFORE[u["pair"]])
            for t in range(NT):
                last = nc.tensor.transpose(ps[:, 1, t * P:(t + 1) * P], u["at"]["by_token"][:, u["pair"] % 2, t, :], ident)
            last.then_inc(turned, 1)

        pe.wait_ge(consts_in, 32)
        pe.wait_ge(x_in, 16)
        norm("mix_pre")
        for panel in range(RET_Q, RET_V):
            dense(panel, ready=n_lo if panel == RET_Q else None)
        token_major(RET_V, 512)
        for panel in range(RET_G, NSA_V):
            dense(panel)
        token_major(NSA_V, 256)
        o = output_of(NSA_GATE)
        pe.wait_ge(w_lo_ready, NSA_GATE + 1)
        pe.wait_ge(tile_out, o - 3)
        for k in range(KD):
            last = product(ps[0:32, o % 4, :], w(NSA_GATE, k * 32, (k + 1) * 32), (h_hi[:, k, :], h_lo[:, k, :]),
                           k == 0, k == KD - 1)
        last.then_inc(panel_read, 1)

        def turn_hidden(kv):
            o = CMP_W1 + 2 * kv
            pe.wait_ge(tile_out, o + 1)
            for m in range(2):
                last = nc.tensor.transpose(ps[:, (o + 1) % 4, m * 64:m * 64 + 62], ev[0:62, o % 4, m * P:(m + 1) * P],
                                           ident[0:62, 0:62])
            last.then_inc(cmp_turned, 1)

        for kv in range(2):
            o = CMP_W1 + 2 * kv
            pe.wait_ge(tile_out, o - 2)
            pe.wait_ge(cmp_in_ready, kv + 1)
            for c in range(4):
                panel = CMP_W1 + 4 * kv + c
                pe.wait_ge(w_lo_ready, panel + 1)
                for kk in range(4):
                    kt = 4 * c + kk
                    last = product(ps[0:62, o % 4, 0:256], (xg_hi[:, kv, kt, :], xg_lo[:, kv, kt, :]),
                                   w(panel, kk * 256, (kk + 1) * 256), kt == 0, kt == 15)
                last.then_inc(panel_read, 1)
                if kv == 0 and c == 0:
                    pe.wait_ge(tile_out, output_of(NSA_GATE) + 1)
                    for t in range(NT):
                        last = nc.tensor.transpose(ps[:, 6, t * 32:(t + 1) * 32],
                                                   ev[0:32, output_of(NSA_GATE) % 4, t * P:(t + 1) * P], ident[0:32, 0:32])
                    last.then_inc(gates_turned, 1)
                if kv == 1 and c == 0:
                    turn_hidden(0)
        turn_hidden(1)
        pe.wait_ge(w_lo_ready, CMP_W2 + 1)
        pe.wait_ge(ev_used, CMP_W1 + 4)
        o = CMP_W1 + 4
        pe.wait_ge(tile_out, o)
        for m in range(2):
            product(ps[:, o % 4, 0:62], w(CMP_W2, m * P, (m + 1) * P), (ch_hi[:, m, 0:62], ch_lo[:, m, 0:62]), m == 0, m == 1)
        for g in range(2):
            for m in range(2):
                last = product(ps[:, (o + 1 + g) % 4, 0:64], (cv_hi[:, m, g, :], cv_lo[:, m, g, :]),
                               w(CMP_W2, 256 + m * 64, 320 + m * 64), m == 0, m == 1)
        last.then_inc(panel_read, 1)

        pe.wait_ge(tile_out, CMP_W1 + 7)
        pe.wait_ge(ev_used, CMP_W1)
        for h in range(4):
            r = slice(64 * (h % 2), 64 * (h % 2) + 64)

            def ret_values(m, kt):
                pe.wait_ge(ret_p, m + 1)
                nc.tensor.matmul(ps[:, h % 2, kt * P:S], rv[:, kt, h * P:(h + 1) * P], at1["pr"][:, m % 4, kt * P:S],
                                 start=kt == 0, stop=kt == NT - 1).then_inc(ret_pv, 1)

            if h >= 2:
                pe.wait_ge(ret_o, h - 1)
            for kt in range(NT):
                m = 4 * h + kt
                if m >= 2:
                    pe.wait_ge(ret_p, m - 1)
                at = slice(kt * P, (kt + 1) * P)
                product(ps[:, 4 + m % 2, kt * P:S], (rk_hi[r, h // 2, at], rk_lo[r, h // 2, at]),
                        (rq_hi[r, h // 2, kt * P:S], rq_lo[r, h // 2, kt * P:S]), True, True).then_inc(ret_s, 1)
                if kt:
                    ret_values(m - 1, kt - 1)
            ret_values(4 * h + 3, 3)

        def ret_widen(h):
            pe.wait_ge(ret_diag, h + 1)
            nc.tensor.matmul(ps[:, 0, :], ones, tmp[:, 3, :], start=True, stop=True).then_inc(ret_wide, 1)

        pe.wait_ge(pool_set, 7)
        pe.wait_ge(cmp_ready, 3)
        nsa = units[:NSA_UNITS]
        maxima(nsa[0])
        maxima(nsa[1])
        turn(nsa[0])
        pe.wait_ge(ret_o, 4)
        for n in range(16):
            last = nc.tensor.matmul(ps[:, 0, n:n + 1], tmp[:, n // 4, n % 4 * P:(n % 4 + 1) * P],
                                    ones[:, 0:1], start=True, stop=True)
        last.then_inc(ret_sum, 1)
        for n, u in enumerate(nsa):
            ahead = nsa[n + 2] if n + 2 < NSA_UNITS else None
            apart = ahead is not None and ahead["kind"] != "cmp"
            scores(u, 0)
            if u["tiles"] > 1:
                scores(u, 1)
            if n:
                turn_result(nsa[n - 1])
            if ahead is not None:
                maxima(ahead, range(0, 1))
            values(u, 0)
            if apart:
                maxima(ahead, range(1, 2))
            if n + 1 < NSA_UNITS:
                turn(nsa[n + 1])
            if n and nsa[n - 1]["last"]:
                turn_pair(nsa[n - 1])
            if u["tiles"] > 1:
                scores(u, 2)
                values(u, 1)
            if apart:
                maxima(ahead, range(2, 3))
            if u["tiles"] > 1:
                scores(u, 3)
                values(u, 2)
            if apart:
                maxima(ahead, range(3, 4))
            if n < 4:
                ret_widen(n)
            if u["tiles"] > 1:
                values(u, 3)
        turn_result(nsa[-1])
        turn_pair(nsa[-1])

        def dense_run(panel, count, **first):
            for j in range(4):
                dense(panel + j, **(first if j == 0 else {}))
            if count > 4:
                with pe.Fori(1, count // 4) as i:
                    for j in range(4):
                        dense(panel + j, i)

        dense_run(OUT1, KD, ready=mix_ready, base=0)
        norm("mix_post")
        norm("ffn_pre")
        panel, hidden = FF0, 0
        for c, tiles in enumerate(FF0_CHUNKS):
            dense_run(panel, 2 * tiles, **(dict(ready=n_lo, base=SPLITS_BEFORE["ffn_pre"]) if c == 0 else {}))
            panel += 2 * tiles
            down(pe, dense, panel, tiles, hidden)
            panel += KD
            hidden += tiles
        norm("ffn_post")

        norm("ab")
        dense(AB_GATE, ready=n_lo, base=SPLITS_BEFORE["ab"])
        for panel in range(AB_QK, AB_V):
            dense(panel)
        token_major(AB_V, 512)
        for panel in range(AB_O, AB_VB):
            dense(panel)
        token_major(AB_VB, 512)
        for panel in range(AB_U, OUT2):
            dense(panel)

        pe.wait_ge(tile_out, output_of(OUT2))
        pe.wait_ge(ev_used, output_of(OUT2))
        for g in range(4):
            for t in range(NT):
                last = nc.tensor.matmul(ps[:, g, t * P:(t + 1) * P], vb[:, t, g * P:(g + 1) * P],
                                        table(second, SECOND, "ws_t")[:, g * P:(g + 1) * P], start=True, stop=True)
            last.then_inc(sgu_ready, 1)
        pe.wait_ge(a_ready, 1)
        pe.wait_ge(floor_exp, 1)
        for n, rows_of in enumerate((la, floor_m)):
            for t in range(NT):
                last = nc.tensor.transpose(ps[:, 6, n * 256 + t * 64:n * 256 + (t + 1) * 64], rows_of[:, t * P:(t + 1) * P],
                                           ident[0:64, 0:64])
        last.then_inc(a_turned, 1)

        def row(h, d):
            if 2 * h + d:
                pe.wait_ge(row_out, 2 * h + d)
            nc.tensor.matmul(ps[:, 7, :], ident[0:64, 32 * d + h:32 * d + h + 1].to_broadcast([64, P]), neg_m[:, :],
                             start=True, stop=True).then_inc(row_wide, 1)

        def turn_head(h):
            pe.wait_ge(head_scaled, h + 1)
            if h:
                pe.wait_ge(mix_ready, 12 + h)
            for t in range(NT):
                last = nc.tensor.transpose(ps[:, 6, t * P:(t + 1) * P], part[:, 0, t * P:(t + 1) * P], ident)
            last.then_inc(head_turned, 1)

        row(0, 0)
        row(0, 1)
        pe.wait_ge(sgu_read, 4)
        for h in range(4):
            def ml_values(m, kt, d):
                pe.wait_ge(ml_p, 8 * h + m + 1)
                begins = kt == (0 if d == 0 else 3)
                for t in range(kt, NT) if d == 0 else range(kt + 1):
                    last = nc.tensor.matmul(ps[:, 2 * d + t // 2, t % 2 * 129:t % 2 * 129 + 129],
                                            weights[:, m % 4, t * P:(t + 1) * P], av[:, kt, h, :],
                                            start=begins and t % 2 == 0, stop=kt == 2, skip_group_check=True)
                last.then_inc(ml_pv, 1)

            def ml_scores(n, kt):
                if 4 * h + n >= 2:
                    pe.wait_ge(ml_p, 8 * h + 2 * n - 2)
                at = slice(kt * P, (kt + 1) * P)
                product(ps[:, 4 + n % 2, :], (aq_hi[:, 4 + h, at], aq_lo[:, 4 + h, at]), (aq_hi[:, h, :], aq_lo[:, h, :]),
                        True, True).then_inc(ml_s, 1)

            ml_scores(0, 0)
            ml_scores(1, 3)
            if h < 3:
                row(h + 1, 0)
            if h:
                pe.wait_ge(ml_o, h)
            ml_values(0, 0, 0)
            ml_scores(2, 1)
            ml_values(3, 3, 1)
            ml_values(1, 0, 1)
            ml_scores(3, 2)
            ml_values(2, 3, 0)
            if h:
                turn_head(h - 1)
            if h < 3:
                row(h + 1, 1)
            ml_values(4, 1, 0)
            ml_values(5, 1, 1)
            ml_values(6, 2, 0)
            ml_values(7, 2, 1)
        turn_head(3)

        pe.wait_ge(ml_o, 4)
        dense_run(OUT2, KD, ready=mix_ready, base=12, most=16)

        def feed_forward(panel, base, hidden, name):
            norm(name)
            dense_run(panel, 8, ready=n_lo, base=SPLITS_BEFORE[name])
            down(pe, dense, panel + 8, 8, hidden)
            with pe.Fori(0, FF_CHUNKS - 1) as c:
                with pe.Fori(0, 2) as j:
                    for n in range(4):
                        dense(panel + 16 + n, c * 4 + j)
                for k in range(4):
                    down_tile(pe, dense, panel + 24 + k, c * 4, 8, hidden + 8 if k == 0 else None, c)
                for k in range(4):
                    down_tile(pe, dense, panel + 28 + k, c * 4, 8, None, None)

        feed_forward(FF1, 0, sum(FF0_CHUNKS), "ffn1")

        norm("c")
        for panel in range(C_IN, MLA_V):
            dense(panel, **(dict(ready=n_lo, base=SPLITS_BEFORE["c"]) if panel == C_IN else {}))
        norm("ckv")
        norm("cq")
        pe.wait_ge(n_lo, SPLITS_BEFORE["ckv"] + 2)
        pe.wait_ge(w_lo_ready, MLA_V + 2)
        pe.wait_ge(tile_out, output_of(MLA_V))
        for j in range(8):
            t, half = j % 4, j // 4
            at = slice(t * P, (t + 1) * P)
            if j >= 4:
                pe.wait_ge(v_copied, j - 3)
            for k in range(2):
                last = product(ps[:, j % 4, :], (cq_hi[:, 3 + k, at], cq_lo[:, 3 + k, at]),
                               w(MLA_V + k, half * 512, half * 512 + 512), k == 0, k == 1)
            last.then_inc(*((v_ready, 1) if j < 7 else (panel_read, 2)))
        pe.wait_ge(v_copied, 8)
        pe.wait_ge(pool_set, 9)
        pe.wait_ge(n_lo, SPLITS_BEFORE["cq"] + 3)

        def project_q(n):
            pe.wait_ge(w_lo_ready, MLA + n + 1)
            if n:
                pe.wait_ge(k_low, n)
            for k in range(3):
                last = product(ps[:, 0, :], w(MLA + n, k * P, (k + 1) * P), (cq_hi[:, k, :], cq_lo[:, k, :]), k == 0, k == 2)
            last.then_inc(q_proj, 1)

        def project_k(n):
            pe.wait_ge(q_scaled, n + 1)
            for k in range(2):
                a = 384 + k * P
                last = product(ps[0:64, 0, :], w(MLA + n, a, a + 64), (cq_hi[:, 3 + k, :], cq_lo[:, 3 + k, :]), k == 0, k == 1)
            last.then_inc(panel_read, 1)

        mla = units[NSA_UNITS:]
        project_q(0)
        project_k(0)
        project_q(1)
        project_k(1)
        pe.wait_ge(k_low, 1)
        maxima(mla[0])
        turn(mla[0])
        for n, u in enumerate(mla):
            more = n + 1 < HEADS
            scores(u, 0)
            scores(u, 1)
            if n:
                turn_result(mla[n - 1])
            if more:
                pe.wait_ge(k_low, n + 2)
                maxima(mla[n + 1], range(0, 2))
            values(u, 0)
            scores(u, 2)
            if more:
                maxima(mla[n + 1], range(2, 4))
            values(u, 1)
            scores(u, 3)
            if n + 2 < HEADS:
                project_q(n + 2)
            values(u, 2)
            if more:
                turn(mla[n + 1])
            if n and mla[n - 1]["last"]:
                turn_pair(mla[n - 1])
            if n + 2 < HEADS:
                project_k(n + 2)
            values(u, 3)
        turn_result(mla[-1])
        turn_pair(mla[-1])

        dense_run(OUT3, KD, ready=mix_ready, base=16)
        feed_forward(FF2, 0, sum(FF0_CHUNKS) + 8 * FF_CHUNKS, "ffn2")
        norm("final")


    @block.scalar
    def _(act):
        def split(panel, i=None):
            act.wait_ge(raw_in[panel % 4], plus(16 * (panel // 4 + 1), i, 16))
            if panel >= 2:
                act.wait_ge(panel_read, plus(panel - 1, i, 4))
            nc.scalar.activation(w_hi[:, panel % 2, :], raw[:, panel % 4, :], ACT.Copy).then_inc(w_hi_ready, 1)

        def out(o, func, read, i=None, cols=S, rows=P, ready=panel_read):
            act.wait_ge(ready, plus(read, i, 4))
            if o >= 4:
                act.wait_ge(ev_used, plus(o - 3, i, 4))
            nc.scalar.activation(ev[0:rows, o % 4, 0:cols], ps[0:rows, o % 4, 0:cols], func).then_inc(tile_out, 1)

        def step(panel, func=ACT.Copy, i=None, **more):
            act.wait_ge(panel_read, plus(panel + 1, i, 4))
            split(panel + 2, i)
            out(output_of(panel), func, panel + 1, i, **more)

        def token_major(panel, func, cols):
            for c in range(4):
                split(panel + c + 2)
            for t in range(NT):
                out(output_of(panel) + t, func, panel + 4, cols=cols)

        def step_run(panel, count, func=ACT.Copy):
            with act.Fori(0, count // 4) as i:
                for j in range(4):
                    step(panel + j, func, i)

        def square(name, k, ready, value):
            m = NORM[name][1] + k
            act.wait_ge(ready, value)
            if m >= 2:
                act.wait_ge(acc_ready, m - 1)
            nc.scalar.activation(sq[:, m % 2, :], norm_source[name][:, k, :], ACT.Square).then_inc(sq_ready, 1)

        def squares(name, ready, value, each=0):
            for k in range(NORM[name][2]):
                square(name, k, ready, value + k * each)

        def step_squares(panel, name):
            for k in range(KD):
                step(panel + k)
                if k:
                    square(name, k - 1, ev_used, output_of(panel) + k)
            square(name, KD - 1, ev_used, output_of(panel) + KD)

        def highs(name):
            _, before, tiles, _, _ = NORM[name]
            for k in range(tiles):
                act.wait_ge(normed, before + k + 1)
                nc.scalar.activation(norm_split[name][0][:, k, :], tmp[:, (before + k) % 2, :], ACT.Copy).then_inc(n_hi, 1)

        act.dma_start(small[:], A["small"]).then_inc(consts_in, 16)
        act.dma_start(masks[:], A["masks"]).then_inc(consts_in, 16)
        act.dma_start(x[:], A["x"].rearrange("k p s -> p k s")).then_inc(x_in, 16)
        act.dma_start(first[:], A["first"]).then_inc(first_in, 16)

        split(0)
        split(1)
        squares("mix_pre", x_in, 16)
        highs("mix_pre")
        for panel in range(RET_Q, RET_V):
            step(panel)
        token_major(RET_V, ACT.Copy, S)
        for panel in range(RET_G, CMP_IN):
            step(panel, ACT.Silu)
        for panel in range(CMP_IN, NSA_V):
            step(panel)
        token_major(NSA_V, ACT.Copy, 256)
        step(NSA_GATE, ACT.Sigmoid, rows=32)
        for kv in range(2):
            panel, o = CMP_W1 + 4 * kv, CMP_W1 + 2 * kv
            for c in range(4):
                split(panel + c + 2)
            out(o, ACT.Gelu_apprx_tanh, panel + 4, cols=256, rows=62)
            out(o + 1, ACT.Copy, kv + 1, cols=P, ready=cmp_turned)
        split(CMP_W2 + 2)
        out(CMP_W1 + 4, ACT.Copy, CMP_W2 + 1, cols=62)
        out(CMP_W1 + 5, ACT.Copy, CMP_W2 + 1, cols=64)
        out(CMP_W1 + 6, ACT.Copy, CMP_W2 + 1, cols=64)

        act.wait_ge(ev_used, CMP_W1 + 7)
        for h in range(4):
            act.wait_ge(ret_pv, 4 * (h + 1))
            nc.scalar.activation(ev[:, h, :], ps[:, h % 2, :], ACT.Copy)
            nc.scalar.activation(tmp[:, h, :], ps[:, h % 2, :], ACT.Square).then_inc(ret_o, 1)

        def weights_of(u, kt):
            m = u["first"] + kt
            a = kt * P if u["kind"] == "causal" else 0
            act.wait_ge(s_ready, m + 1)
            if m >= 4:
                act.wait_ge(pv_done, m - 3)
            nc.scalar.activation(u["at"]["pr"][:, m % 4, a:S], ps[:, 4 + m % 2, a:S], ACT.Exp,
                                 scale=u["scale"]).then_inc(exp_done, 1)

        def result_of(u):
            n = u["n"]
            act.wait_ge(pv_done, u["first"] + u["tiles"])
            if n >= 2:
                act.wait_ge(o_turned, n - 1)
            nc.scalar.activation(u["at"]["osb"][:, n % 2, :], ps[0:65, 6, :], ACT.Copy).then_inc(o_out, 1)

        def pair_high(u):
            act.wait_ge(turned, u["pair"] + 1)
            nc.scalar.activation(h_hi[:, u["k_mix"], :], ps[:, 1, :], ACT.Copy).then_inc(turned_high, 1)

        nsa = units[:NSA_UNITS]
        for n, u in enumerate(nsa):
            for kt in range(u["tiles"]):
                weights_of(u, kt)
                if kt == 0 and n:
                    result_of(nsa[n - 1])
                if kt == 0 and n and nsa[n - 1]["last"]:
                    pair_high(nsa[n - 1])
        result_of(nsa[-1])
        pair_high(nsa[-1])

        step_squares(OUT1, "mix_post")
        squares("ffn_pre", x_ready, 1, each=1)
        highs("ffn_pre")

        def hidden_high(k, slot, ready, value):
            act.wait_ge(ready, value)
            nc.scalar.activation(hid_hi[:, k, :], hid_f[:, slot, :], ACT.Copy).then_inc(hid_hi_ready, 1)

        panel, hidden = FF0, 0
        for tiles in FF0_CHUNKS:
            def pair(j, i=None, skip=False):
                a = panel + 2 * j
                step(a, i=i)
                step(a + 1, i=i)
                act.wait_ge(ev_used, plus(output_of(a) + 1, i, 4))
                if hidden + j or i is not None:
                    act.wait_ge(hid_ready, plus(hidden + j, i, 2))
                nc.scalar.activation(act_t[:], conv_t[:, 0, :], ACT.Gelu_apprx_tanh).then_inc(gelu_done, 1)
                if not skip:
                    hidden_high(plus(j - 1, i, 2), (j - 1) % 2, hid_ready, plus(hidden + j, i, 2))

            pair(0, skip=True)
            pair(1)
            with act.Fori(1, tiles // 2) as i:
                pair(0, i)
                pair(1, i)
            hidden_high(tiles - 1, 1, hid_ready, hidden + tiles)
            if panel + 2 * tiles + KD < AB_GATE:
                step_run(panel + 2 * tiles, KD)
            else:
                step_squares(panel + 2 * tiles, "ffn_post")
            panel += 2 * tiles + KD
            hidden += tiles
        squares("ab", x_ready, KD + 1, each=1)
        highs("ab")

        act.wait_ge(ev_used, output_of(AB_GATE))
        act.dma_start(second[:], A["second"]).then_inc(second_in, 16)
        step(AB_GATE)
        act.wait_ge(gate_raw, 2)
        nc.scalar.activation(gt[64:P, 1, :], gt[64:P, 0, :], ACT.Abs).then_inc(gate_abs, 1)
        act.wait_ge(gate_abs, 1)
        nc.scalar.activation(gt[64:P, 2, :], gt[64:P, 1, :], ACT.Exp, scale=-1.0).then_inc(gate_exp, 1)
        act.wait_ge(gate_exp, 1)
        nc.scalar.activation(gt[64:P, 1, :], gt[64:P, 2, :], ACT.Ln, bias=1.0).then_inc(gate_ln, 1)

        def silu(n):
            act.wait_ge(ev_used, output_of(AB_QK) + n + 1)
            if n >= 2:
                act.wait_ge(qk_low, n - 1)
            nc.scalar.activation(qk_s[:, n % 2, :], qk_c[:, n % 2, :], ACT.Silu).then_inc(qk_silu, 1)
            act.wait_ge(qk_silu, n + 1)
            nc.scalar.activation(aq_hi[:, n, :], qk_s[:, n % 2, :], ACT.Copy).then_inc(qk_high, 1)

        for n in range(8):
            step(AB_QK + n)
            act.wait_ge(tile_out, output_of(AB_QK) + n + 1)
            nc.scalar.activation(qk_c[:, n % 2, :], ev[:, (output_of(AB_QK) + n) % 4, :], ACT.Copy,
                                 scale=col("conv1", 5 * n + 2)).then_inc(qk_mid, 1)
            if n:
                silu(n - 1)
        silu(7)
        token_major(AB_V, ACT.Copy, S)
        for panel in range(AB_O, AB_VB):
            step(panel, ACT.Sigmoid)
        token_major(AB_VB, ACT.Gelu_apprx_tanh, S)
        for panel in range(AB_U, OUT2):
            step(panel, ACT.Gelu_apprx_tanh)

        act.wait_ge(scan_floor, 1)
        nc.scalar.activation(floor_m[:, :], floor_m[:, :], ACT.Exp, scale=-1.0).then_inc(floor_exp, 1)

        def row_copy(h, d):
            act.wait_ge(row_wide, 2 * h + d + 1)
            if h >= 2:
                act.wait_ge(ml_diag, 8 * h - 8)
            nc.scalar.activation(rows[:, h % 2 * 2 + d, :], ps[:, 7, :], ACT.Copy).then_inc(row_out, 1)

        def head_squares(h):
            act.wait_ge(ml_o, h + 1)
            nc.scalar.activation(head_sq[:, :], part[:, 1, :], ACT.Square).then_inc(head_square, 1)

        act.wait_ge(a_turned, 1)
        act.wait_ge(sgu_read, 4)
        row_copy(0, 0)
        row_copy(0, 1)
        for h in range(4):
            for n, kt in enumerate((0, 3, 1, 2)):
                for d in range(2):
                    m = 8 * h + 2 * n + d
                    at = slice(kt * P, (kt + 1) * P)
                    rest = slice((kt + 1) * P, S) if d == 0 else slice(0, kt * P)
                    bias = a_t[:, 0, kt, 32 * d + h:32 * d + h + 1]
                    act.wait_ge(ml_diag, m + 1)
                    if m >= 2:
                        act.wait_ge(ml_p, m - 1)
                    last = nc.scalar.activation(decays[:, m % 2, at], diag[:, m % 2, :], ACT.Exp, bias=bias)
                    if rest.start < rest.stop:
                        last = nc.scalar.activation(decays[:, m % 2, rest], rows[:, h % 2 * 2 + d, rest], ACT.Exp, bias=bias)
                    last.then_inc(ml_decay, 1)
                if n == 0 and h:
                    head_squares(h - 1)
                if n in (1, 3) and h < 3:
                    row_copy(h + 1, n // 2)
        head_squares(3)

        def feed_forward(panel, name, following):
            highs(name)

            def chunk(panel, i=None):
                o = output_of(panel)
                for k in range(8):
                    step(panel + k, ACT.Relu, i)
                    if k:
                        hidden_high(k - 1, (k - 1) % 2, ev_used, plus(o + k, i, 4))
                hidden_high(7, 1, ev_used, plus(o + 8, i, 4))

            with act.Fori(0, FF_CHUNKS - 1) as c:
                chunk(panel, c * 4)
                for k in range(8):
                    step(panel + 8 + k, ACT.Copy, c * 4)
            last = panel + 16 * (FF_CHUNKS - 1)
            chunk(last)
            step_squares(last + 8, following)

        step_squares(OUT2, "ffn1")
        feed_forward(FF1, "ffn1", "c")

        act.dma_start(pos_i[64:P, :], A["positions"]).then_inc(pos_in, 16)
        highs("c")
        for panel in range(C_IN, MLA_V):
            step(panel)
        for d in range(2):
            act.wait_ge(ang_ready, d + 1)
            nc.scalar.activation(trig[64:P, d, :], ang[64:P, 1 + d, :], ACT.Sin).then_inc(trig_ready, 1)
        squares("ckv", ev_used, output_of(MLA_V))
        highs("ckv")
        squares("cq", n_lo, SPLITS_BEFORE["cq"])
        highs("cq")
        for j in range(8):
            t, half = j % 4, j // 4
            act.wait_ge(*((v_ready, j + 1) if j < 7 else (panel_read, MLA)))
            nc.scalar.activation(mla_v[:, t, 8 * half:8 * half + 8, 0:64], ps[:, j % 4, :].rearrange("p (h d) -> p h d", h=8),
                                 ACT.Copy).then_inc(v_copied, 1)

        def q_of(n):
            act.wait_ge(q_scaled, n + 1)
            nc.scalar.activation(qf_hi[:, n % 2, :], q_f[:, :], ACT.Copy).then_inc(q_high, 1)

        def k_of(n):
            act.wait_ge(panel_read, MLA + n + 1)
            nc.scalar.activation(kf_hi[0:64, n % 2, :], ps[0:64, 0, :], ACT.Copy).then_inc(k_high, 1)
            split(MLA + n + 2)

        mla = units[NSA_UNITS:]
        split(MLA)
        split(MLA + 1)
        for n in range(2):
            q_of(n)
            k_of(n)
        for n, u in enumerate(mla):
            for kt in range(4):
                weights_of(u, kt)
                if kt == 0 and n:
                    result_of(mla[n - 1])
            if n + 2 < HEADS:
                q_of(n + 2)
            if n and mla[n - 1]["last"]:
                pair_high(mla[n - 1])
            if n + 2 < HEADS:
                k_of(n + 2)
        result_of(mla[-1])
        pair_high(mla[-1])

        step_squares(OUT3, "ffn2")
        feed_forward(FF2, "ffn2", "final")

    @block.vector
    def _(dve):
        V = nc.vector
        so_far, loop = {}, {"i": None, "each": {}}

        def signal(ins, s, n=1, wait=True):
            so_far[s] = so_far.get(s, 0) + n
            ins.then_inc(s, n)
            if wait:
                dve.wait_ge(s, plus(so_far[s], loop["i"], loop["each"].get(s, 0)))

        def link(ins):
            signal(ins, dve_step)

        def enter(i, each, first=0):
            for s, k in each.items():
                so_far[s] = so_far.get(s, 0) - k * first
            loop["i"], loop["each"], loop["start"], loop["first"] = i, each, dict(so_far), first

        def leave(turns):
            for s, k in loop["each"].items():
                assert so_far.get(s, 0) - loop["start"].get(s, 0) == k, s
                so_far[s] += k * (turns - 1 + loop["first"])
            loop["i"], loop["each"] = None, {}

        def low(panel, i=None):
            dve.wait_ge(w_hi_ready, plus(panel + 1, i, 4))
            signal(V.tensor_tensor(w_lo[:, panel % 2, :], raw[:, panel % 4, :], w_hi[:, panel % 2, :].bitcast(F32),
                            ALU.subtract), w_lo_ready, wait=False)

        def take(panel, i=None, extra=0):
            low(panel + 2, i)
            o = output_of(panel)
            dve.wait_ge(tile_out, plus(o + 1, i, 4))
            return ev[:, o % 4, :]

        def take_four(panel):
            for c in range(4):
                low(panel + c + 2)
            for t in range(NT):
                dve.wait_ge(tile_out, output_of(panel) + t + 1)
                yield t, ev[:, (output_of(panel) + t) % 4, :]

        def used(ins):
            signal(ins, ev_used)

        def parts(hi, lo, src):
            link(V.tensor_copy(hi, src))
            return V.tensor_tensor(lo, src, hi.bitcast(F32), ALU.subtract)

        def wide(t4, n=P):
            return t4.unsqueeze(2).to_broadcast([t4.shape[0], 4, n])

        def fours(t):
            return t.rearrange("p (a b) -> p a b", a=4)

        def rope(src, dst, c, s, swapped):
            link(V.stream_shuffle(swapped, src, HALF_SWAP))
            link(V.tensor_tensor(swapped, swapped, s, ALU.mult))
            link(V.tensor_tensor(dst, src, c, ALU.mult))
            link(V.tensor_tensor(dst, dst, swapped, ALU.add))

        def accumulate(name, k):
            m = NORM[name][1] + k
            dve.wait_ge(sq_ready, m + 1)
            if k == 0:
                signal(V.tensor_copy(tmp[:, 2, :], sq[:, m % 2, :]), acc_ready, wait=False)
            else:
                dve.wait_ge(acc_ready, m)
                signal(V.tensor_tensor(tmp[:, 2, :], tmp[:, 2, :], sq[:, m % 2, :], ALU.add), acc_ready, wait=False)

        def inverse(name, gathered=False):
            n, before, tiles, width, eps = NORM[name]
            if not gathered:
                for k in range(tiles):
                    accumulate(name, k)
            dve.wait_ge(ss_ready, n + 1)
            signal(V.tensor_scalar(r4[:, 0, :], ps[:, 6, 0:4], 1.0 / width, eps, ALU.mult, ALU.add), ms_ready)
            dve.wait_ge(inv_ready, n + 1)
            signal(V.tensor_tensor(fours(tmp[:, 3, :]), ident.unsqueeze(1).to_broadcast([P, 4, P]), wide(r4[:, 1, :]),
                            ALU.mult), inv_diag)
            dve.wait_ge(inv_wide, n + 1)

        def scaled(name, k, gain, out=None, wait=True):
            m = NORM[name][1] + k
            out = tmp[:, m % 2, :] if out is None else out
            signal(V.scalar_tensor_tensor(out, norm_source[name][:, k, :], gain, ps[:, 7, :], ALU.mult, ALU.mult), normed,
                   wait=wait)

        def norm_split_of(name, gathered=False):
            _, before, tiles, _, _ = NORM[name]
            inverse(name, gathered)
            hi, lo = norm_split[name]
            at = SPLITS_BEFORE[name]

            def lower(k):
                dve.wait_ge(n_hi, at + k + 1)
                signal(V.tensor_tensor(lo[:, k, :], tmp[:, (before + k) % 2, :], hi[:, k, :].bitcast(F32), ALU.subtract), n_lo)

            for k in range(tiles):
                scaled(name, k, col(norm_gain[name], k), wait=False)
                if k:
                    lower(k - 1)
            lower(tiles - 1)

        def norm_add(name, following, added):
            inverse(name, gathered=True)
            for k in range(KD):
                if k >= 2:
                    dve.wait_ge(x_ready, added + k - 1)
                scaled(name, k, col(norm_gain[name], k), wait=False)
                if k >= 2:
                    accumulate(following, k - 2)
            accumulate(following, KD - 2)
            accumulate(following, KD - 1)
            dve.wait_ge(x_ready, added + KD)

        def take_run(panel, n, each):
            with dve.Fori(0, n // 4) as i:
                enter(i, {ev_used: 4, w_lo_ready: 4})
                for j in range(4):
                    each(j, i, take(panel + j, i))
                leave(n // 4)

        def take_squares(panel, name, each):
            for k in range(KD):
                each(k, None, take(panel + k))
                if k:
                    accumulate(name, k - 1)
            accumulate(name, KD - 1)

        dve.wait_ge(consts_in, 32)
        low(0)
        low(1)
        dve.wait_ge(x_in, 16)
        norm_split_of("mix_pre")
        dve.wait_ge(first_in, 16)
        c64, s64 = table(first, FIRST, "rope_c"), table(first, FIRST, "rope_s")

        def rope_parts(src, hi, lo):
            rope(src, tmp[:, 2, :], c64, s64, tmp[:, 3, :])
            used(parts(hi, lo, tmp[:, 2, :]))

        for panel in range(RET_Q, RET_V):
            t = panel % 2
            hi, lo = (rq_hi, rq_lo) if panel < RET_K else (rk_hi, rk_lo)
            rope_parts(take(panel), hi[:, t, :], lo[:, t, :])
        for t, src in take_four(RET_V):
            link(V.tensor_reduce(r4[:, 4, :], fours(src), AX.X, ALU.add))
            link(V.tensor_scalar(r4[:, 5, :], r4[:, 4, :], -1.0 / P, None, ALU.mult))
            used(V.tensor_tensor(fours(rv[:, t, :]), fours(src), wide(r4[:, 5, :]), ALU.add))
        for t in range(4):
            used(V.tensor_copy(rg[:, t, :], take(RET_G + t)))
        for kv in range(2):
            src = take(CMP_IN + kv)
            if kv:
                dve.wait_ge(cmp_in_ready, 1)
            for g in range(2):
                for odd in range(2):
                    r = slice(64 * odd, 64 * odd + 64)
                    by_block = src[64 * g:64 * g + 64, :].rearrange("p (n i two) -> p i n two", i=8, two=2)
                    for later in range(2):
                        out = xg_f[r, 8 * later:8 * later + 8, 31 * g:31 * g + 31]
                        pos = small[64 * g:64 * g + 64, SMALL["cmp_pos"][0]:SMALL["cmp_pos"][0] + 64]
                        pos = pos.rearrange("p (kv two i) -> p kv two i", kv=2, two=2)[:, kv, odd, 8 * later:8 * later + 8]
                        last = V.tensor_tensor(out, by_block[:, :, later:later + 31, odd],
                                               pos.unsqueeze(2).to_broadcast([64, 8, 31]), ALU.add)
            used(last)
            dve.wait_ge(ev_used, output_of(CMP_IN + kv) + 1)
            signal(parts(xg_hi[:, kv, :, :], xg_lo[:, kv, :, :], xg_f[:, :, :]), cmp_in_ready)
        for t in range(4):
            rope_parts(take(NSA_Q + t), nq_hi[:, t, :], nq_lo[:, t, :])
        for t in range(2):
            rope_parts(take(NSA_K + t), nk_hi[:, t, :], nk_lo[:, t, :])
        dve.wait_ge(pool_set, 7)
        for t, src in take_four(NSA_V):
            by = src[:, 0:256].rearrange("p (s g d) -> p s g d", s=2, g=2)
            used(V.tensor_copy(nv[:, t, :, :, 0:64], by))
        take(NSA_GATE)
        dve.wait_ge(gates_turned, 1)
        used(V.tensor_copy(gates[:, :, :], fours(ps[:, 6, 0:P])))
        for kv in range(2):
            panel, o = CMP_W1 + 4 * kv, CMP_W1 + 2 * kv
            for c in range(4):
                low(panel + c + 2)
            dve.wait_ge(tile_out, o + 2)
            src = ev[:, (o + 1) % 4, 0:P].rearrange("p (m c) -> p m c", m=2)[:, :, 0:62]
            if kv == 0:
                used(V.tensor_copy(ch_hi[:, :, 0:62], src))
                used(V.tensor_tensor(ch_lo[:, :, 0:62], src, ch_hi[:, :, 0:62].bitcast(F32), ALU.subtract))
            else:
                by = src.rearrange("p m (g n) -> p m g n", g=2)
                for m in range(2):
                    link(V.tensor_copy(cv_hi[:, m, :, 0:31], by[:, m]))
                    used(V.tensor_tensor(cv_lo[:, m, :, 0:31], by[:, m], cv_hi[:, m, :, 0:31].bitcast(F32), ALU.subtract))
            dve.wait_ge(ev_used, o + 2)
        low(CMP_W2 + 2)
        dve.wait_ge(tile_out, CMP_W1 + 5)
        src = ev[:, (CMP_W1 + 4) % 4, :]
        V.tensor_copy(kc_f[0:64, 0, 0:31], src[0:64, 0:31])
        used(V.tensor_copy(kc_f[64:P, 0, 0:31], src[64:P, 31:62]))
        dve.wait_ge(ev_used, CMP_W1 + 5)
        rope(kc_f[:, 0, 0:31], kc_f[:, 1, 0:31], table(first, FIRST, "cmp_c")[:, 0:31],
             table(first, FIRST, "cmp_s")[:, 0:31], kc_f[:, 2, 0:31])
        signal(parts(kc_hi[:, 0:31], kc_lo[:, 0:31], kc_f[:, 1, 0:31]), cmp_ready)
        for g in range(2):
            dve.wait_ge(tile_out, CMP_W1 + 6 + g)
            used(V.tensor_copy(vc[:, g, 0:64], ev[:, (CMP_W1 + 5 + g) % 4, 0:64]))
            dve.wait_ge(ev_used, CMP_W1 + 6 + g)
            signal(V.memset(r4[:, 2, 0:1], 0.0), cmp_ready)

        decay = table(first, FIRST, "decay")
        for h in range(4):
            for kt in range(NT):
                m = 4 * h + kt
                dve.wait_ge(ret_s, m + 1)
                if m >= 4:
                    dve.wait_ge(ret_pv, m - 3)
                signal(V.tensor_tensor(at1["pr"][:, m % 4, kt * P:S], ps[:, 4 + m % 2, kt * P:S],
                                decay[:, 512 * h:512 * h + S - kt * P], ALU.mult), ret_p)

        def ret_diagonal(h):
            dve.wait_ge(ret_inv, 1)
            signal(V.tensor_tensor(fours(tmp[:, 3, :]), ident.unsqueeze(1).to_broadcast([P, 4, P]),
                                   wide(ret16[:, 1, 4 * h:4 * h + 4]), ALU.mult), ret_diag, wait=False)

        def ret_finish(h):
            t = tmp[:, 0, :]
            dve.wait_ge(ret_wide, h + 1)
            link(V.scalar_tensor_tensor(t, ev[:, h, :], col("gn", h), ps[:, 0, :], ALU.mult, ALU.mult))
            link(V.tensor_tensor(t, t, rg[:, h, :], ALU.mult))
            signal(parts(h_hi[:, h, :], h_lo[:, h, :], t), mix_ready)

        def largest(u, tiles=range(NT)):
            n, at = u["n"], u["at"]
            if u["kind"] == "cmp":
                if tiles.start == 0:
                    dve.wait_ge(mx_ready, 4 * n + 4)
                    signal(V.tensor_reduce(at["mx"][:, n % 2, :], ps[:, 2, 0:P].rearrange("p (a b) -> p a b", a=4), AX.X,
                                           ALU.max), mx_done, 4, wait=False)
            else:
                for t in tiles:
                    keys = (t + 1) * P if u["kind"] == "causal" else S
                    dve.wait_ge(mx_ready, 4 * n + t + 1)
                    signal(V.tensor_reduce(at["mx"][:, n % 2, t:t + 1], ps[:, 2 + t % 2, 0:keys], AX.X, ALU.max), mx_done,
                           wait=False)
            if tiles.stop < NT:
                return
            dve.wait_ge(mx_done, 4 * n + 4)
            signal(V.tensor_scalar(at["negm"][:, n % 2, :], at["mx"][:, n % 2, :], -1e20, -1.0, ALU.max, ALU.mult), negm_ready,
                   wait=False)

        def shift_of(u):
            n = u["n"]
            dve.wait_ge(negm_turned, n + 1)
            signal(V.tensor_tensor(fours(u["at"]["shift"][:, n % 2, :]),
                                   ps[0:4, 7, 384:512].unsqueeze(1).to_broadcast([4, 4, P]),
                                   ident[0:4, 0:4].unsqueeze(2).to_broadcast([4, 4, P]), ALU.mult), shift_ready, wait=False)

        def result(u):
            n, at = u["n"], u["at"]
            dve.wait_ge(o_turned, n + 1)
            if u["pair"] % 4 >= 2 and u["half"] == 0 and u["s"] == 0:
                dve.wait_ge(turned, u["pair"] - 1)
            by = ps[:, 7, 0:NT * 65].rearrange("p (t d) -> p t d", t=NT)
            w4 = at["w4"][:].unsqueeze(2)
            if u["gate"] is None:
                link(V.reciprocal(w4, by[:, :, 64:65]))
            else:
                link(V.tensor_scalar(w4, by[:, :, 64:65], 1e-30, None, ALU.max))
                link(V.reciprocal(at["w4"][:], at["w4"][:]))
                link(V.tensor_tensor(at["w4"][:], at["w4"][:], gates[:, :, u["gate"]], ALU.mult))
            total = at["by_token"][:, u["pair"] % 2, :, 64 * u["half"]:64 * u["half"] + 64]
            if u["s"] == 0:
                signal(V.tensor_tensor(total, by[:, :, 0:64], wide(at["w4"][:], 64), ALU.mult), o_used)
            else:
                link(V.tensor_tensor(at["term"][:], by[:, :, 0:64], wide(at["w4"][:], 64), ALU.mult))
                signal(V.tensor_tensor(total, total, at["term"][:], ALU.add), o_used)

        def pair_low(u):
            dve.wait_ge(turned_high, u["pair"] + 1)
            k = u["k_mix"]
            signal(V.tensor_tensor(h_lo[:, k, :], ps[:, 1, :], h_hi[:, k, :].bitcast(F32), ALU.subtract), mix_ready, wait=False)

        nsa = units[:NSA_UNITS]
        largest(nsa[0])
        largest(nsa[1])
        shift_of(nsa[0])
        dve.wait_ge(ret_sum, 1)
        signal(V.tensor_scalar(ret16[:, 0, :], ps[:, 0, 0:16], 1.0 / P, 1e-5, ALU.mult, ALU.add), ret_ms)
        for n, u in enumerate(nsa):
            if n:
                result(nsa[n - 1])
            if n + 2 < NSA_UNITS:
                largest(nsa[n + 2], range(0, 2))
            if n + 1 < NSA_UNITS:
                shift_of(nsa[n + 1])
            if n and nsa[n - 1]["last"]:
                pair_low(nsa[n - 1])
            if 1 <= n <= 4:
                ret_finish(n - 1)
            if n + 2 < NSA_UNITS:
                largest(nsa[n + 2], range(2, 4))
            if n < 4:
                ret_diagonal(n)
        result(nsa[-1])
        pair_low(nsa[-1])

        take_squares(OUT1, "mix_post", lambda k, i, src: used(V.tensor_copy(y[:, k, :], src)))
        norm_add("mix_post", "ffn_pre", 0)
        norm_split_of("ffn_pre", gathered=True)
        conv0 = SMALL["conv0"][0]

        def hidden_low(k, slot, value):
            dve.wait_ge(hid_hi_ready, value)
            signal(V.tensor_tensor(hid_lo[:, k, :], hid_f[:, slot, :], hid_hi[:, k, :].bitcast(F32), ALU.subtract), hid_lo_ready)

        panel, hidden = FF0, 0
        for c, tiles in enumerate(FF0_CHUNKS):
            def pair(j, i=None, skip=False):
                q = hidden + j
                for side in range(2):
                    src = take(panel + 2 * j + side, i)
                    t = conv_t[:, side, :]

                    def tap(n):
                        at = plus(conv0 + (2 * q + side) * 3 + n, i, 12)
                        return small[:, at:at + 1] if i is None else small[:, bass.ds(at, 1)]

                    link(V.tensor_scalar(t, src, tap(2), None, ALU.mult))
                    link(V.scalar_tensor_tensor(t[:, 1:S], src[:, 0:S - 1], tap(1), t[:, 1:S], ALU.mult, ALU.add))
                    used(V.scalar_tensor_tensor(t[:, 2:S], src[:, 0:S - 2], tap(0), t[:, 2:S], ALU.mult, ALU.add))
                    dve.wait_ge(ev_used, plus(output_of(panel) + 2 * j + side + 1, i, 4))
                dve.wait_ge(gelu_done, plus(q + 1, i, 2))
                signal(V.tensor_tensor(hid_f[:, j % 2, :], act_t[:], conv_t[:, 1, :], ALU.mult), hid_ready)
                if not skip:
                    hidden_low(plus(j - 1, i, 2), (j - 1) % 2, plus(q, i, 2))

            pair(0, skip=True)
            pair(1)
            with dve.Fori(1, tiles // 2) as i:
                enter(i, {ev_used: 4, w_lo_ready: 4, dve_step: 4 * 2, hid_ready: 2, hid_lo_ready: 2}, first=1)
                pair(0, i)
                pair(1, i)
                leave(tiles // 2 - 1)
            hidden_low(tiles - 1, 1, hidden + tiles)
            down_panel = panel + 2 * tiles

            def gather(j, i, src):
                k = plus(j, i, 4)
                if c == 0:
                    used(V.tensor_copy(y[:, k, :], src))
                else:
                    used(V.tensor_tensor(y[:, k, :], y[:, k, :], src, ALU.add))

            if down_panel + KD < AB_GATE:
                take_run(down_panel, KD, gather)
            else:
                take_squares(down_panel, "ffn_post", gather)
            panel += 2 * tiles + KD
            hidden += tiles
        norm_add("ffn_post", "ab", KD)
        norm_split_of("ab", gathered=True)

        src = take(AB_GATE)
        signal(V.tensor_scalar(gt[:, 0, :], src, col("gate_b"), None, ALU.add), gate_raw)
        dve.wait_ge(gate_raw, 1)
        used(V.tensor_scalar(li[:, :], src[0:64, :], col("gate_b")[0:64, :], None, ALU.add))
        dve.wait_ge(ev_used, output_of(AB_GATE) + 1)
        signal(V.memset(r4[:, 2, 0:1], 0.0), gate_raw)
        link(V.memset(scan[:, :, :], 0.0))
        dve.wait_ge(gate_ln, 1)
        mid = slice(256, 768)
        link(V.scalar_tensor_tensor(scan[:, 0, mid], gt[64:P, 0, :], 0.0, gt[64:P, 1, :], ALU.min, ALU.subtract))

        def scan_step(k):
            if k == 9:
                link(V.tensor_copy(neg_m[:, :], scan[:, 1, mid]))
                signal(V.tensor_tensor(la[:, :], li[:, :], neg_m[:, :], ALU.subtract), a_ready)
                link(V.memset(scan[:, :, :], NEG))
                link(V.tensor_copy(scan[:, 0, mid], la[:, :]))
            n, op = k % 9, ALU.add if k < 9 else ALU.max
            a, b = n % 2, 1 - n % 2
            V.tensor_tensor(scan[0:32, b, mid], scan[0:32, a, mid], scan[0:32, a, 256 - 2 ** n:768 - 2 ** n], op)
            link(V.tensor_tensor(scan[32:64, b, mid], scan[32:64, a, mid], scan[32:64, a, 256 + 2 ** n:768 + 2 ** n], op))

        conv1 = SMALL["conv1"][0]

        def qk_lower(n):
            dve.wait_ge(qk_high, n + 1)
            signal(V.tensor_tensor(aq_lo[:, n, :], qk_s[:, n % 2, :], aq_hi[:, n, :].bitcast(F32), ALU.subtract), qk_low,
                   wait=False)

        for n in range(8):
            src = take(AB_QK + n)
            t = qk_c[:, n % 2, :]

            def add_tap(k, a, b):
                return V.scalar_tensor_tensor(t[:, a:b], src[:, a + k - 2:b + k - 2], col("conv1", 5 * n + k), t[:, a:b],
                                              ALU.mult, ALU.add)

            dve.wait_ge(qk_mid, n + 1)
            link(add_tap(1, 1, S))
            link(add_tap(0, 2, S))
            link(add_tap(3, 0, S - 1))
            used(add_tap(4, 0, S - 2))
            if n:
                qk_lower(n - 1)
        qk_lower(7)
        for c in range(4):
            low(AB_V + c + 2)
            scan_step(2 * c)
            scan_step(2 * c + 1)
        for t in range(NT):
            dve.wait_ge(tile_out, output_of(AB_V) + t + 1)
            used(V.tensor_copy(av[:, t, :, 0:P], fours(ev[:, (output_of(AB_V) + t) % 4, :])))
        link(V.memset(av[:, :, :, 128:129], 1.0))
        for t in range(4):
            used(V.tensor_copy(ao[:, t, :], take(AB_O + t)))
            for k in range(3 if t < 2 else 2):
                scan_step(8 + (3 * t if t < 2 else 2 * t + 2) + k)
        link(V.tensor_scalar(scan[:, 0, mid], scan[:, 1, mid], 0.0, None, ALU.max))
        link(V.tensor_tensor(floor_m[:, :], neg_m[:, :], scan[:, 0, mid], ALU.add))
        signal(V.tensor_scalar(neg_m[:, :], scan[:, 0, mid], -1.0, None, ALU.mult), scan_floor)
        dve.wait_ge(second_in, 16)
        for t, src in take_four(AB_VB):
            link(V.tensor_tensor(tmp[:, 2, :], src, src, ALU.mult))
            link(V.tensor_reduce(r4[:, 4, :], fours(tmp[:, 2, :]), AX.X, ALU.add))
            signal(V.tensor_scalar(r4[:, 2, :], r4[:, 4, :], 1.0 / P, 1e-6, ALU.mult, ALU.add), vb_ms)
            dve.wait_ge(vb_inv, t + 1)
            link(V.tensor_tensor(fours(tmp[:, 3, :]), fours(src), wide(r4[:, 3, :]), ALU.mult))
            used(V.tensor_tensor(vb[:, t, :], tmp[:, 3, :], table(second, SECOND, "g_v"), ALU.mult))

        def gt_u(g):
            return gt[:, g, :] if g < 3 else qk_c[:, 0, :]

        for g in range(4):
            used(V.tensor_copy(gt_u(g), take(AB_U + g)))
        for g in range(4):
            dve.wait_ge(sgu_ready, g + 1)
            b = table(second, SECOND, "sgu_b")[:, g * P:(g + 1) * P].unsqueeze(1).to_broadcast([P, 4, P])
            signal(V.tensor_tensor(fours(tmp[:, 2, :]), fours(ps[:, g, :]), b, ALU.add), sgu_read)
            dve.wait_ge(sgu_read, g + 1)
            link(V.tensor_tensor(tmp[:, 2, :], tmp[:, 2, :], gt_u(g), ALU.mult))
            link(parts(h_hi[:, 4 + g, :], h_lo[:, 4 + g, :], tmp[:, 2, :]))
            signal(V.memset(r4[:, 2, 0:1], 0.0), mix_ready)
        dve.wait_ge(a_turned, 1)
        link(V.tensor_copy(a_t[:, :, :, :], ps[:, 6, :].rearrange("p (n a b) -> p n a b", n=2, a=4)))

        def weigh(h, n, kt):
            at = slice(kt * P, (kt + 1) * P)
            for d in range(2):
                m = 8 * h + 2 * n + d
                dve.wait_ge(row_out, 2 * h + d + 1)
                if m >= 2:
                    dve.wait_ge(ml_decay, m - 1)
                signal(V.tensor_tensor(diag[:, m % 2, :], rows[:, h % 2 * 2 + d, at], mask("k_q" if d == 0 else "q_k"), ALU.add),
                       ml_diag, wait=False)
            dve.wait_ge(ml_s, 4 * h + n + 1)
            for d in range(2):
                m = 8 * h + 2 * n + d
                a, b = (kt * P, S) if d == 0 else (0, (kt + 1) * P)
                dve.wait_ge(ml_decay, m + 1)
                if m >= 4:
                    dve.wait_ge(ml_pv, m // 4 * 4)
                signal(V.scalar_tensor_tensor(weights[:, m % 4, a:b], ps[:, 4 + n % 2, a:b], P ** -0.5, decays[:, m % 2, a:b],
                                              ALU.mult, ALU.mult), ml_p, wait=False)

        def combine(h):
            dve.wait_ge(ml_pv, 8 * h + 8)
            for d in range(2):
                out = ps[:, 2 * d:2 * d + 2, 0:258].rearrange("p b (t e) -> p b t e", e=129)
                total = out[:, :, :, 128]
                floor = a_t[:, 1, :, 32 * d + h].rearrange("p (b t) -> p b t", b=2)
                w = den[:, d, :].rearrange("p (b t) -> p b t", b=2)
                link(V.tensor_tensor(w, total, floor, ALU.max))
                link(V.scalar_tensor_tensor(w, total, -1.0, w, ALU.mult, ALU.max))
                link(V.reciprocal(den[:, d, :], den[:, d, :]))
                for b in range(2):
                    link(V.tensor_tensor(part[:, d, b * 256:(b + 1) * 256].rearrange("p (t e) -> p t e", t=2),
                                         out[:, b, :, 0:P], w[:, b, :].unsqueeze(2).to_broadcast([P, 2, P]), ALU.mult))
            signal(V.tensor_tensor(part[:, 1, :], part[:, 1, :], part[:, 0, :], ALU.add), ml_o)

        def head_mean(h):
            dve.wait_ge(head_square, h + 1)
            link(V.tensor_reduce(r4[:, 4, :], fours(head_sq[:, :]), AX.X, ALU.add))
            signal(V.tensor_scalar(r4[:, 4, :], r4[:, 4, :], 1.0 / P, 1e-6, ALU.mult, ALU.add), head_ms, wait=False)

        def head_scale(h):
            dve.wait_ge(head_inv, h + 1)
            signal(V.tensor_tensor(fours(part[:, 0, :]), fours(part[:, 1, :]), wide(r4[:, 5, :]), ALU.mult), head_scaled)

        def head_finish(h):
            dve.wait_ge(head_turned, h + 1)
            t = tmp[:, 2, :]
            link(V.scalar_tensor_tensor(t, ps[:, 6, :], col("g_head", h), ao[:, h, :], ALU.mult, ALU.mult))
            signal(parts(h_hi[:, h, :], h_lo[:, h, :], t), mix_ready)

        for h in range(4):
            weigh(h, 0, 0)
            if h:
                head_mean(h - 1)
            weigh(h, 1, 3)
            if h:
                head_scale(h - 1)
            weigh(h, 2, 1)
            if h:
                head_finish(h - 1)
            weigh(h, 3, 2)
            combine(h)
        head_mean(3)
        head_scale(3)
        head_finish(3)

        def add_to_x(j, i, src):
            used(V.tensor_tensor(x[:, plus(j, i, 4), :], x[:, plus(j, i, 4), :], src, ALU.add))

        def feed_forward(panel, name, hidden, following):
            norm_split_of(name, gathered=True)

            def chunk(panel, hidden, c=None):
                i = None if c is None else c * 4
                for k in range(8):
                    src = take(panel + k, i)
                    used(V.tensor_tensor(hid_f[:, k % 2, :], src, src, ALU.mult))
                    if k:
                        hidden_low(k - 1, (k - 1) % 2, plus(hidden + k, c, 8))
                hidden_low(7, 1, plus(hidden + 8, c, 8))

            with dve.Fori(0, FF_CHUNKS - 1) as c:
                enter(c, {ev_used: 16, w_lo_ready: 16, hid_lo_ready: 8})
                chunk(panel, hidden, c)
                for k in range(8):
                    src = take(panel + 8 + k, c * 4)
                    used(V.tensor_tensor(x[:, k, :], x[:, k, :], src, ALU.add))
                leave(FF_CHUNKS - 1)
            last = panel + 16 * (FF_CHUNKS - 1)
            chunk(last, hidden + 8 * (FF_CHUNKS - 1))
            take_squares(last + 8, following, add_to_x)

        take_squares(OUT2, "ffn1", add_to_x)
        feed_forward(FF1, "ffn1", sum(FF0_CHUNKS), "c")

        norm_split_of("c", gathered=True)
        rr = slice(64, P)
        dve.wait_ge(pos_in, 16)
        TWO_PI, MAGIC = 2 * np.pi, 1.5 * 2.0 ** 23
        C1, C2 = 6.28125, 0.0019350051879882812
        C3 = TWO_PI - C1 - C2
        link(V.tensor_copy(ang[rr, 2, :], pos_i[rr, :]))
        link(V.tensor_scalar(ang[rr, 0, :], ang[rr, 2, :], col("freq")[rr, :], None, ALU.mult))
        for d in range(2):
            quarter = 0.25 * (1 - d)
            k, r = c_raw[rr, 0, :], ang[rr, 1 + d, :]
            link(V.tensor_scalar(k, ang[rr, 0, :], 1 / TWO_PI, quarter, ALU.mult, ALU.add))
            link(V.tensor_scalar(k, k, MAGIC, None, ALU.add))
            link(V.tensor_scalar(k, k, MAGIC, None, ALU.subtract))
            link(V.scalar_tensor_tensor(r, k, -C1, ang[rr, 0, :], ALU.mult, ALU.add))
            link(V.scalar_tensor_tensor(r, k, -C2, r, ALU.mult, ALU.add))
            link(V.scalar_tensor_tensor(r, k, -C3, r, ALU.mult, ALU.add))
            link(V.tensor_scalar(r, r, quarter * TWO_PI, None, ALU.add))
            signal(V.tensor_scalar(r, r, 3.1415925, -3.1415925, ALU.min, ALU.max), ang_ready)
            dve.wait_ge(ang_ready, d + 1)
        for k in range(5):
            used(V.tensor_copy(c_raw[:, k, :], take(C_IN + k)))
        src = take(C_IN + 5)
        dve.wait_ge(trig_ready, 2)
        link(V.tensor_scalar(trig[rr, 1, :], trig[rr, 1, :], col("rope_sign")[rr, :], None, ALU.mult))
        rope(src[rr, :], ang[rr, 0, :], trig[rr, 0, :], trig[rr, 1, :], ang[rr, 1, :])
        link(V.tensor_copy(q_turn[64:96, :], trig[64:96, 0, :]))
        link(V.tensor_copy(q_turn[96:P, :], trig[96:P, 1, :]))
        link(V.tensor_copy(kf_hi[rr, 0, :], ang[rr, 0, :]))
        link(V.tensor_tensor(kf_lo[rr, 0, :], ang[rr, 0, :], kf_hi[rr, 0, :].bitcast(F32), ALU.subtract))
        link(V.tensor_copy(kf_hi[rr, 1, :], kf_hi[rr, 0, :]))
        used(V.tensor_copy(kf_lo[rr, 1, :], kf_lo[rr, 0, :]))
        dve.wait_ge(ev_used, output_of(MLA_V))
        norm_split_of("ckv")
        norm_split_of("cq")
        dve.wait_ge(pool_set, 9)

        def q_scale(n):
            dve.wait_ge(q_proj, n + 1)
            if n:
                dve.wait_ge(q_low, n)
            signal(V.tensor_tensor(q_f[:, :], ps[:, 0, :], q_turn[:, :], ALU.mult), q_scaled, wait=False)

        def q_lower(n):
            dve.wait_ge(q_high, n + 1)
            signal(V.tensor_tensor(qf_lo[:, n % 2, :], q_f[:, :], qf_hi[:, n % 2, :].bitcast(F32), ALU.subtract), q_low,
                   wait=False)

        def k_lower(n):
            dve.wait_ge(k_high, n + 1)
            dve.wait_ge(q_low, n + 1)
            signal(V.tensor_tensor(kf_lo[0:64, n % 2, :], ps[0:64, 0, :], kf_hi[0:64, n % 2, :].bitcast(F32), ALU.subtract),
                   k_low, wait=False)
            low(MLA + n + 2)

        mla = units[NSA_UNITS:]
        low(MLA)
        low(MLA + 1)
        for n in range(2):
            q_scale(n)
            q_lower(n)
            k_lower(n)
        largest(mla[0])
        shift_of(mla[0])
        for n, u in enumerate(mla):
            more = n + 1 < HEADS
            if n:
                result(mla[n - 1])
            if more:
                largest(mla[n + 1])
            if n + 2 < HEADS:
                q_scale(n + 2)
            if more:
                shift_of(mla[n + 1])
            if n + 2 < HEADS:
                q_lower(n + 2)
            if n and mla[n - 1]["last"]:
                pair_low(mla[n - 1])
            if n + 2 < HEADS:
                k_lower(n + 2)
        result(mla[-1])
        pair_low(mla[-1])

        take_squares(OUT3, "ffn2", add_to_x)
        feed_forward(FF2, "ffn2", sum(FF0_CHUNKS) + 8 * FF_CHUNKS, "final")
        inverse("final", gathered=True)
        for k in range(KD):
            scaled("final", k, col("g_final", k), out=y[:, k, :])


def swapped_order():
    return np.concatenate([np.arange(0, 16), np.arange(32, 48), np.arange(16, 32), np.arange(48, 64)])


def by_feature(w, cols):
    cols = np.asarray(cols)
    out = np.zeros((len(cols) // P, P, PANEL), np.float32)
    for n in range(len(cols) // P):
        c = cols[n * P:(n + 1) * P]
        block = np.zeros((w.shape[0], P), np.float32)
        block[:, c >= 0] = w[:, c[c >= 0]]
        kt = w.shape[0] // P
        out[n, :, :kt * P] = block.reshape(kt, P, P).transpose(1, 0, 2).reshape(P, kt * P)
    return out


def by_token(w, width):
    out = np.zeros((4, P, 2, 512), np.float32)
    out[:, :, :, :width] = w.reshape(4, 2, P, width).transpose(0, 2, 1, 3)
    return out.reshape(4, P, PANEL)


def lay_panels(a):
    order = swapped_order()
    w = a["w_in"][0]
    heads = lambda at, hs: np.concatenate([at + 64 * h + order for h in hs])
    out = [by_feature(w, heads(0, range(4))), by_feature(w, heads(256, range(4))), by_token(w[:, 512:1024], 512),
           by_feature(w, np.arange(1024, 1536)), by_feature(w, np.arange(2048, 2304)),
           by_feature(w, np.concatenate([heads(1536, (t, 4 + t)) for t in range(4)])),
           by_feature(w, heads(2304, range(2))), by_feature(w, heads(2560, range(2))),
           by_token(np.concatenate([w[:, 2432:2560], w[:, 2688:2816]], 1), 256)]
    gate = np.zeros((1, P, PANEL), np.float32)
    g = np.zeros((P, KD, 32), np.float32)
    g[:, :, :24] = w[:, 2816:2840].reshape(KD, P, 24).transpose(1, 0, 2)
    gate[0, :, :256] = g.reshape(P, 256)
    out.append(gate)
    for name in ("cmp_k_w1", "cmp_v_w1"):
        out.append(a[name][0].reshape(4, 4, P, 256).transpose(0, 2, 1, 3).reshape(4, P, PANEL))
    w2 = np.zeros((1, P, PANEL), np.float32)
    k2, v2 = a["cmp_k_w2"][0][:, order], a["cmp_v_w2"][0]
    for m in range(2):
        w2[0, :, m * P:m * P + 64] = k2[m * P:(m + 1) * P]
        w2[0, :, m * P + 64:(m + 1) * P] = k2[m * P:(m + 1) * P]
        w2[0, :, 256 + 64 * m:320 + 64 * m] = v2[m * P:(m + 1) * P]
    out.append(w2)
    rows = np.concatenate([np.arange(512)] + [512 + 64 * h + np.arange(64) for t in range(4) for h in (t, 4 + t)])
    out.append(by_feature(a["w_out"][0][rows], np.arange(D)))

    def down(w, at, tiles):
        part = w[at * P:(at + tiles) * P]
        return by_feature(part, np.arange(D))

    up, dn = a["ffn_w_up"][0], a["ffn_w_down"][0]
    half, at = up.shape[1] // 2, 0
    for tiles in FF0_CHUNKS:
        cols = np.concatenate([side * half + (at + t) * P + np.arange(P) for t in range(tiles) for side in range(2)])
        out += [by_feature(up, cols), down(dn, at, tiles)]
        at += tiles
    w = a["ab_w_in_2"][0]
    gates = -np.ones(P, int)
    for n, row in enumerate((0, 64, 32, 96)):
        gates[row:row + 4] = 2048 + 4 * n + np.arange(4)
    out += [by_feature(w, gates), by_feature(w, np.arange(1024)), by_token(w[:, 1024:1536], 512),
            by_feature(w, np.arange(1536, 2048)), by_token(w[:, 2576:3088], 512), by_feature(w, np.arange(2064, 2576)),
            by_feature(a["ab_w_out_2"][0], np.arange(D))]

    def feed_forward(n):
        for c in range(FF_CHUNKS):
            out.append(by_feature(a["ffn_w1_2"][n], np.arange(c * 1024, (c + 1) * 1024)))
            out.append(down(a["ffn_w2_2"][n], c * 8, 8))

    feed_forward(0)
    kr = -np.ones(P, int)
    kr[64:96] = kr[96:P] = 640 + np.arange(32)
    out.append(by_feature(a["c_w_in_2"][0], np.concatenate([np.arange(640), kr])))
    uq, ukv = a["c_w_uq_2"][0], a["c_w_ukv_2"][0]
    mla = np.zeros((HEADS, P, PANEL), np.float32)
    for h in range(HEADS):
        for k in range(3):
            block = uq[k * P:(k + 1) * P, h * 96:(h + 1) * 96]
            mla[h, :, k * P:k * P + 96] = block
            mla[h, :, k * P + 96:(k + 1) * P] = block[:, 64 + np.array(HALF_SWAP)]
        for k in range(2):
            mla[h, :, 384 + k * P:448 + k * P] = ukv[k * P:(k + 1) * P, h * P:h * P + 64]
    out += [ukv.reshape(2, P, HEADS, 2, 64)[:, :, :, 1, :].reshape(2, P, PANEL), mla, by_feature(a["c_w_out_2"][0], np.arange(D))]
    feed_forward(1)
    out.append(np.zeros((PANELS - PANELS_USED, P, PANEL), np.float32))
    out = np.concatenate(out)
    assert out.shape == (PANELS, P, PANEL), out.shape
    return out


def lay_small(a):
    out = np.zeros((P, SMALL_N), np.float32)

    def put(name, value):
        at, n = SMALL[name]
        out[:, at:at + n] = value

    def columns_of(v):
        return np.asarray(v).reshape(-1, P).T

    put("ident", np.eye(P))
    put("ones", 1.0)
    for name, key in (("g_mix_pre", "norm_mix_pre"), ("g_mix_post", "norm_mix_post"), ("g_ffn_pre", "norm_ffn_pre"),
                      ("g_ffn_post", "norm_ffn_post"), ("gn", "ret_gn_w"), ("g_ab", "ab_norm_2"), ("g_head", "ab_head_g_2"),
                      ("g_c", "c_norm_2"), ("g_cq", "c_q_g_2"), ("g_ckv", "c_kv_g_2"), ("g_final", "final_norm_2")):
        put(name, columns_of(a[key]))
    put("g_ffn1", columns_of(a["ffn_norm_2"][0]))
    put("g_ffn2", columns_of(a["ffn_norm_2"][1]))
    pos = np.stack([a["cmp_k_pos"][0], a["cmp_v_pos"][0]])
    pos = pos.reshape(2, 16, 2, 64).transpose(3, 0, 2, 1).reshape(64, 64)
    put("cmp_pos", np.concatenate([pos, pos]))
    conv = a["ffn_conv"][0].reshape(3, 2, 22, P).transpose(3, 2, 1, 0)
    put("conv0", conv.reshape(P, 132))
    put("conv1", a["ab_conv_2"][0].reshape(5, 8, P).transpose(2, 1, 0).reshape(P, 40))
    at = SMALL["gate_b"][0]
    for n, row in enumerate((0, 64, 32, 96)):
        out[row:row + 4, at] = a["ab_gate_b_2"][0][4 * n:4 * n + 4]
    freq = (np.float32(10000.0) ** (-np.arange(16, dtype=np.float32) / np.float32(16))).astype(np.float32)
    put("freq", np.tile(freq, 8)[:, None])
    put("rope_sign", np.tile(np.repeat([-1.0, 1.0], 16), 4)[:, None])
    put("minus_half", -0.5)
    return out


def rope_tables(positions):
    inv = 1.0 / (np.float32(10000.0) ** (np.arange(0, 64, 2, dtype=np.float32) / np.float32(64)))
    ang = (positions.astype(np.float32)[:, None] * inv.astype(np.float32)[None, :]).astype(np.float64)
    p = np.arange(P)
    f = p % 16 + 16 * (p // 32 % 2)
    sign = np.where(p % 32 < 16, -1.0, 1.0)
    return np.cos(ang)[:, f].T, np.sin(ang)[:, f].T * sign[:, None]


def lay_first():
    out = np.zeros((P, FIRST_N), np.float32)

    def put(name, value):
        at = FIRST[name][0]
        out[:, at:at + value.shape[1]] = value

    c, s = rope_tables(np.arange(S))
    put("rope_c", c)
    put("rope_s", s)
    c, s = rope_tables(np.arange(31) * 16 + 31)
    put("cmp_c", c)
    put("cmp_s", s)
    diff = np.arange(S)[None, :] - np.arange(P)[:, None]
    decay = [np.where(diff >= 0, np.exp(np.log(1.0 - 2.0 ** (-5.0 - h)) * np.maximum(diff, 0)), 0.0) * 64 ** -0.5
             for h in range(4)]
    put("decay", np.concatenate(decay, 1))
    return out


def lay_second(a):
    out = np.zeros((P, SECOND_N), np.float32)
    out[:, 0:512] = a["ab_bs_2"][0].reshape(1, 512)
    out[:, 512:1024] = a["ab_v_g_2"][0][None, :]
    out[:, 1024:] = a["ab_ws_2"][0].transpose(2, 0, 1).reshape(P, 512)
    return out


def lay_masks(dtype):
    out = np.zeros((P, MASKS_N), np.float32)

    def put(name, value):
        out[:, MASKS[name][0]:MASKS[name][0] + value.shape[1]] = value

    r, c = np.arange(P)[:, None], np.arange(P)[None, :]
    put("ident", np.eye(P))
    put("q_k", np.where(c > r, NEG, 0.0))
    put("k_q", np.where(r > c, NEG, 0.0))
    key, query = np.arange(P), np.arange(S)
    bad = (key[:, None] * 16 + 31 > query[None, :]) | (key[:, None] >= 31)
    put("cmp_k_q", np.where(bad, NEG, 0.0))
    by_tile = np.where(bad, NEG, 0.0)[:32].reshape(32, NT, P).transpose(2, 1, 0).reshape(P, P)
    put("cmp_q_k", by_tile)
    return out.astype(dtype)


def kernel(**inputs):
    import concourse.bacc as bacc
    from concourse.bass_utils import run_bass_kernel_spmd

    a = {k: np.asarray(v) for k, v in inputs.items()}
    bf16 = mybir.dt.np(BF16)
    arrays = {
        "in_panels": lay_panels(a), "in_small": lay_small(a), "in_first": lay_first(), "in_second": lay_second(a),
        "in_masks": lay_masks(bf16), "in_x": np.ascontiguousarray(a["x"][0].T.reshape(KD, P, S)),
        "in_positions": np.ascontiguousarray(np.broadcast_to(a["positions_2"].astype(np.int32), (64, S))),
    }
    nc = bacc.Bacc("TRN2", target_bir_lowering=False, num_devices=1)
    dram = {name[3:]: nc.dram_tensor(name, v.shape, mybir.dt.from_np(v.dtype), kind="ExternalInput").ap()
            for name, v in arrays.items()}
    dram["out"] = nc.dram_tensor("out_0", (KD, P, S), F32, kind="ExternalOutput").ap()
    build(nc, dram)
    r = run_bass_kernel_spmd(nc, [arrays], core_ids=[0])
    return np.ascontiguousarray(np.asarray(r.results[0]["out_0"]).reshape(D, S).T)[None]
```
